# Optimizing a Trainium2 kernel written in Bass

```python
import jax, jax.numpy as jnp
from jax import lax
import numpy as np
import jax
import jax.numpy as jnp

D_MODEL = 1024
BATCH = 1
SEQ = 256
DEPTH = 2

GRID_W = 64
CTX_LEN = 256
HEAD_DIM = 64
ATT_WIDTH = D_MODEL // 2
ML_WIDTH = D_MODEL // 4
POOL_WIDTH = D_MODEL - ATT_WIDTH - ML_WIDTH
MIX_WIDTH = ATT_WIDTH + ML_WIDTH + POOL_WIDTH
ATT_HEADS = ATT_WIDTH // HEAD_DIM
ATT_KV_HEADS = ATT_HEADS // 4
KV_WIDTH = ATT_KV_HEADS * HEAD_DIM
ML_HEADS = ML_WIDTH // HEAD_DIM
POOL_WINDOWS = (2, 4, 8, 16)
POOL_GROUPS = len(POOL_WINDOWS)
POOL_GROUP_DIM = POOL_WIDTH // POOL_GROUPS
N_GATES = 4 * ML_HEADS
IN_SPLITS = (ATT_WIDTH, KV_WIDTH, KV_WIDTH, ML_WIDTH, ML_WIDTH, ML_WIDTH, ML_WIDTH, N_GATES, POOL_WIDTH)
IN_WIDTH = sum(IN_SPLITS)
IN_OFFSETS = tuple(int(o) for o in np.cumsum(IN_SPLITS)[:-1])
D_FF = -(-8 * D_MODEL // (3 * 256)) * 256
Q_BLOCK = 128
CHUNK = 128
ROPE_THETA = 10000.0
EPS = 1e-6


F32 = jnp.float32

def rms_norm(x, g):
    xf = x.astype(F32)
    y = xf * lax.rsqrt(jnp.mean(xf * xf, -1, keepdims=True) + EPS)
    return (y * g.astype(F32)).astype(x.dtype)

def axial_rope_tables(rows):
    half = HEAD_DIM // 2
    inv_freq = 1.0 / (ROPE_THETA ** (jnp.arange(0, half, 2, dtype=F32) / half))
    row = jnp.repeat(jnp.arange(rows, dtype=F32), GRID_W)
    col = jnp.tile(jnp.arange(GRID_W, dtype=F32), rows)
    a_row = row[:, None] * inv_freq
    a_col = col[:, None] * inv_freq
    ang = jnp.concatenate([a_row, a_row, a_col, a_col], -1)
    return jnp.cos(ang), jnp.sin(ang)

def apply_rope(x, cos, sin):
    q = HEAD_DIM // 4
    xr = x.reshape(x.shape[:-1] + (2, 2, q))
    rot = jnp.stack([-xr[..., 1, :], xr[..., 0, :]], -2).reshape(x.shape)
    out = x.astype(F32) * cos[:, None, :] + rot.astype(F32) * sin[:, None, :]
    return out.astype(x.dtype)

def block_attention(q, k, v):
    B, T, Hq, d = q.shape
    Hk = k.shape[2]
    G = Hq // Hk
    nb = T // Q_BLOCK
    qb = q.reshape(B, nb, Q_BLOCK, Hk, G, d).swapaxes(0, 1)
    scale = d ** -0.5

    def one_block(qi):
        s = jnp.einsum('bqhgd,bkhd->bhgqk', qi, k, preferred_element_type=F32) * scale
        p = jax.nn.softmax(s, -1).astype(v.dtype)
        return jnp.einsum('bhgqk,bkhd->bqhgd', p, v)

    o = lax.map(one_block, qb)
    return o.swapaxes(0, 1).reshape(B, T, Hq * d)

def mlstm_scan(q, k, v, log_i, log_f, state):
    B, H, T, d = q.shape
    nc = T // CHUNK

    def split(a):
        a = a.astype(F32)
        return jnp.moveaxis(a.reshape(a.shape[:2] + (nc, CHUNK) + a.shape[3:]), 2, 0)

    xs = (split(q), split(k * d ** -0.5), split(v), split(log_i), split(log_f))
    tril = jnp.tril(jnp.ones((CHUNK, CHUNK), bool))

    def step(carry, inp):
        C, n, m = carry
        qc, kc, vc, li, lf = inp
        b = jnp.cumsum(lf, -1)
        dmat = jnp.where(tril, b[..., :, None] - b[..., None, :] + li[..., None, :], -jnp.inf)
        inter = b + m[..., None]
        m_t = jnp.maximum(inter, jnp.max(dmat, -1))
        w_inter = jnp.exp(inter - m_t)
        s = jnp.einsum('bhtd,bhsd->bhts', qc, kc) * jnp.exp(dmat - m_t[..., None])
        num = w_inter[..., None] * jnp.einsum('bhvk,bhtk->bhtv', C, qc) + jnp.einsum('bhts,bhsv->bhtv', s, vc)
        den = w_inter * jnp.einsum('bhk,bhtk->bht', n, qc) + jnp.sum(s, -1)
        h = num / jnp.maximum(jnp.abs(den), jnp.exp(-m_t))[..., None]
        b_last = b[..., -1]
        g = b_last[..., None] - b + li
        m_new = jnp.maximum(b_last + m, jnp.max(g, -1))
        a = jnp.exp(b_last + m - m_new)
        wk = jnp.exp(g - m_new[..., None])
        C_new = a[..., None, None] * C + jnp.einsum('bhs,bhsv,bhsk->bhvk', wk, vc, kc)
        n_new = a[..., None] * n + jnp.einsum('bhs,bhsk->bhk', wk, kc)
        return (C_new, n_new, m_new), h

    state, hs = lax.scan(step, state, xs)
    return jnp.moveaxis(hs, 0, 2).reshape(B, H, T, d), state

def bidir_mlstm(q_c, k_c, v_c, g_c, q_l, k_l, v_l, g_l):
    B, H, _, d = q_l.shape
    zero = (jnp.zeros((B, H, d, d), F32), jnp.zeros((B, H, d), F32), jnp.zeros((B, H), F32))
    outs_c, outs_l = [], []
    for direc in range(2):
        rev = (lambda a: jnp.flip(a, 2)) if direc else (lambda a: a)
        li_c, lf_c = g_c[2 * direc], jax.nn.log_sigmoid(g_c[2 * direc + 1])
        li_l, lf_l = g_l[2 * direc], jax.nn.log_sigmoid(g_l[2 * direc + 1])
        h_c, st = mlstm_scan(rev(q_c), rev(k_c), rev(v_c), rev(li_c), rev(lf_c), zero)
        h_l, _ = mlstm_scan(rev(q_l), rev(k_l), rev(v_l), rev(li_l), rev(lf_l), st)
        outs_c.append(rev(h_c))
        outs_l.append(rev(h_l))
    return outs_c[0] + outs_c[1], outs_l[0] + outs_l[1]

def mlstm_readout(h, o_pre, ml_norm):
    B, H, T, d = h.shape
    hn = rms_norm(h.transpose(0, 2, 1, 3), ml_norm.reshape(H, d)).reshape(B, T, H * d)
    return (hn * jax.nn.sigmoid(o_pre.astype(F32))).astype(o_pre.dtype)

def pool_mix(u, pool_w, pool_scale):
    B, T, _ = u.shape
    uf = u.astype(F32)
    cs = jnp.concatenate([jnp.zeros((B, 1, POOL_WIDTH), F32), jnp.cumsum(uf, 1)], 1)
    t = jnp.arange(T)
    outs = []
    for gi, w in enumerate(POOL_WINDOWS):
        lo = jnp.maximum(t - w // 2, 0)
        hi = jnp.minimum(t + w // 2, T)
        sl = slice(gi * POOL_GROUP_DIM, (gi + 1) * POOL_GROUP_DIM)
        csg = cs[:, :, sl]
        mean = (csg[:, hi] - csg[:, lo]) / (hi - lo).astype(F32)[None, :, None]
        outs.append(mean - uf[:, :, sl])
    p = jnp.stack(outs, 2)
    y = jnp.einsum('btgi,gio->btgo', p, pool_w.astype(F32)).reshape(B, T, POOL_WIDTH)
    return (y * pool_scale.astype(F32)).astype(u.dtype)

def swiglu(h, w_g, w_u, w_d):
    return (jax.nn.silu(h @ w_g) * (h @ w_u)) @ w_d

def hybrid_layer(xl, xc, c, c_ctx, w_ada, b_ada, norm_mix, w_in, b_gates, q_norm, k_norm, ml_norm,
                 pool_w, pool_scale, w_out, norm_ffn, w_ffn_gate, w_ffn_up, w_ffn_down, cos, sin, with_ctx_out):
    B, T, _ = xl.shape
    Tc = xc.shape[1]
    mod_l = (jax.nn.silu(c) @ w_ada + b_ada)[:, None, :]
    mod_c = jax.nn.silu(c_ctx) @ w_ada + b_ada
    sh1_l, sc1_l, g1_l, sh2_l, sc2_l, g2_l = jnp.split(mod_l, 6, -1)
    sh1_c, sc1_c, g1_c, sh2_c, sc2_c, g2_c = jnp.split(mod_c, 6, -1)

    hl = rms_norm(xl, norm_mix) * (1.0 + sc1_l) + sh1_l
    hc = rms_norm(xc, norm_mix) * (1.0 + sc1_c) + sh1_c
    aq_l, ak_l, av_l, mq_l, mk_l, mv_l, mo_l, mg_l, pp_l = jnp.split(hl @ w_in, IN_OFFSETS, -1)
    aq_c, ak_c, av_c, mq_c, mk_c, mv_c, mo_c, mg_c, pp_c = jnp.split(hc @ w_in, IN_OFFSETS, -1)

    q_l = apply_rope(rms_norm(aq_l.reshape(B, T, ATT_HEADS, HEAD_DIM), q_norm), cos, sin)
    k_l = apply_rope(rms_norm(ak_l.reshape(B, T, ATT_KV_HEADS, HEAD_DIM), k_norm), cos, sin)
    v_l = av_l.reshape(B, T, ATT_KV_HEADS, HEAD_DIM)
    k_c = rms_norm(ak_c.reshape(B, Tc, ATT_KV_HEADS, HEAD_DIM), k_norm)
    v_c = av_c.reshape(B, Tc, ATT_KV_HEADS, HEAD_DIM)
    att_l = block_attention(q_l, jnp.concatenate([k_l, k_c], 1), jnp.concatenate([v_l, v_c], 1))

    def ml_heads(a, n):
        return a.reshape(B, n, ML_HEADS, HEAD_DIM).transpose(0, 2, 1, 3)

    def ml_gates(gp, n):
        return (gp + b_gates).astype(F32).reshape(B, n, 4, ML_HEADS).transpose(2, 0, 3, 1)

    hm_c, hm_l = bidir_mlstm(ml_heads(mq_c, Tc), ml_heads(mk_c, Tc), ml_heads(mv_c, Tc), ml_gates(mg_c, Tc),
                             ml_heads(mq_l, T), ml_heads(mk_l, T), ml_heads(mv_l, T), ml_gates(mg_l, T))
    ml_l = mlstm_readout(hm_l, mo_l, ml_norm)

    pool_l = pool_mix(pp_l, pool_w, pool_scale)

    xl = xl + g1_l * (jnp.concatenate([att_l, ml_l, pool_l], -1) @ w_out)
    h2l = rms_norm(xl, norm_ffn) * (1.0 + sc2_l) + sh2_l
    xl = xl + g2_l * swiglu(h2l, w_ffn_gate, w_ffn_up, w_ffn_down)

    if with_ctx_out:
        q_c = rms_norm(aq_c.reshape(B, Tc, ATT_HEADS, HEAD_DIM), q_norm)
        att_c = block_attention(q_c, k_c, v_c)
        ml_c = mlstm_readout(hm_c, mo_c, ml_norm)
        pool_c = pool_mix(pp_c, pool_w, pool_scale)
        xc = xc + g1_c * (jnp.concatenate([att_c, ml_c, pool_c], -1) @ w_out)
        h2c = rms_norm(xc, norm_ffn) * (1.0 + sc2_c) + sh2_c
        xc = xc + g2_c * swiglu(h2c, w_ffn_gate, w_ffn_up, w_ffn_down)
    return xl, xc

def first_inputs(seed: int = 0) -> dict:
    key = jax.random.key(seed)
    ks = jax.random.split(key, 22)

    def dense(k, shape, fan_in, mult=1.0):
        return mult * jax.random.normal(k, shape, F32) * fan_in ** -0.5

    def gain(k, shape):
        return 1.0 + 0.05 * jax.random.normal(k, shape, F32)

    f_bias = jnp.linspace(3.0, 6.0, ML_HEADS, dtype=F32)
    gate_base = jnp.stack([jnp.zeros_like(f_bias), f_bias, jnp.zeros_like(f_bias), f_bias])
    b_gates = (gate_base[None] + 0.1 * jax.random.normal(ks[8], (DEPTH, 4, ML_HEADS), F32)).reshape(DEPTH, N_GATES)
    return {
        'x': jax.random.normal(ks[0], (BATCH, SEQ, D_MODEL), F32),
        'c': jax.random.normal(ks[1], (BATCH, D_MODEL), F32),
        'ctx': jax.random.normal(ks[2], (BATCH, CTX_LEN, D_MODEL), F32),
        'c_ctx': jax.random.normal(ks[3], (D_MODEL,), F32),
        'w_ada': dense(ks[4], (DEPTH, D_MODEL, 6 * D_MODEL), D_MODEL, 0.5),
        'b_ada': 0.02 * jax.random.normal(ks[5], (DEPTH, 6 * D_MODEL), F32),
        'norm_mix': gain(ks[6], (DEPTH, D_MODEL)),
        'w_in': dense(ks[7], (DEPTH, D_MODEL, IN_WIDTH), D_MODEL),
        'b_gates': b_gates,
        'q_norm': gain(ks[9], (DEPTH, HEAD_DIM)),
        'k_norm': gain(ks[10], (DEPTH, HEAD_DIM)),
        'ml_norm': gain(ks[11], (DEPTH, ML_WIDTH)),
        'pool_w': dense(ks[12], (DEPTH, POOL_GROUPS, POOL_GROUP_DIM, POOL_GROUP_DIM), POOL_GROUP_DIM),
        'pool_scale': 1.0 + 0.1 * jax.random.normal(ks[13], (DEPTH, POOL_WIDTH), F32),
        'w_out': dense(ks[14], (DEPTH, MIX_WIDTH, D_MODEL), MIX_WIDTH),
        'norm_ffn': gain(ks[15], (DEPTH, D_MODEL)),
        'w_ffn_gate': dense(ks[16], (DEPTH, D_MODEL, D_FF), D_MODEL),
        'w_ffn_up': dense(ks[17], (DEPTH, D_MODEL, D_FF), D_MODEL),
        'w_ffn_down': dense(ks[18], (DEPTH, D_FF, D_MODEL), D_FF),
        'final_norm': gain(ks[19], (D_MODEL,)),
    }

def first_block(x, c, ctx, c_ctx, w_ada, b_ada, norm_mix, w_in, b_gates, q_norm, k_norm, ml_norm,
              pool_w, pool_scale, w_out, norm_ffn, w_ffn_gate, w_ffn_up, w_ffn_down, final_norm):
    ROWS = x.shape[1] // GRID_W
    cos, sin = axial_rope_tables(ROWS)
    xl, xc = x, ctx
    for layer in range(DEPTH):
        xl, xc = hybrid_layer(xl, xc, c, c_ctx, w_ada[layer], b_ada[layer], norm_mix[layer], w_in[layer],
                              b_gates[layer], q_norm[layer], k_norm[layer], ml_norm[layer], pool_w[layer],
                              pool_scale[layer], w_out[layer], norm_ffn[layer], w_ffn_gate[layer],
                              w_ffn_up[layer], w_ffn_down[layer], cos, sin, layer < DEPTH - 1)
    return rms_norm(xl, final_norm)


DEPTH_2 = 1

NORM_EPS = 1e-6
D_FF_2 = 2816

ATTN_HEAD_DIM = 64
ATTN_HEADS_PER_GROUP = 4
ATTN_GROUPS = ((128, 1), (512, 4), (2048, 16))
N_ATTN_GROUPS = 3
ATTN_WIDTH = N_ATTN_GROUPS * ATTN_HEADS_PER_GROUP * ATTN_HEAD_DIM
ATTN_OUT_WIDTH = ATTN_HEADS_PER_GROUP * ATTN_HEAD_DIM
ROPE_THETA_2 = 500000.0
ROPE_DIM = ATTN_HEAD_DIM // 4

RWKV_HEAD_DIM = 64
RWKV_WIDTH = D_MODEL
RWKV_HEADS = RWKV_WIDTH // RWKV_HEAD_DIM
DECAY_LORA = 64
ICLR_LORA = 64
GATE_LORA = 160
RWKV_GN_EPS = 64e-5
RWKV_STREAM = 3 * RWKV_WIDTH + DECAY_LORA + ICLR_LORA + GATE_LORA

IN_COLS = 3 * ATTN_WIDTH + RWKV_STREAM + 2 * D_MODEL


def rms_norm_2(x, gain):
    xf = x.astype(jnp.float32)
    y = xf * lax.rsqrt(jnp.mean(xf * xf, axis=-1, keepdims=True) + NORM_EPS)
    return (y * gain.astype(jnp.float32)).astype(x.dtype)

def swiglu_2(h, w_gate, w_up, w_down):
    return (jax.nn.silu(h @ w_gate) * (h @ w_up)) @ w_down

def partial_rope(x, positions):
    half = ROPE_DIM // 2
    inv_freq = jnp.power(ROPE_THETA_2, -jnp.arange(half, dtype=jnp.float32) * (2.0 / ROPE_DIM))
    ang = positions.astype(jnp.float32)[:, None] * inv_freq[None, :]
    cos = jnp.cos(ang)[None, :, None, :]
    sin = jnp.sin(ang)[None, :, None, :]
    xr = x[..., :ROPE_DIM].astype(jnp.float32)
    x1, x2 = xr[..., :half], xr[..., half:]
    rot = jnp.concatenate([x1 * cos - x2 * sin, x2 * cos + x1 * sin], axis=-1).astype(x.dtype)
    return jnp.concatenate([rot, x[..., ROPE_DIM:]], axis=-1)

def dilated_group(q, k, v, window, dilation):
    B, S, H, Dh = q.shape
    n = window // dilation
    L = S // dilation
    nb = -(-L // n)
    Lp = nb * n

    def to_sub(t):
        t = t.reshape(B, L, dilation, H, Dh).transpose(0, 2, 3, 1, 4)
        t = jnp.pad(t, ((0, 0), (0, 0), (0, 0), (0, Lp - L), (0, 0)))
        return t.reshape(B, dilation, H, nb, n, Dh)

    def with_prev(t):
        prev = jnp.pad(t, ((0, 0), (0, 0), (0, 0), (1, 0), (0, 0), (0, 0)))[:, :, :, :-1]
        return jnp.concatenate([prev, t], axis=4)

    def from_sub(t):
        t = t.reshape(B, dilation, H, Lp, t.shape[-1])[:, :, :, :L]
        return t.transpose(0, 3, 1, 2, 4).reshape(B, S, H, t.shape[-1])

    qb = to_sub(q)
    kw = with_prev(to_sub(k))
    vw = with_prev(to_sub(v))
    s = jnp.einsum('brhiqd,brhikd->brhiqk', qb, kw, preferred_element_type=jnp.float32)
    qi = jnp.arange(n)[:, None]
    ki = jnp.arange(2 * n)[None, :]
    rel = qi + n - ki
    band = (rel >= 0) & (rel <= n)
    blk = jnp.arange(nb)[:, None, None]
    valid = band[None] & ((blk > 0) | (ki[None] >= n))
    s = jnp.where(valid, s, -jnp.inf)
    m = jnp.max(s, axis=-1)
    p = jnp.exp(s - m[..., None])
    l = jnp.sum(p, axis=-1)
    acc = jnp.einsum('brhiqk,brhikd->brhiqd', p, vw.astype(jnp.float32))
    return from_sub(acc), from_sub(m[..., None])[..., 0], from_sub(l[..., None])[..., 0]

def dilated_attention(qkv, positions):
    B, S, _ = qkv.shape
    G, Hg, Dh = N_ATTN_GROUPS, ATTN_HEADS_PER_GROUP, ATTN_HEAD_DIM
    q, k, v = jnp.split(qkv, 3, axis=-1)
    q = partial_rope(q.reshape(B, S, G * Hg, Dh), positions) * (Dh ** -0.5)
    k = partial_rope(k.reshape(B, S, G * Hg, Dh), positions)
    v = v.reshape(B, S, G * Hg, Dh)
    accs, ms, ls = [], [], []
    for g, (window, dilation) in enumerate(ATTN_GROUPS):
        sl = slice(g * Hg, (g + 1) * Hg)
        acc, m, l = dilated_group(q[:, :, sl], k[:, :, sl], v[:, :, sl], window, dilation)
        accs.append(acc)
        ms.append(m)
        ls.append(l)
    m_all = jnp.stack(ms)
    c = jnp.exp(m_all - jnp.max(m_all, axis=0))
    num = jnp.sum(c[..., None] * jnp.stack(accs), axis=0)
    den = jnp.sum(c * jnp.stack(ls), axis=0)
    out = (num / den[..., None]).astype(qkv.dtype)
    return out.reshape(B, S, Hg * Dh)

def token_shift(z, mu):
    prev = jnp.pad(z, ((0, 0), (1, 0), (0, 0)))[:, :-1]
    return z + (prev - z) * mu

def wkv7_scan(r, w, k, v, a, b):
    B, S, H, N = r.shape

    def step(state, inp):
        r_t, w_t, k_t, v_t, a_t, b_t = inp
        sa = jnp.einsum('bhvk,bhk->bhv', state, a_t)
        state = (state * w_t[:, :, None, :] + sa[..., None] * b_t[:, :, None, :]
                 + v_t[..., None] * k_t[:, :, None, :])
        return state, jnp.einsum('bhvk,bhk->bhv', state, r_t)

    xs = tuple(jnp.moveaxis(t.astype(jnp.float32), 1, 0) for t in (r, w, k, v, a, b))
    _, ys = lax.scan(step, jnp.zeros((B, H, N, N), jnp.float32), xs)
    return jnp.moveaxis(ys, 0, 1)

def rwkv7_time_mix(z, w0, w2, a0, a2, g2, k_k, k_a, r_k, ln_w, ln_b, w_out):
    B, S, _ = z.shape
    RW, H, N = RWKV_WIDTH, RWKV_HEADS, RWKV_HEAD_DIM
    o1, o2, o3 = RW, 2 * RW, 3 * RW
    o4, o5 = o3 + DECAY_LORA, o3 + DECAY_LORA + ICLR_LORA
    r, k, v = z[..., :o1], z[..., o1:o2], z[..., o2:o3]
    zw, za, zg = z[..., o3:o4], z[..., o4:o5], z[..., o5:]
    logw = -jax.nn.softplus(-(w0 + jnp.tanh(zw) @ w2)) - 0.5
    decay = jnp.exp(-jnp.exp(logw.astype(jnp.float32)))
    a = jax.nn.sigmoid(a0 + za @ a2)
    g = jax.nn.sigmoid(zg) @ g2
    kk = (k * k_k).astype(jnp.float32).reshape(B, S, H, N)
    kk = kk / jnp.maximum(jnp.sqrt(jnp.sum(kk * kk, axis=-1, keepdims=True)), 1e-12)
    k = k * (1.0 + (a - 1.0) * k_a)
    rh = r.reshape(B, S, H, N).astype(jnp.float32)
    kh = k.reshape(B, S, H, N).astype(jnp.float32)
    vh = v.reshape(B, S, H, N).astype(jnp.float32)
    ah = a.reshape(B, S, H, N).astype(jnp.float32)
    y = wkv7_scan(rh, decay.reshape(B, S, H, N), kh, vh, -kk, kk * ah)
    mu = jnp.mean(y, axis=-1, keepdims=True)
    var = jnp.mean(jnp.square(y - mu), axis=-1, keepdims=True)
    yn = ((y - mu) * lax.rsqrt(var + RWKV_GN_EPS)).reshape(B, S, RW)
    yn = yn * ln_w.astype(jnp.float32) + ln_b.astype(jnp.float32)
    bonus = (jnp.sum(rh * kh * r_k.astype(jnp.float32), axis=-1, keepdims=True) * vh).reshape(B, S, RW)
    return ((yn + bonus) * g.astype(jnp.float32)).astype(z.dtype) @ w_out

def hybrid_mixer(h, positions, w_in, gate_bias, attn_w_up, rwkv_mu, rwkv_w0, rwkv_w2, rwkv_a0,
                 rwkv_a2, rwkv_g2, rwkv_k_k, rwkv_k_a, rwkv_r_k, rwkv_ln_w, rwkv_ln_b,
                 rwkv_w_out, w_o):
    proj = h @ w_in
    aw, rs = 3 * ATTN_WIDTH, RWKV_STREAM
    gates = jax.nn.sigmoid(proj[..., aw + rs:] + gate_bias)
    y_attn = dilated_attention(proj[..., :aw], positions) @ attn_w_up
    y_rwkv = rwkv7_time_mix(token_shift(proj[..., aw:aw + rs], rwkv_mu), rwkv_w0, rwkv_w2,
                            rwkv_a0, rwkv_a2, rwkv_g2, rwkv_k_k, rwkv_k_a, rwkv_r_k,
                            rwkv_ln_w, rwkv_ln_b, rwkv_w_out)
    merged = gates[..., :D_MODEL] * y_attn + gates[..., D_MODEL:] * y_rwkv
    return merged @ w_o

def second_inputs(seed: int = 0) -> dict:
    key = jax.random.key(seed)
    ks = iter(jax.random.split(key, 40))
    f32 = jnp.float32

    def nrm(shape, scale):
        return jax.random.normal(next(ks), shape, f32) * scale

    def gain(shape):
        return 1.0 + 0.05 * jax.random.normal(next(ks), shape, f32)

    L, D, F = DEPTH_2, D_MODEL, D_FF_2
    RW, H, N = RWKV_WIDTH, RWKV_HEADS, RWKV_HEAD_DIM
    return {
        'x': nrm((BATCH, SEQ, D), 1.0),
        'ffn1_norm': gain((L, D)),
        'ffn1_w_gate': nrm((L, D, F), D ** -0.5),
        'ffn1_w_up': nrm((L, D, F), D ** -0.5),
        'ffn1_w_down': nrm((L, F, D), F ** -0.5),
        'mix_norm': gain((L, D)),
        'w_in': nrm((L, D, IN_COLS), D ** -0.5),
        'gate_bias': nrm((L, 2 * D), 0.1),
        'attn_w_up': nrm((L, ATTN_OUT_WIDTH, D), ATTN_OUT_WIDTH ** -0.5),
        'rwkv_mu': jax.random.uniform(next(ks), (L, RWKV_STREAM), f32),
        'rwkv_w0': jax.random.uniform(next(ks), (L, RW), f32, -6.0, -1.0),
        'rwkv_w2': nrm((L, DECAY_LORA, RW), 0.1 * DECAY_LORA ** -0.5),
        'rwkv_a0': nrm((L, RW), 0.1),
        'rwkv_a2': nrm((L, ICLR_LORA, RW), 0.1 * ICLR_LORA ** -0.5),
        'rwkv_g2': nrm((L, GATE_LORA, RW), GATE_LORA ** -0.5),
        'rwkv_k_k': 0.85 + 0.05 * jax.random.normal(next(ks), (L, RW), f32),
        'rwkv_k_a': gain((L, RW)),
        'rwkv_r_k': nrm((L, H, N), 0.1),
        'rwkv_ln_w': gain((L, RW)),
        'rwkv_ln_b': nrm((L, RW), 0.02),
        'rwkv_w_out': nrm((L, RW, D), RW ** -0.5),
        'w_o': nrm((L, D, D), D ** -0.5),
        'ffn2_norm': gain((L, D)),
        'ffn2_w_gate': nrm((L, D, F), D ** -0.5),
        'ffn2_w_up': nrm((L, D, F), D ** -0.5),
        'ffn2_w_down': nrm((L, F, D), F ** -0.5),
        'final_norm': gain((D,)),
    }

def second_block(x, ffn1_norm, ffn1_w_gate, ffn1_w_up, ffn1_w_down, mix_norm, w_in, gate_bias,
              attn_w_up, rwkv_mu, rwkv_w0, rwkv_w2, rwkv_a0, rwkv_a2, rwkv_g2, rwkv_k_k,
              rwkv_k_a, rwkv_r_k, rwkv_ln_w, rwkv_ln_b, rwkv_w_out, w_o, ffn2_norm,
              ffn2_w_gate, ffn2_w_up, ffn2_w_down, final_norm):
    positions = jnp.arange(x.shape[1], dtype=jnp.int32)
    for layer in range(DEPTH_2):
        x = x + 0.5 * swiglu_2(rms_norm_2(x, ffn1_norm[layer]), ffn1_w_gate[layer],
                             ffn1_w_up[layer], ffn1_w_down[layer])
        x = x + hybrid_mixer(rms_norm_2(x, mix_norm[layer]), positions, w_in[layer],
                             gate_bias[layer], attn_w_up[layer], rwkv_mu[layer],
                             rwkv_w0[layer], rwkv_w2[layer], rwkv_a0[layer], rwkv_a2[layer],
                             rwkv_g2[layer], rwkv_k_k[layer], rwkv_k_a[layer],
                             rwkv_r_k[layer], rwkv_ln_w[layer], rwkv_ln_b[layer],
                             rwkv_w_out[layer], w_o[layer])
        x = x + 0.5 * swiglu_2(rms_norm_2(x, ffn2_norm[layer]), ffn2_w_gate[layer],
                             ffn2_w_up[layer], ffn2_w_down[layer])
    return rms_norm_2(x, final_norm)


def setup_inputs(seed=0):
    out = dict(first_inputs(seed))
    for name, value in second_inputs(seed + 1).items():
        if name != "x":
            out[name + "_2"] = value
    return out


def reference(
    x, c, ctx, c_ctx, w_ada, b_ada, norm_mix, w_in, b_gates, q_norm, k_norm, ml_norm, pool_w,
    pool_scale, w_out, norm_ffn, w_ffn_gate, w_ffn_up, w_ffn_down, final_norm, ffn1_norm_2,
    ffn1_w_gate_2, ffn1_w_up_2, ffn1_w_down_2, mix_norm_2, w_in_2, gate_bias_2, attn_w_up_2,
    rwkv_mu_2, rwkv_w0_2, rwkv_w2_2, rwkv_a0_2, rwkv_a2_2, rwkv_g2_2, rwkv_k_k_2, rwkv_k_a_2,
    rwkv_r_k_2, rwkv_ln_w_2, rwkv_ln_b_2, rwkv_w_out_2, w_o_2, ffn2_norm_2, ffn2_w_gate_2,
    ffn2_w_up_2, ffn2_w_down_2, final_norm_2,
):
    x = first_block(
        x, c, ctx, c_ctx, w_ada, b_ada, norm_mix, w_in, b_gates, q_norm, k_norm, ml_norm,
        pool_w, pool_scale, w_out, norm_ffn, w_ffn_gate, w_ffn_up, w_ffn_down, final_norm,
    )
    return second_block(
        x, ffn1_norm_2, ffn1_w_gate_2, ffn1_w_up_2, ffn1_w_down_2, mix_norm_2, w_in_2,
        gate_bias_2, attn_w_up_2, rwkv_mu_2, rwkv_w0_2, rwkv_w2_2, rwkv_a0_2, rwkv_a2_2,
        rwkv_g2_2, rwkv_k_k_2, rwkv_k_a_2, rwkv_r_k_2, rwkv_ln_w_2, rwkv_ln_b_2, rwkv_w_out_2,
        w_o_2, ffn2_norm_2, ffn2_w_gate_2, ffn2_w_up_2, ffn2_w_down_2, final_norm_2,
    )


_drawn_inputs = setup_inputs


def setup_inputs(seed=0):
    import zlib

    import numpy as np

    out = dict(_drawn_inputs(seed))
    spreads = {}
    factors = {'q_norm': 8.0,
     'k_norm': 8.0,
     'ml_norm': 7.679,
     'gate_bias_2': 4.885,
     'rwkv_w2_2': 8.0,
     'rwkv_a0_2': 4.299,
     'rwkv_a2_2': 4.651,
     'rwkv_k_k_2': 5.367,
     'rwkv_k_a_2': 3.812,
     'rwkv_ln_w_2': 4.188,
     'rwkv_ln_b_2': 8.0,
     'ffn2_norm_2': 3.095}
    for name, (base, spread) in spreads.items():
        noise = np.random.default_rng([zlib.crc32(name.encode()), seed]).standard_normal(out[name].shape)
        drawn = base * np.exp(spread * noise) if base else spread * noise
        out[name] = jnp.asarray(drawn.astype(out[name].dtype))
    for name, factor in factors.items():
        out[name] = (out[name] * factor).astype(out[name].dtype)
    return out
```

```python
from contextlib import ExitStack

import numpy as np
import concourse.bass as bass
from concourse import mybir

F32 = mybir.dt.float32
ALU = mybir.AluOpType
ACT = mybir.ActivationFunctionType
AX = mybir.AxisListType.X

P = 128
D = 1024
KT = D // P
T = 256
TA = 2 * T
HD = 64
DEPTH = 2
FF = 2816
FT = FF // P
ADA_UNITS, ADA_COLS = 16, 384
SLOTS, SLOT = 4, 3072
EPS = 1e-6
GN_EPS = 64e-5
POOL_WINDOWS = (2, 4, 8, 16)
GRID_W = 64
CHUNK = 64
DECAY = float(np.exp(-0.5))
LEVELS = 6

AQ, MQ, MO, MK, AK, FM_TILES = 0, 4, 6, 8, 10, 11
MV, MG, AV, PP, TM = 0, 256, 272, 400, 656
RR, RK, RV, RL, R_TILES = 0, 8, 16, 24, 27


def constant_table():
    c = {}
    i = np.arange(P)
    c["ident"] = np.eye(P)
    c["ones"] = np.ones((P, P))
    c["blockones"] = (i[:, None] // HD == i[None] // HD) * 1.0
    rot = np.zeros((P, P))
    for o in range(P):
        if o % 32 < 16:
            rot[o + 16, o] = -1
        else:
            rot[o - 16, o] = 1
    c["rot1"] = rot
    rot = np.zeros((P, P))
    for o in range(P):
        d = o % HD
        if d < 8:
            rot[o + 8, o] = -1
        elif d < 16:
            rot[o - 8, o] = 1
    c["rot2"] = rot
    half = HD // 2
    f32 = np.float32
    inv = (1.0 / (f32(10000.0) ** (np.arange(0, half, 2, dtype=f32) / f32(half)))).astype(f32)
    row = np.repeat(np.arange(T // GRID_W, dtype=f32), GRID_W)
    col = np.tile(np.arange(GRID_W, dtype=f32), T // GRID_W)
    ar, ac = row[:, None] * inv, col[:, None] * inv
    ang = np.concatenate([ar, ar, ac, ac], 1).astype(f32)
    cos1, sin1 = np.ones((P, TA)), np.zeros((P, TA))
    cos1[:, T:] = np.tile(np.cos(ang).T, (2, 1))
    sin1[:, T:] = np.tile(np.sin(ang).T, (2, 1))
    c["cos1"], c["sin1"] = cos1, sin1
    inv2 = np.power(f32(500000.0), -np.arange(8, dtype=f32) * f32(2.0 / 16)).astype(f32)
    a2 = (np.arange(T, dtype=f32)[:, None] * inv2[None]).astype(f32)
    cos2, sin2 = np.ones((HD, T)), np.zeros((HD, T))
    cos2[0:16] = np.tile(np.cos(a2).T, (2, 1))
    sin2[0:16] = np.tile(np.sin(a2).T, (2, 1))
    c["cos2"], c["sin2"] = np.tile(cos2, (2, 1)), np.tile(sin2, (2, 1))
    c["tri0"] = (i[:, None] <= i[None]) * 1.0
    c["tri1"] = (i[:, None] >= i[None]) * 1.0
    for qt in range(2):
        nk = (qt + 1) * P
        t = qt * P + i[:, None]
        s = np.arange(nk)[None]
        see = [(s <= t) & (t - s <= P), (s <= t) & ((t - s) % 4 == 0), (s <= t) & ((t - s) % 16 == 0)]
        c[f"see{qt}"] = np.concatenate([np.where(m, 0.0, -1e30) for m in see], 1)
    t = np.arange(T)
    band = np.zeros((T, 4, T))
    for g, w in enumerate(POOL_WINDOWS):
        lo, hi = np.maximum(t - w // 2, 0), np.minimum(t + w // 2, T)
        s = t[:, None]
        band[:, g] = ((s >= lo) & (s < hi)) / (hi - lo).astype(f32)[None] - (s == t[None])
    c["band"] = band.reshape(2, P, 4, T).transpose(1, 0, 2, 3).reshape(P, -1)
    sel = np.zeros((P, 4, P))
    for h in range(4):
        sel[h, h] = 1
    c["sel"] = sel.reshape(P, -1)
    fold = np.zeros((P, 2))
    for j in range(4):
        fold[32 * j, 0] = fold[32 * j + 1, 1] = 1
    c["fold"] = fold
    s, t = i[:, None] % CHUNK, np.arange(CHUNK)[None]
    c["gram"] = np.concatenate([s < t, s <= t, s < t, s <= t], 1) * 1.0
    c["eye64"] = (s == t) * 1.0
    lev, levT = [], []
    for l in range(LEVELS):
        b = 1 << l
        low = (s // (2 * b) == t // (2 * b)) & (s % (2 * b) >= b) & (t % (2 * b) < b)
        lev.append(low)
        levT.append((s // (2 * b) == t // (2 * b)) & (t % (2 * b) >= b) & (s % (2 * b) < b))
    c["lev0"] = lev[0] * 1.0
    c["levT"] = np.concatenate(levT, 1) * 1.0
    reset = np.ones((P, TA))
    reset[:, ::CHUNK] = 0
    c["reset"] = reset
    return {k: np.ascontiguousarray(v, dtype=f32) for k, v in c.items()}


def column_map(groups):
    at, out = 0, {}
    for name, n in groups:
        out[name] = (at, n)
        at += n
    return out, at


CONSTS = constant_table()
COMMON = ("ident", "ones", "blockones")
BLOCK1 = ("rot1", "cos1", "sin1", "tri0", "tri1", "band", "sel", "fold")
BLOCK2 = tuple(k for k in CONSTS if k not in COMMON + BLOCK1)
CONST_AT, COMMON_N = column_map([(k, CONSTS[k].shape[1]) for k in COMMON])
_one, ONE_N = column_map([(k, CONSTS[k].shape[1]) for k in BLOCK1])
_two, TWO_N = column_map([(k, CONSTS[k].shape[1]) for k in BLOCK2] + [("wa2", D), ("g2a", D), ("g2b", D)])
CONST_AT.update({k: (COMMON_N + at, n) for m in (_one, _two) for k, (at, n) in m.items()})
CONST_N = COMMON_N + max(ONE_N, TWO_N)

PAR1 = [("norm_mix", 8), ("norm_ffn", 8), ("b_ada", 48), ("q_norm", 1), ("k_norm", 1), ("ml_norm", 2),
        ("pool_scale", 2), ("b_gates", 4), ("pool_w", 2 * HD)]
PAR2 = [("final_norm", 8), ("ffn1_norm", 8), ("mix_norm", 8), ("ffn2_norm", 8), ("final_norm_2", 8),
        ("gate_bias", 16), ("mu", R_TILES), ("w0", 8), ("a0", 8), ("k_k", 8), ("k_a", 8), ("r_k", 8),
        ("ln_w", 8), ("ln_b", 8), ("cond", 16)]
PAR_AT, PAR_N = column_map([(f"{n}{l}", k) for l in range(DEPTH) for n, k in PAR1] + PAR2)

PHASES = []
for _l in range(DEPTH):
    PHASES += [(f"ada{_l}", ADA_UNITS, KT * ADA_COLS), (f"fm{_l}", 6, 2 * D), (f"tma{_l}", 1, KT * 272),
               (f"tmb{_l}", 1, KT * 384), (f"out{_l}", 4, 2 * D), (f"up{_l}", FT, 2 * D), (f"down{_l}", 8, FT * P)]
PHASES += [("up2", FT, 2 * D), ("down2", 8, FT * P), ("qk", 4, 3 * D), ("v", 2, KT * 384), ("rkv", 8, 3 * D),
           ("lora", 1, KT * 288), ("attn_up", 2, D), ("rwkv_out", 4, 2 * D), ("gates", 8, 2 * D), ("w_o", 4, 2 * D),
           ("up3", FT, 2 * D), ("down3", 8, FT * P)]
FIRST = {}
_u = 0
for _n, _k, _ in PHASES:
    FIRST[_n] = _u
    _u += _k
UNITS = _u


class Chain:

    def __init__(self, eng, sem):
        self.eng, self.sem, self.n, self.reg = eng, sem, 0, None

    def __call__(self, ins):
        ins.then_inc(self.sem, 1)
        self.n += 1
        self.eng.wait_ge(self.sem, self.n if self.reg is None else self.reg + self.n)


def over_units(eng, phase, body, chain=None):
    first, n = FIRST[phase], dict((a, b) for a, b, _ in PHASES)[phase]
    i = 0
    if first == 0:
        while i < SLOTS:
            body(i % SLOTS, i, i)
            i += 1
    trips = (n - i) // SLOTS
    if trips > 1:
        per = 0
        n0 = chain.n if chain else 0
        with eng.Fori(0, trips) as r:
            if chain:
                chain.reg = r * chain.per
            for j in range(SLOTS):
                body((first + i + j) % SLOTS, r * SLOTS + (first + i + j), r * SLOTS + (i + j))
        if chain:
            assert chain.n - n0 == chain.per, (chain.n, n0, chain.per)
            chain.n = n0 + chain.per * trips
            chain.reg = None
        i += trips * SLOTS
    while i < n:
        body((first + i) % SLOTS, first + i, i)
        i += 1


def build(nc, dram, out):
    ctx = ExitStack()
    with ctx:
        def sb(name, *shape):
            return ctx.enter_context(nc.sbuf_tensor(name, [P, *shape], F32))

        def sem(name):
            return ctx.enter_context(nc.semaphore(name))

        xT = sb("xT", KT, TA)
        hT = sb("hT", KT, TA)
        ring = sb("ring", SLOTS, SLOT)
        const = sb("const", CONST_N)
        par = sb("par", PAR_N)
        mod = sb("mod", 48, 2)
        scl = sb("scl", 2, KT, 2)
        eps_col = sb("eps_col", 2)
        WORK = 25200
        work = sb("work", WORK)
        ps = ctx.enter_context(nc.psum_tensor("ps", [P, 8, 512], F32))

        def K(name):
            at, n = CONST_AT[name]
            return const[:, at:at + n]

        def C(name, j=0, n=1, rows=slice(0, P)):
            at, _ = PAR_AT[name]
            return par[rows, at + j:at + j + n]

        class Area:

            def __init__(self, at=0):
                self.at = at

            def __call__(self, n):
                self.at += n
                assert self.at <= WORK, self.at
                return work[:, self.at - n:self.at]

        a = Area()
        proj = a(FM_TILES * TA).rearrange("p (m t) -> p m t", t=TA)
        tm = a(4 * TM).rearrange("p (k c) -> p k c", c=TM)
        mixT = a(KT * TA).rearrange("p (m t) -> p m t", t=TA)
        mixer_free = a.at
        hidden = work[:, 0:FT * TA].rearrange("p (m t) -> p m t", t=TA)
        stage_buf = work[:, WORK - 2048:WORK].rearrange("p (b n) -> p b n", b=2)

        params_in = sem("params_in")
        second_in = sem("second_in")
        loaded = [sem(f"loaded{j}") for j in range(SLOTS)]
        unit_done = sem("unit_done")
        act_out = sem("act_out")
        dve_out = sem("dve_out")
        chains = {e: sem(f"{e}_chain") for e in ("act", "dve", "pool")}
        met = {e: sem(f"{e}_met") for e in ("pe", "act", "dve", "pool")}
        stored = sem("stored")

        class Meet:

            def __init__(self, eng, me):
                self.eng, self.me, self.n = eng, me, 0

            def __call__(self):
                self.n += 1
                self.eng.drain().then_inc(met[self.me], 1)
                for other in met:
                    if other != self.me:
                        self.eng.wait_ge(met[other], self.n)

        def load_weights(sp):
            for phase, n, size in PHASES:
                src = dram[f"w_{phase}"]

                def body(j, u, i):
                    if not (isinstance(u, int) and u < SLOTS):
                        sp.wait_ge(unit_done, u - (SLOTS - 1))
                    sp.dma_start(ring[:, j, 0:size], src[bass.ds(i, 1), :, :].rearrange("a p n -> p (a n)"))\
                        .then_inc(loaded[j], 16)
                over_units(sp, phase, body)

        def pe_unit_ready(pe, j, u):
            pe.wait_ge(loaded[j], (u - j) * (16 // SLOTS) + 16)
            if not (isinstance(u, int) and u < 2):
                pe.wait_ge(act_out, u - 1)
                pe.wait_ge(dve_out, u - 1)

        def pe_feature_tiles(pe, phase, tiles, rhs, c0, n, kt=KT, per_bank=None, straight=False):
            per_bank = per_bank or 512 // n

            def body(j, u, i):
                pe_unit_ready(pe, j, u)
                for m in range(tiles):
                    bank = 2 * (j % 2) + m // per_bank
                    o = (m % per_bank) * n
                    for k in range(kt):
                        w = ring[:, j, (m * kt + k) * P:(m * kt + k + 1) * P]
                        mm = pe.matmul(ps[:, bank, o:o + n], w, rhs[:, k, c0:c0 + n], start=(k == 0), stop=(k == kt - 1))
                mm.then_inc(unit_done, 1)
            if straight:
                straight_units(phase, body)
            else:
                over_units(pe, phase, body)

        def pe_ada(pe, layer, cond):
            def body(j, u, i):
                pe_unit_ready(pe, j, u)
                half = ADA_COLS // 2
                for x in range(2):
                    for k in range(KT):
                        g, o = k % 4, k * ADA_COLS + x * half
                        mm = pe.matmul(ps[32 * g:32 * g + 32, 2 * (j % 2) + x, 0:half], cond[:, k, :],
                                       ring[:, j, o:o + half], start=(k < 4), stop=(k >= 4),
                                       tile_position=(0, 32 * g), skip_group_check=True)
                mm.then_inc(unit_done, 1)
                pe.wait_ge(act_out, u + 1)
                pe.wait_ge(dve_out, u + 1)
                for m in range(3):
                    pe.matmul(ps[:, 4, bass.ds(i * 6 + 2 * m, 2)], stage_buf[:, j % 2, m * P:(m + 1) * P],
                              K("fold"), start=True, stop=True)
            over_units(pe, f"ada{layer}", body)

        def copy_rows(eng, copy, my_out, phase, me):
            half = ADA_COLS // 2

            def body(j, u, i):
                eng.wait_ge(unit_done, u + 1)
                copy(stage_buf[:, j % 2, me * half:(me + 1) * half], ps[:, 2 * (j % 2) + me, 0:half]).then_inc(my_out, 1)
            over_units(eng, phase, body)

        def act_copy(act):
            return lambda o, i: act.activation(o, i, ACT.Copy)

        def act_residual(act, phase, n, gates, tiles):
            def body(j, u, i):
                act.wait_ge(unit_done, u + 1)
                act.wait_ge(dve_out, u - 1)
                for m in range(tiles):
                    for lo, hi, s in gates(i * tiles + m):
                        ins = act.activation(stage_buf[:, j % 2, m * n + lo:m * n + hi],
                                             ps[:, 2 * (j % 2) + (m * n) // 512, (m * n) % 512 + lo:(m * n) % 512 + hi],
                                             ACT.Copy, scale=s)
                ins.then_inc(act_out, 1)
            over_units(act, phase, body)

        def dve_residual(dve, phase, c0, n, tiles):
            def body(j, u, i):
                dve.wait_ge(act_out, u + 1)
                x = xT[:, bass.ds(i * tiles, tiles), c0:c0 + n]
                dve.tensor_tensor(x, x, stage_buf[:, j % 2, 0:tiles * n].rearrange("p (m t) -> p m t", t=n), ALU.add)\
                    .then_inc(dve_out, 1)
            over_units(dve, phase, body)

        def pe_ffn(pe, r, c0, n):
            pe_feature_tiles(pe, f"up{r}", 2, hT, c0, n, per_bank=1)
            meet["pe"]()
            pe_feature_tiles(pe, f"down{r}", 1, hidden, 0, n, kt=FT)

        def act_ffn(act, r, c0, n, gates):
            def body(j, u, i):
                act.wait_ge(unit_done, u + 1)
                act.wait_ge(dve_out, u - 1)
                act.activation(stage_buf[:, j % 2, 0:n], ps[:, 2 * (j % 2), 0:n], ACT.Silu).then_inc(act_out, 1)
            over_units(act, f"up{r}", body)
            meet["act"]()
            act_residual(act, f"down{r}", n, gates, 1)

        def dve_ffn(dve, r, c0, n):
            def body(j, u, i):
                dve.wait_ge(act_out, u + 1)
                dve.tensor_tensor(hidden[:, bass.ds(i, 1), 0:n].rearrange("p a n -> p (a n)"),
                                  stage_buf[:, j % 2, 0:n], ps[:, 2 * (j % 2) + 1, 0:n], ALU.mult).then_inc(dve_out, 1)
            over_units(dve, f"up{r}", body)
            meet["dve"]()
            dve_residual(dve, f"down{r}", c0, n, 1)

        norm_sq, norm_sum, norm_rt = sem("norm_sq"), sem("norm_sum"), sem("norm_rt")
        square = work[:, WORK - 4096 - 2048 - 512:WORK - 2048 - 512].rearrange("p (m t) -> p m t", t=TA)
        rstd = work[:, WORK - 2048 - 512:WORK - 2048]

        def pe_norm(pe, r, c0, n):
            pe.wait_ge(norm_sq, r + 1)
            for k in range(KT):
                mm = pe.matmul(ps[:, 5, 0:n], K("ones"), square[:, k, 0:n], start=(k == 0), stop=(k == KT - 1))
            mm.then_inc(norm_sum, 1)

        def act_norm(act, r, c0, n):
            act.activation(square[:, :, 0:n], xT[:, :, c0:c0 + n], ACT.Square, scale=1.0 / 32).then_inc(norm_sq, 1)
            act.wait_ge(norm_sum, r + 1)
            act.activation(rstd[:, 0:n], ps[:, 5, 0:n], ACT.Sqrt, bias=eps_col[:, 0:1]).then_inc(norm_rt, 1)

        def dve_norm(dve, r, c0, n, dst, scale, shift):
            dve.wait_ge(norm_rt, r + 1)
            link(dve.reciprocal(rstd[:, 0:n], rstd[:, 0:n]))
            link(dve.tensor_tensor(square[:, :, 0:n], xT[:, :, c0:c0 + n],
                                   rstd[:, 0:n].unsqueeze(1).broadcast_to([P, KT, n]), ALU.mult))
            for m in range(KT):
                for (lo, hi, s), (_, _, b) in zip(scale(m), shift(m)):
                    if b is None:
                        dve.tensor_scalar(dst[:, m, c0 + lo:c0 + hi], square[:, m, lo:hi], s, None, ALU.mult)
                    else:
                        dve.tensor_scalar(dst[:, m, c0 + lo:c0 + hi], square[:, m, lo:hi], s, b, ALU.mult, ALU.add)

        def segments(c0, n, col):
            return [(s * T - c0, s * T - c0 + T, col(s)) for s in range(2) if c0 <= s * T]

        from_blocks = {"pe": [], "act": [], "dve": [], "pool": []}
        meet, links = {}, {}

        def link(ins):
            links["dve"](ins)

        def alink(ins):
            links["act"](ins)

        def plink(ins):
            links["pool"](ins)

        cond = work[:, 0:KT * 32].rearrange("p (k c) -> p k c", c=32)
        mcol = lambda part, m, s: mod[:, part * KT + m, s:s + 1]

        def dve_mod(dve, layer):
            link(dve.tensor_tensor(mod[:, :, :], ps[:, 4, 0:96].rearrange("p (m s) -> p m s", s=2),
                                   C(f"b_ada{layer}", 0, 48).unsqueeze(2).broadcast_to([P, 48, 2]), ALU.add))
            for i, (part, name) in enumerate(((1, "norm_mix"), (4, "norm_ffn"))):
                link(dve.scalar_tensor_tensor(out=scl[:, i], in0=mod[:, part * KT:(part + 1) * KT, :], scalar=1.0,
                                              in1=C(f"{name}{layer}", 0, 8).unsqueeze(2).broadcast_to([P, KT, 2]),
                                              op0=ALU.add, op1=ALU.mult))

        FM_ORDER = [(AQ, False), (AQ + 2, False), (MQ, False), (MO, False), (MK, True), (AK, True)]

        def unit_tokens(layer, full):
            return (0, TA) if full or layer < DEPTH - 1 else (T, T)

        def pe_project(pe, layer):
            def body(j, u, i):
                tile, full = FM_ORDER[i]
                c0, n = unit_tokens(layer, full)
                pe_unit_ready(pe, j, u)
                for m in range(min(2, FM_TILES - tile)):
                    for k in range(KT):
                        mm = pe.matmul(ps[:, 2 * (j % 2) + m, 0:n], ring[:, j, (m * KT + k) * P:(m * KT + k + 1) * P],
                                       hT[:, k, c0:c0 + n], start=(k == 0), stop=(k == KT - 1))
                mm.then_inc(unit_done, 1)
            straight_units(f"fm{layer}", body)
            for phase, cols, spare in ((f"tma{layer}", 272, 4), (f"tmb{layer}", 384, 6)):
                def body(j, u, i):
                    pe_unit_ready(pe, j, u)
                    for tt in range(4):
                        bank = 2 * (j % 2) + tt if tt < 2 else spare + tt - 2
                        for k in range(KT):
                            mm = pe.matmul(ps[:, bank, 0:cols], hT[:, k, tt * P:(tt + 1) * P],
                                           ring[:, j, k * cols:(k + 1) * cols], start=(k == 0), stop=(k == KT - 1))
                    mm.then_inc(unit_done, 1)
                straight_units(phase, body)

        def straight_units(phase, body):
            first, n = FIRST[phase], dict((a, b) for a, b, _ in PHASES)[phase]
            for i in range(n):
                body((first + i) % SLOTS, first + i, i)

        def evacuate_project(eng, copy, my_out, layer, me):
            def body(j, u, i):
                tile, full = FM_ORDER[i]
                c0, n = unit_tokens(layer, full)
                eng.wait_ge(unit_done, u + 1)
                if tile + 1 < FM_TILES:
                    ins = copy(proj[:, tile + me, c0:c0 + n], ps[:, 2 * (j % 2) + me, 0:n])
                else:
                    if me:
                        eng.wait_ge(act_out, u + 1)
                    ins = copy(proj[:, tile, me * T:(me + 1) * T], ps[:, 2 * (j % 2), me * T:(me + 1) * T])
                ins.then_inc(my_out, 1)
            straight_units(f"fm{layer}", body)
            for phase, cols, at, spare in ((f"tma{layer}", 272, MV, 4), (f"tmb{layer}", 384, AV, 6)):
                def body(j, u, i):
                    eng.wait_ge(unit_done, u + 1)
                    bank = spare if me else 2 * (j % 2)
                    copy(tm[:, 2 * me:2 * me + 2, at:at + cols], ps[:, bank:bank + 2, 0:cols]).then_inc(my_out, 1)
                straight_units(phase, body)

        qk_sq, qk_sum, qk_rt, qk_n, qk_rot, qk_cos, qk_r = (
            sem(f"qk_{x}") for x in ("sq", "sum", "rt", "n", "rot", "cos", "r"))
        qa = Area(mixer_free)
        qk_buf = [[qa(TA) for _ in range(2)] for _ in range(4)]

        def qk_tiles(layer):
            c0, n = unit_tokens(layer, False)
            return [(AQ + m, c0, n, f"q_norm{layer}") for m in range(4)] + [(AK, 0, TA, f"k_norm{layer}")]

        def pe_qk(pe, layer):
            for i, (m, c0, n, _) in enumerate(qk_tiles(layer), 5 * layer):
                pe.wait_ge(qk_sq, i + 1)
                if i >= 2:
                    pe.wait_ge(qk_rt, i - 1)
                pe.matmul(ps[:, 4 + i % 2, 0:n], K("blockones"), qk_buf[0][i % 2][:, 0:n], start=True, stop=True)\
                    .then_inc(qk_sum, 1)
                if i > 5 * layer:
                    rotate(pe, i - 1, qk_tiles(layer)[i - 1 - 5 * layer])
            rotate(pe, 5 * layer + 4, qk_tiles(layer)[4])

        def rotate(pe, i, tile):
            m, c0, n, _ = tile
            pe.wait_ge(qk_n, i + 1)
            if i >= 2:
                pe.wait_ge(qk_r, i - 1)
            pe.matmul(ps[:, 6 + i % 2, 0:n], K("rot1"), qk_buf[1][i % 2][:, 0:n], start=True, stop=True)\
                .then_inc(qk_rot, 1)

        def act_qk(act, layer):
            for i, (m, c0, n, _) in enumerate(qk_tiles(layer), 5 * layer):
                if i >= 2:
                    act.wait_ge(qk_sum, i - 1)
                act.activation(qk_buf[0][i % 2][:, 0:n], proj[:, m, c0:c0 + n], ACT.Square, scale=0.125)\
                    .then_inc(qk_sq, 1)
                if i > 5 * layer:
                    root(act, i - 1, qk_tiles(layer)[i - 1 - 5 * layer][2])
            root(act, 5 * layer + 4, qk_tiles(layer)[4][2])

        def root(act, i, n):
            act.wait_ge(qk_sum, i + 1)
            if i >= 2:
                act.wait_ge(qk_r, i - 1)
            act.activation(qk_buf[3][i % 2][:, 0:n], ps[:, 4 + i % 2, 0:n], ACT.Sqrt, bias=eps_col[:, 0:1]).then_inc(qk_rt, 1)

        def dve_qk(dve, layer):
            def finish(i, tile):
                m, c0, n, _ = tile
                dve.wait_ge(qk_rot, i + 1)
                link(dve.tensor_tensor(qk_buf[3][i % 2][:, 0:n], ps[:, 6 + i % 2, 0:n], K("sin1")[:, c0:c0 + n], ALU.mult))
                dve.wait_ge(qk_cos, i + 1)
                dve.tensor_tensor(proj[:, m, c0:c0 + n], qk_buf[2][i % 2][:, 0:n], qk_buf[3][i % 2][:, 0:n], ALU.add)\
                    .then_inc(qk_r, 1)
                dve.wait_ge(qk_r, i + 1)
            tiles = qk_tiles(layer)
            for i, (m, c0, n, gain) in enumerate(tiles, 5 * layer):
                dve.wait_ge(qk_rt, i + 1)
                link(dve.reciprocal(qk_buf[3][i % 2][:, 0:n], qk_buf[3][i % 2][:, 0:n]))
                if i >= 2:
                    dve.wait_ge(qk_cos, i - 1)
                dve.scalar_tensor_tensor(out=qk_buf[1][i % 2][:, 0:n], in0=proj[:, m, c0:c0 + n], scalar=C(gain),
                                         in1=qk_buf[3][i % 2][:, 0:n], op0=ALU.mult, op1=ALU.mult).then_inc(qk_n, 1)
                dve.wait_ge(qk_n, i + 1)
                if i > 5 * layer:
                    finish(i - 1, tiles[i - 1 - 5 * layer])
            finish(5 * layer + 4, tiles[4])

        def pool_qk(pool, layer):
            for i, (m, c0, n, _) in enumerate(qk_tiles(layer), 5 * layer):
                pool.wait_ge(qk_n, i + 1)
                if i >= 2:
                    pool.wait_ge(qk_r, i - 1)
                pool.tensor_tensor(qk_buf[2][i % 2][:, 0:n], qk_buf[1][i % 2][:, 0:n], K("cos1")[:, c0:c0 + n], ALU.mult)\
                    .then_inc(qk_cos, 1)

        at_s, at_max, at_exp, at_p, at_t, at_pt, at_o, at_out = (
            sem(f"at_{x}") for x in ("scores", "max", "exp", "probs", "turned", "probsT", "o", "out"))
        aa = Area(mixer_free)
        probs = [aa(768) for _ in range(2)]
        probsT = [aa(768) for _ in range(2)]
        at_small = aa(4 * 64).rearrange("p (k n) -> p k n", k=4)
        at_masked = [aa(768) for _ in range(2)]

        def attention_units(layer):
            tiles = range(4) if layer < DEPTH - 1 else range(2, 4)
            return [(qt, h // 2, h % 2, (2 if qt < 2 else 4) * P) for qt in tiles for h in range(8)]

        AT_BASE = [0, 32, 48]

        def pe_attention(pe, layer):
            units, base = attention_units(layer), AT_BASE[layer]
            n = len(units)
            for i in range(n + 2):
                if i < n:
                    qt, j, b, nk = units[i]
                    g = base + i
                    if i >= 2:
                        pe.wait_ge(at_exp, g - 1)
                    pe.matmul(ps[:, 4 + g % 2, 0:nk], proj[64 * b:64 * b + 64, AQ + j, qt * P:(qt + 1) * P],
                              proj[64 * b:64 * b + 64, AK, 0:nk], start=True, stop=True).then_inc(at_s, 1)
                if 1 <= i <= n:
                    qt, j, b, nk = units[i - 1]
                    g = base + i - 1
                    pe.wait_ge(at_p, g + 1)
                    if i >= 3:
                        pe.wait_ge(at_pt, g - 1)
                    for s in range(nk // P):
                        mm = pe.transpose(ps[:, 6 + g % 2, s * P:(s + 1) * P], probs[g % 2][:, s * P:(s + 1) * P], K("ident"))
                    mm.then_inc(at_t, 1)
                if i >= 2:
                    qt, j, b, nk = units[i - 2]
                    g = base + i - 2
                    pe.wait_ge(at_pt, g + 1)
                    if i - 2 >= 8 and b == 0:
                        pe.wait_ge(at_out, g // 2 - 3)
                    for s in range(nk // P):
                        mm = pe.matmul(ps[64 * b:64 * b + 64, (g // 2) % 4, 0:P], tm[:, s, AV + 64 * b:AV + 64 * b + 64],
                                       probsT[g % 2][:, s * P:(s + 1) * P], start=(s == 0), stop=(s == nk // P - 1),
                                       skip_group_check=True)
                    mm.then_inc(at_o, 1)

        def act_attention(act, layer):
            units, base = attention_units(layer), AT_BASE[layer]
            for i, (qt, j, b, nk) in enumerate(units):
                g = base + i
                act.wait_ge(at_max, g + 1)
                if i >= 2:
                    act.wait_ge(at_t, g - 1)
                act.activation(probs[g % 2][:, 0:nk], ps[:, 4 + g % 2, 0:nk], ACT.Exp, scale=0.125,
                               bias=at_small[:, 1, i:i + 1], accum_out=at_small[:, 2, i:i + 1]).then_inc(at_exp, 1)
                if i >= 1:
                    turned(act, g - 1, units[i - 1][3], i - 1)
            turned(act, base + len(units) - 1, units[-1][3], len(units) - 1)

        def turned(act, g, nk, i):
            act.wait_ge(at_t, g + 1)
            if i >= 2:
                act.wait_ge(at_o, g - 1)
            act.activation(probsT[g % 2][:, 0:nk], ps[:, 6 + g % 2, 0:nk], ACT.Copy).then_inc(at_pt, 1)

        def dve_attention(dve, layer):
            units, base = attention_units(layer), AT_BASE[layer]
            n = len(units)
            for i in range(n + 3):
                if i < n:
                    qt, j, b, nk = units[i]
                    g = base + i
                    dve.wait_ge(at_s, g + 1)
                    link(dve.tensor_reduce(at_small[:, 0, i:i + 1], ps[:, 4 + g % 2, 0:nk], AX, ALU.max))
                    dve.tensor_scalar(at_small[:, 1, i:i + 1], at_small[:, 0, i:i + 1], -0.125, None, ALU.mult)\
                        .then_inc(at_max, 1)
                if 1 <= i <= n:
                    normalise(dve, base + i - 1, i - 1, units[i - 1][3])
                if i >= 3:
                    qt, j, b, nk = units[i - 3]
                    if b == 1:
                        pair = (base + i - 3) // 2
                        dve.wait_ge(at_o, base + i - 2)
                        dve.tensor_copy(mixT[:, j, qt * P:(qt + 1) * P], ps[:, pair % 4, 0:P]).then_inc(at_out, 1)

        def normalise(dve, g, i, nk):
            dve.wait_ge(at_exp, g + 1)
            link(dve.reciprocal(at_small[:, 3, i:i + 1], at_small[:, 2, i:i + 1]))
            dve.tensor_scalar(probs[g % 2][:, 0:nk], probs[g % 2][:, 0:nk], at_small[:, 3, i:i + 1], None, ALU.mult)\
                .then_inc(at_p, 1)

        pl_mean, pl_in, pl_y, pl_out = (sem(f"pl_{x}") for x in ("mean", "in", "y", "out"))
        pa = Area(mixer_free)
        pooled = pa(2 * TA).rearrange("p (g t) -> p g t", t=TA)

        def pool_segments(layer):
            return (0, 1) if layer < DEPTH - 1 else (1,)

        def pe_pool(pe, layer):
            for seg in pool_segments(layer):
                for g in range(4):
                    b = 64 * (g % 2)
                    for s in range(2):
                        mm = pe.matmul(ps[b:b + 64, seg, (g // 2) * T:(g // 2 + 1) * T],
                                       tm[:, 2 * seg + s, PP + 64 * g:PP + 64 * g + 64],
                                       K("band")[:, (s * 4 + g) * T:(s * 4 + g + 1) * T], start=(s == 0), stop=(s == 1),
                                       skip_group_check=True)
            mm.then_inc(pl_mean, 1)
            pe.wait_ge(pl_in, layer + 1)
            c0, n = unit_tokens(layer, False)
            for g in range(4):
                b = 64 * (g % 2)
                mm = pe.matmul(ps[b:b + 64, 2 + g // 2, 0:n], C(f"pool_w{layer}", 64 * (g // 2), 64, slice(b, b + 64)),
                               pooled[b:b + 64, g // 2, c0:c0 + n], start=True, stop=True, skip_group_check=True)
            mm.then_inc(pl_y, 1)

        def dve_pool(dve, layer):
            dve.wait_ge(pl_mean, layer + 1)
            for seg in pool_segments(layer):
                ins = dve.tensor_copy(pooled[:, :, seg * T:(seg + 1) * T], ps[:, seg, :].rearrange("p (g t) -> p g t", g=2))
            ins.then_inc(pl_in, 1)
            dve.wait_ge(pl_y, layer + 1)
            c0, n = unit_tokens(layer, False)
            for g in range(2):
                dve.tensor_scalar(mixT[:, 6 + g, c0:c0 + n], ps[:, 2 + g, 0:n], C(f"pool_scale{layer}", g), None, ALU.mult)

        ml_t, ml_abs, ml_ln, ml_rows, ml_cols, ml_d, ml_enm = (
            sem(f"ml_{x}") for x in ("gates_t", "abs", "ln", "rows", "cols", "dcols", "enm"))
        ml_nb, ml_nbs, ml_s, ml_z, ml_e, ml_ez, ml_p, ml_num, ml_h = (
            sem(f"ml_{x}") for x in ("nb", "nb_sb", "s", "z", "e", "masked", "p", "num", "h"))
        ml_sq, ml_hn, ml_hT, ml_one = (sem(f"ml_{x}") for x in ("sq", "hn", "hT", "vones"))
        ma = Area(mixer_free)
        vones = ma(4 * 4 * 65).rearrange("p (t h c) -> p t h c", t=4, h=4)
        ml_pre = mixT[0:4, 0:4, :]
        ml_row = hT[0:4, 0:8, :]
        ml_e1 = mixT[0:4, 6:8, :]
        zero_row = ma(TA)
        cols = ma(64).rearrange("p (k d t h) -> p k d t h", k=2, d=2, t=4)
        nb = ma(2 * 2 * TA).rearrange("p (b d t) -> p b d t", b=2, d=2)
        pbuf = ma(8 * TA).rearrange("p (s d t) -> p s d t", s=4, d=2)
        ebuf = ma(4 * TA).rearrange("p (b d t) -> p b d t", b=2, d=2)
        hsum = hT[:, 0:2, :].rearrange("p a (t h v) -> p (a t) h v", h=4, v=64)
        hnum = hT[:, 2:6, :].rearrange("p (d a) (t h v) -> p d (a t) h v", d=2, h=4, v=64)
        hden = ma(3 * 2 * 4).rearrange("p (k d t) -> p k d t", k=3, d=2)
        hss = ma(2 * 16).rearrange("p (k n) -> p k n", k=2)

        def ml_range(s, d, c0):
            lo, hi = (s * P, TA) if d == 0 else ((0, TA) if s < 2 else (T, T + P) if s == 2 else (T, TA))
            return max(lo, c0), hi

        def ml_sources(tt, d):
            if d == 0:
                return range(0, tt + 1)
            return range(tt, 2) if tt < 2 else [0, 1] + list(range(tt, 4))

        def ml_tiles(layer):
            return range(0, 4) if layer < DEPTH - 1 else range(2, 4)

        def pe_mlstm(pe, layer):
            c0, _ = unit_tokens(layer, False)
            for ty in range(4):
                for tt in range(4):
                    mm = pe.transpose(ps[0:4, 4 + ty, tt * P:(tt + 1) * P], tm[:, tt, MG + 4 * ty:MG + 4 * ty + 4], K("ident"))
            mm.then_inc(ml_t, 1)
            pe.wait_ge(ml_rows, layer + 1)
            for k, row in enumerate((2, 0)):
                for d in range(2):
                    for tt in range(4):
                        mm = pe.transpose(ps[:, 4, 4 * ((k * 2 + d) * 4 + tt):4 * ((k * 2 + d) * 4 + tt) + 4],
                                          ml_row[:, row + d, tt * P:(tt + 1) * P], K("ident")[0:4, 0:4])
            mm.then_inc(ml_cols, 1)
            for h in range(4):
                hh = 4 * layer + h
                b = 64 * (h % 2)
                for d in range(2):
                    n = 2 * hh + d
                    if n > 8 * layer:
                        pe.wait_ge(ml_nbs, n)
                    pe.matmul(ps[:, 5, 0:TA], K("sel")[0:4, h * P:(h + 1) * P], ml_row[:, 6 + d, :], start=True, stop=True)\
                        .then_inc(ml_nb, 1)
                for s in range(4):
                    n = 4 * hh + s
                    if n >= 2 + 16 * layer:
                        pe.wait_ge(ml_p, n - 1)
                    pe.matmul(ps[:, n % 2, c0:TA], proj[b:b + 64, MK + h // 2, s * P:(s + 1) * P],
                              proj[b:b + 64, MQ + h // 2, c0:TA], start=True, stop=True).then_inc(ml_s, 1)
                pe.wait_ge(ml_p, 4 * hh + 4)
                if h >= 2:
                    pe.wait_ge(ml_h, hh - 1)
                for d in range(2):
                    for tt in ml_tiles(layer):
                        src = list(ml_sources(tt, d))
                        for s in src:
                            mm = pe.matmul(ps[:, (6 if h % 2 else 2) + d, 65 * tt:65 * tt + 65], pbuf[:, s, d, tt * P:(tt + 1) * P],
                                           vones[:, s, h, :], start=(s == src[0]), stop=(s == src[-1]))
                mm.then_inc(ml_num, 1)
            pe.wait_ge(ml_hn, layer + 1)
            for tt in ml_tiles(layer):
                for f in range(2):
                    mm = pe.transpose(ps[:, f, tt * P:(tt + 1) * P],
                                      hsum[:, tt, 2 * f:2 * f + 2, :].rearrange("p h v -> p (h v)"), K("ident"))
            mm.then_inc(ml_hT, 1)

        def act_mlstm(act, layer):
            c0, n = unit_tokens(layer, False)
            act.wait_ge(ml_abs, layer + 1)
            alink(act.activation(ml_e1, ml_e1, ACT.Exp, scale=-1.0))
            act.activation(ml_e1, ml_e1, ACT.Ln, bias=1.0).then_inc(ml_ln, 1)
            act.wait_ge(ml_cols, layer + 1)
            act.activation(cols[:, 1].rearrange("p d t h -> p (d t h)"), ps[:, 4, 32:64], ACT.Exp, scale=-1.0)\
                .then_inc(ml_enm, 1)
            k = 16 * layer * 2
            for h in range(4):
                hh = 4 * layer + h
                for d in range(2):
                    act.wait_ge(ml_nb, 2 * hh + d + 1)
                    if h >= 2:
                        act.wait_ge(ml_z, 8 * (hh - 1))
                    act.activation(nb[:, h % 2, d, :], ps[:, 5, 0:TA], ACT.Copy).then_inc(ml_nbs, 1)
                for s in range(4):
                    for d in range(2):
                        lo, hi = ml_range(s, d, c0)
                        m = 8 * hh + 2 * s + d
                        act.wait_ge(ml_z, m + 1)
                        act.activation(ebuf[:, s % 2, d, lo:hi], ebuf[:, s % 2, d, lo:hi], ACT.Exp).then_inc(ml_e, 1)
            act.wait_ge(ml_h, 4 * layer + 4)
            act.wait_ge(ml_hsum, layer + 1)
            t0 = ml_tiles(layer)[0]
            act.activation(hnum[:, 0, t0:4], hsum[:, t0:4], ACT.Square, scale=0.125).then_inc(ml_sq, 1)
            act.activation(proj[:, MO:MO + 2, c0:TA], proj[:, MO:MO + 2, c0:TA], ACT.Sigmoid).then_inc(ml_sig, 1)
            act.wait_ge(ml_ss, layer + 1)
            nn = (4 - t0) * 4
            act.activation(hss[:, 1, 0:nn], hss[:, 0, 0:nn], ACT.Sqrt, bias=eps_col[:, 0:1]).then_inc(ml_rt, 1)

        ml_hsum, ml_sig, ml_ss, ml_rt = sem("ml_hsum"), sem("ml_sig"), sem("ml_ss"), sem("ml_rt")

        def pool_mlstm(pool, layer):
            c0, _ = unit_tokens(layer, False)
            pool.memset(vones[:, :, :, 64:65], 1.0)
            for tt in range(4):
                ins = pool.tensor_copy(vones[:, tt, :, 0:64], tm[:, tt, MV:MV + 256].rearrange("p (h v) -> p h v", h=4))
            ins.then_inc(ml_one, 1)
            for h in range(4):
                for s in range(4):
                    for d in range(2):
                        m = 8 * (4 * layer + h) + 2 * s + d
                        pool.wait_ge(ml_e, m + 1)
                        lo, hi = ml_range(s, d, c0)
                        if lo <= s * P < hi:
                            diag = ebuf[:, s % 2, d, s * P:(s + 1) * P]
                            pool.tensor_tensor(diag, diag, K(f"tri{d}"), ALU.mult).then_inc(ml_ez, 1)

        def dve_mlstm(dve, layer):
            c0, _ = unit_tokens(layer, False)
            dve.memset(zero_row, 0.0)
            dve.wait_ge(ml_t, layer + 1)
            for ty in range(4):
                ins = dve.tensor_scalar(ml_pre[:, ty, :], ps[0:4, 4 + ty, :], C(f"b_gates{layer}", ty, 1, slice(0, 4)), None, ALU.add)
            link(ins)
            lf, li = ml_pre[:, 1:4:2, :], ml_pre[:, 0:4:2, :]
            dve.scalar_tensor_tensor(out=ml_e1, in0=lf, scalar=-1.0, in1=lf, op0=ALU.mult, op1=ALU.max).then_inc(ml_abs, 1)
            dve.wait_ge(ml_ln, layer + 1)
            link(dve.scalar_tensor_tensor(out=lf, in0=lf, scalar=0.0, in1=ml_e1, op0=ALU.min, op1=ALU.subtract))
            z = zero_row[0:4, :]
            B, Dr, M, NM = (ml_row[:, 2 * k:2 * k + 2, :] for k in range(4))

            def scans(dst, a, b, op):
                dve.tensor_tensor_scan(dst[:, 0, :], a[:, 0, :], b[:, 0, :], 0.0, op, op)
                link(dve.tensor_tensor_scan(dst[:, 1, 0:T][:, ::-1], a[:, 1, 0:T][:, ::-1], b[:, 1, 0:T][:, ::-1], 0.0, op, op))
                link(dve.tensor_tensor_scan(dst[:, 1, T:TA][:, ::-1], a[:, 1, T:TA][:, ::-1], b[:, 1, T:TA][:, ::-1],
                                            dst[:, 1, 0:1], op, op))
            scans(B, lf, z.unsqueeze(1).broadcast_to([4, 2, TA]), ALU.add)
            link(dve.tensor_tensor(Dr, li, B, ALU.subtract))
            scans(M, Dr, Dr, ALU.max)
            dve.tensor_scalar(NM, M, -1.0, None, ALU.mult)
            dve.tensor_tensor(B, B, M, ALU.add).then_inc(ml_rows, 1)
            dve.wait_ge(ml_enm, layer + 1)
            link(dve.tensor_copy(cols[:, 0].rearrange("p d t h -> p (d t h)"), ps[:, 4, 0:32]))
            ez = 0
            for h in range(4):
                hh = 4 * layer + h
                for s in range(4):
                    n = 4 * hh + s
                    for d in range(2):
                        lo, hi = ml_range(s, d, c0)
                        m = 8 * hh + 2 * s + d
                        dve.wait_ge(ml_nbs, 2 * hh + d + 1)
                        dve.tensor_scalar(ebuf[:, s % 2, d, lo:hi], nb[:, h % 2, d, lo:hi], cols[:, 0, d, s, h:h + 1], 0.0,
                                          ALU.add, ALU.min).then_inc(ml_z, 1)
                    dve.wait_ge(ml_s, n + 1)
                    if s == 0 and h >= 1:
                        dve.wait_ge(ml_num, hh)
                    for d in range(2):
                        lo, hi = ml_range(s, d, c0)
                        m = 8 * hh + 2 * s + d
                        dve.wait_ge(ml_e, m + 1)
                        if lo <= s * P < hi:
                            ez += 1
                            dve.wait_ge(ml_ez, ML_EZ[layer] + ez)
                        ins = dve.scalar_tensor_tensor(out=pbuf[:, s, d, lo:hi], in0=ps[:, n % 2, lo:hi], scalar=0.125,
                                                       in1=ebuf[:, s % 2, d, lo:hi], op0=ALU.mult, op1=ALU.mult)
                        if d == 0:
                            link(ins)
                    ins.then_inc(ml_p, 1)
                    dve.wait_ge(ml_p, n + 1)
                dve.wait_ge(ml_num, hh + 1)
                dve.wait_ge(ml_enm, layer + 1)
                bank = 6 if h % 2 else 2
                t0 = ml_tiles(layer)[0]
                both = ps[:, bank:bank + 2, 0:260].rearrange("p d (t c) -> p d t c", c=65)[:, :, t0:4]
                link(dve.tensor_copy(hden[:, 0, :, t0:4], both[:, :, :, 64]))
                link(dve.scalar_tensor_tensor(out=hden[:, 1, :, t0:4], in0=hden[:, 0, :, t0:4], scalar=-1.0,
                                              in1=hden[:, 0, :, t0:4], op0=ALU.mult, op1=ALU.max))
                link(dve.tensor_tensor(hden[:, 1, :, t0:4], hden[:, 1, :, t0:4], cols[:, 1, :, t0:4, h], ALU.max))
                link(dve.reciprocal(hden[:, 2, :, t0:4], hden[:, 1, :, t0:4]))
                for d in range(2):
                    ins = dve.tensor_tensor(hnum[:, d, t0:4, h, :], both[:, d, :, 0:64],
                                            hden[:, 2, d, t0:4].unsqueeze(2).broadcast_to([P, 4 - t0, 64]), ALU.mult)
                ins.then_inc(ml_h, 1)
                dve.wait_ge(ml_h, hh + 1)
            dve.tensor_tensor(hsum[:, t0:4], hnum[:, 0, t0:4], hnum[:, 1, t0:4], ALU.add).then_inc(ml_hsum, 1)
            dve.wait_ge(ml_sq, layer + 1)
            nn = (4 - t0) * 4
            dve.tensor_reduce(hss[:, 0, 0:nn], hnum[:, 0, t0:4].rearrange("p t h v -> p (t h) v"), AX, ALU.add)\
                .then_inc(ml_ss, 1)
            dve.wait_ge(ml_rt, layer + 1)
            link(dve.reciprocal(hss[:, 1, 0:nn], hss[:, 1, 0:nn]))
            hs = hsum[:, t0:4].rearrange("p t h v -> p (t h) v")
            dve.tensor_tensor(hs, hs, hss[:, 1, 0:nn].unsqueeze(2).broadcast_to([P, nn, 64]), ALU.mult).then_inc(ml_hn, 1)
            dve.wait_ge(ml_hT, layer + 1)
            dve.wait_ge(ml_sig, layer + 1)
            for f in range(2):
                dve.scalar_tensor_tensor(out=mixT[:, 4 + f, c0:TA], in0=ps[:, f, c0:TA], scalar=C(f"ml_norm{layer}", f),
                                         in1=proj[:, MO + f, c0:TA], op0=ALU.mult, op1=ALU.mult)

        def ez_total(layer):
            c0 = unit_tokens(layer, False)[0]
            return 4 * sum(ml_range(s, d, c0)[0] <= s * P < ml_range(s, d, c0)[1] for s in range(4) for d in range(2))

        ML_EZ = [0, ez_total(0)]

        a = Area()
        rproj = a(R_TILES * T).rearrange("p (m t) -> p m t", t=T)
        attnT = a(2 * T).rearrange("p (m t) -> p m t", t=T)
        yT = a(KT * T).rearrange("p (m t) -> p m t", t=T)
        second_free = a.at
        a = Area(second_free)
        qkT = a(12 * T).rearrange("p (m t) -> p m t", t=T)
        vtm = a(2 * 768).rearrange("p (k c) -> p k c", c=768)
        s_probs = [a(768) for _ in range(2)]
        s_probsT = [a(768) for _ in range(2)]
        s_masked = [a(768) for _ in range(2)]
        s_small = a(64).rearrange("p (k n) -> p k n", k=4)
        s_cos = [a(2 * T) for _ in range(2)]
        s_sin = [a(2 * T) for _ in range(2)]
        a = Area(second_free)
        ya = a(KT * T).rearrange("p (m t) -> p m t", t=T)
        yr = a(KT * T).rearrange("p (m t) -> p m t", t=T)
        merged = a(KT * T).rearrange("p (m t) -> p m t", t=T)

        def copy_out(eng, copy, my_out, phase, pieces):
            def body(j, u, i):
                eng.wait_ge(unit_done, u + 1)
                for o, s in pieces(j, i):
                    ins = copy(o, s)
                ins.then_inc(my_out, 1)
            over_units(eng, phase, body)

        def three_tiles(dst, me):
            def pieces(j, i):
                if me == 0:
                    return [(dst[:, bass.ds(i * 3, 2), :], ps[:, 2 * (j % 2), :].rearrange("p (m t) -> p m t", t=T))]
                return [(dst[:, bass.ds(i * 3 + 2, 1), :], ps[:, 2 * (j % 2) + 1, 0:T].unsqueeze(1))]
            return pieces

        def value_halves(me):
            def pieces(j, i):
                return [(vtm[:, me, i * 384:(i + 1) * 384], ps[:, 2 * (j % 2) + me, 0:384])]
            return pieces

        def lora_tiles(me):
            def pieces(j, i):
                if me == 0:
                    return [(rproj[:, RL:RL + 2, :], ps[:, 2 * (j % 2), :].rearrange("p (m t) -> p m t", t=T))]
                return [(rproj[0:32, RL + 2, :], ps[0:32, 2 * (j % 2) + 1, 0:T])]
            return pieces

        def bank_each(dst, me, per):
            def pieces(j, i):
                return [(dst[:, i * 2 * per + me * per:i * 2 * per + (me + 1) * per, :],
                         ps[:, 2 * (j % 2) + me, 0:per * T].rearrange("p (m t) -> p m t", t=T))]
            return pieces

        def pe_values(pe):
            def body(j, u, i):
                pe_unit_ready(pe, j, u)
                for tt in range(2):
                    for k in range(KT):
                        mm = pe.matmul(ps[:, 2 * (j % 2) + tt, 0:384], hT[:, k, T + tt * P:T + (tt + 1) * P],
                                       ring[:, j, k * 384:(k + 1) * 384], start=(k == 0), stop=(k == KT - 1))
                mm.then_inc(unit_done, 1)
            straight_units("v", body)

        def pe_lora(pe):
            def body(j, u, i):
                pe_unit_ready(pe, j, u)
                for at, m, bank, o in ((0, P, 0, 0), (P, P, 0, T), (2 * P, 32, 1, 0)):
                    for k in range(KT):
                        w = ring[:, j, k * 288 + at:k * 288 + at + m]
                        mm = pe.matmul(ps[0:m, 2 * (j % 2) + bank, o:o + T], w, hT[:, k, T:TA],
                                       start=(k == 0), stop=(k == KT - 1))
                mm.then_inc(unit_done, 1)
            straight_units("lora", body)

        sr_rot, sr_cos, sr_out = (sem(f"sr_{x}") for x in ("rot", "cos", "out"))
        two = lambda v: v.rearrange("p (m t) -> p m t", t=T)

        def pe_rope(pe):
            for i in range(6):
                if i >= 2:
                    pe.wait_ge(sr_out, i - 1)
                pe.matmul(ps[:, 4 + i % 2, :], K("rot2"), qkT[:, 2 * i:2 * i + 2, :].rearrange("p m t -> p (m t)"),
                          start=True, stop=True).then_inc(sr_rot, 1)

        def pool_rope(pool):
            for i in range(6):
                if i >= 2:
                    pool.wait_ge(sr_out, i - 1)
                pool.tensor_tensor(two(s_cos[i % 2]), qkT[:, 2 * i:2 * i + 2, :],
                                   K("cos2").unsqueeze(1).broadcast_to([P, 2, T]), ALU.mult).then_inc(sr_cos, 1)

        def dve_rope(dve):
            for i in range(6):
                dve.wait_ge(sr_rot, i + 1)
                link(dve.tensor_tensor(two(s_sin[i % 2]), two(ps[:, 4 + i % 2, :]),
                                       K("sin2").unsqueeze(1).broadcast_to([P, 2, T]), ALU.mult))
                dve.wait_ge(sr_cos, i + 1)
                dve.tensor_tensor(qkT[:, 2 * i:2 * i + 2, :], two(s_cos[i % 2]), two(s_sin[i % 2]), ALU.add)\
                    .then_inc(sr_out, 1)

        S_UNITS = [(qt, hh) for qt in range(2) for hh in range(4)]
        s_max, s_copied = sem("s_max"), sem("s_copied")
        SB = 48

        def score_banks(i):
            return 4 if i % 2 == 0 else 2

        def s_scores(i, w):
            return ps[:, score_banks(i):score_banks(i) + 2, :].rearrange("p b n -> p (b n)")[:, 0:w]

        def pe_dilated(pe):
            n = len(S_UNITS)
            for i in range(n + 2):
                if i < n:
                    qt, hh = S_UNITS[i]
                    nk = (qt + 1) * P
                    b = 64 * (hh % 2)
                    if i >= 2:
                        pe.wait_ge(s_max, i - 1)
                    for g in range(3):
                        m = (4 * g + hh) // 2
                        o = score_banks(i) * 512 + g * nk
                        mm = pe.matmul(ps[:, o // 512, o % 512:o % 512 + nk], qkT[b:b + 64, m, qt * P:(qt + 1) * P],
                                       qkT[b:b + 64, 6 + m, 0:nk], start=True, stop=True)
                    mm.then_inc(at_s, 1)
                if 1 <= i <= n:
                    qt, hh = S_UNITS[i - 1]
                    blocks = 3 * (qt + 1)
                    pe.wait_ge(at_p, SB + i)
                    if i >= 2:
                        pe.wait_ge(at_pt, SB + i - 1)
                    for s in range(blocks):
                        mm = pe.transpose(ps[:, 6 + s // 4, (s % 4) * P:(s % 4 + 1) * P],
                                          s_probs[(i - 1) % 2][:, s * P:(s + 1) * P], K("ident"))
                    mm.then_inc(at_t, 1)
                if i >= 2:
                    qt, hh = S_UNITS[i - 2]
                    b = 64 * (hh % 2)
                    pe.wait_ge(at_pt, SB + i - 1)
                    blocks = [(g, s) for g in range(3) for s in range(qt + 1)]
                    for x, (g, s) in enumerate(blocks):
                        v = vtm[:, s, (4 * g + hh) * 64:(4 * g + hh + 1) * 64]
                        o = ((i - 2) // 2) * P
                        mm = pe.matmul(ps[b:b + 64, 0, o:o + P], v, s_probsT[i % 2][:, x * P:(x + 1) * P],
                                       start=(x == 0), stop=(x == len(blocks) - 1), skip_group_check=True)
                    mm.then_inc(at_o, 1)

        def act_dilated(act):
            def turn(i):
                w = 3 * (S_UNITS[i][0] + 1) * P
                act.wait_ge(at_t, SB + i + 1)
                if i >= 2:
                    act.wait_ge(at_o, SB + i - 1)
                act.activation(s_probsT[i % 2][:, 0:w], ps[:, 6:8, :].rearrange("p b n -> p (b n)")[:, 0:w], ACT.Copy)\
                    .then_inc(at_pt, 1)
            for i, (qt, hh) in enumerate(S_UNITS):
                w = 3 * (qt + 1) * P
                act.wait_ge(at_max, SB + i + 1)
                if i >= 2:
                    act.wait_ge(at_t, SB + i - 1)
                act.activation(s_probs[i % 2][:, 0:w], s_masked[i % 2][:, 0:w], ACT.Exp, scale=0.125,
                               bias=s_small[:, 1, i:i + 1], accum_out=s_small[:, 2, i:i + 1]).then_inc(at_exp, 1)
                if i >= 1:
                    turn(i - 1)
            turn(len(S_UNITS) - 1)

        def dve_dilated(dve):
            n = len(S_UNITS)
            for i in range(n + 1):
                if i < n:
                    qt, hh = S_UNITS[i]
                    w = 3 * (qt + 1) * P
                    dve.wait_ge(at_s, SB + i + 1)
                    if i >= 2:
                        dve.wait_ge(at_exp, SB + i - 1)
                    dve.tensor_tensor(s_masked[i % 2][:, 0:w], s_scores(i, w), K(f"see{qt}"), ALU.add).then_inc(s_max, 1)
                    dve.wait_ge(s_max, i + 1)
                    link(dve.tensor_reduce(s_small[:, 0, i:i + 1], s_masked[i % 2][:, 0:w], AX, ALU.max))
                    dve.tensor_scalar(s_small[:, 1, i:i + 1], s_small[:, 0, i:i + 1], -0.125, None, ALU.mult)\
                        .then_inc(at_max, 1)
                if i >= 1:
                    w = 3 * (S_UNITS[i - 1][0] + 1) * P
                    dve.wait_ge(at_exp, SB + i)
                    link(dve.reciprocal(s_small[:, 3, i - 1:i], s_small[:, 2, i - 1:i]))
                    pr = s_probs[(i - 1) % 2][:, 0:w]
                    dve.tensor_scalar(pr, pr, s_small[:, 3, i - 1:i], None, ALU.mult).then_inc(at_p, 1)
            dve.wait_ge(at_o, SB + n)
            dve.tensor_copy(attnT.rearrange("p m (q t) -> p q m t", q=2),
                            ps[:, 0, :].rearrange("p (q m t) -> p q m t", q=2, m=2))

        GROUPS = KT // 2
        (rw_log, rw_exp, rw_kk, rw_sq, rw_ss, rw_mx, rw_rt, rw_rk, rw_bon, rw_b, rw_lora) = (
            sem(f"rw_{x}") for x in ("log", "exp", "kk", "sq", "ss", "mx", "rt", "rk", "bonus", "b", "lora"))
        (rw_tr, rw_taken, rw_gram, rw_gm, rw_aab, rw_T0, rw_X, rw_P, rw_Pc, rw_U, rw_T, rw_f, rw_fc, rw_z) = (
            sem(f"rw_{x}") for x in ("turned", "taken", "gram", "masked", "aab", "t0", "x", "p", "p_sb", "tp", "t", "f",
                                     "f_sb", "z"))
        (rs_u, rs_U, rs_s, rs_st, rs_y, gn_c, gn_sq, gn_ss, gn_rt, gn_n, gn_t) = (
            sem(f"rs_{x}") for x in ("u", "u_sb", "s", "state", "y", "centred", "sq", "ss", "rt", "normed", "turned"))
        a = Area(second_free)
        pair = lambda: a(2 * T).rearrange("p (j t) -> p j t", j=2)
        g_gate, g_bonus, g_eW = pair(), pair(), pair()
        g_ar = a(4 * T).rearrange("p (j x t) -> p j x t", j=2, x=2)
        g_kt, g_bt = pair(), pair()
        g_at, g_kh, g_bh, g_v = (a(2 * T).rearrange("p (q d) -> p q d", d=HD) for _ in range(4))
        later = a.at
        g_gm = a(8 * 4 * CHUNK).rearrange("p (q x) -> p q x", q=8)
        g_T = a(8 * 2 * CHUNK).rearrange("p (q x t) -> p q x t", q=8, x=2)
        g_X = a((LEVELS - 1) * 8 * CHUNK).rearrange("p (l q t) -> p l q t", l=LEVELS - 1, q=8)
        g_P, g_F, g_Z = (a(8 * CHUNK).rearrange("p (q t) -> p q t", q=8) for _ in range(3))
        g_TA = a(8 * CHUNK).rearrange("p (j c t) -> p j c t", j=2, c=4)
        g_y = a(8 * CHUNK).rearrange("p (q t) -> p q t", q=8)
        g_st = a(2 * 2 * HD).rearrange("p (b j v) -> p b j v", b=2, j=2)
        g_small = a(32).rearrange("p (k n) -> p k n", k=4)
        a = Area(later)
        e_sg, e_ai, e_ls, e_lp, e_le, e_eWp, e_eWi, e_eWe, e_kk, e_rn, e_b, e_kh, e_bh = (pair() for _ in range(13))
        e_sh = a(4 * T).rearrange("p (m t) -> p m t", t=T)
        e_shp = e_kh

        def shift(eng, lk, tile, n, buf, rows=P):
            z, d = rproj[0:rows, tile:tile + n, :], buf[0:rows, 0:n, :]
            eng.tensor_tensor(d[:, :, 1:T], z[:, :, 0:T - 1], z[:, :, 1:T], ALU.subtract)
            lk(eng.tensor_scalar(d[:, :, 0:1], z[:, :, 0:1], -1.0, None, ALU.mult))
            lk(eng.tensor_tensor(d, d, C("mu", tile, n, slice(0, rows)).unsqueeze(2).broadcast_to([rows, n, T]), ALU.mult))
            lk(eng.tensor_tensor(z, z, d, ALU.add))

        def per_tile(name, g):
            return C(name, 2 * g, 2).unsqueeze(2).broadcast_to([P, 2, T])

        def unit_of(q):
            return q // 4, (q // 2) % 2, q % 2

        def pe_rwkv(pe):
            meet["pe"]()
            meet["pe"]()
            for g in range(GROUPS):
                for j in range(2):
                    m = (2 * g + j) * P
                    o = j * T
                    pe.matmul(ps[:, 4, o:o + T], K("wa2")[0:64, m:m + P], rproj[0:64, RL, :], start=True, stop=True)
                    pe.matmul(ps[:, 5, o:o + T], K("wa2")[64:P, m:m + P], rproj[64:P, RL, :], start=True, stop=True)
                    pe.matmul(ps[:, 6, o:o + T], K("g2a")[:, m:m + P], rproj[:, RL + 1, :], start=True, stop=False)
                    mm = pe.matmul(ps[:, 6, o:o + T], K("g2b")[0:32, m:m + P], rproj[0:32, RL + 2, :],
                                   start=False, stop=True)
                mm.then_inc(rw_lora, 1)
                meet["pe"]()
                pe.wait_ge(rw_sq, g + 1)
                pe.matmul(ps[:, 7, :], K("blockones"), e_rn.rearrange("p j t -> p (j t)"), start=True, stop=True)\
                    .then_inc(rw_ss, 1)
                pe.wait_ge(rw_rk, g + 1)
                pe.matmul(ps[:, 3, :], K("blockones"), e_le.rearrange("p j t -> p (j t)"), start=True, stop=True)\
                    .then_inc(rw_bon, 1)
                meet["pe"]()
                for bank, src in enumerate((None, e_kh, e_bh, rproj[:, RV + 2 * g:RV + 2 * g + 2, :])):
                    for tt in range(2):
                        for j in range(2):
                            x = (g_ar[:, j, 0] if src is None else src[:, j])[:, tt * P:(tt + 1) * P]
                            mm = pe.transpose(ps[:, bank, (2 * tt + j) * P:(2 * tt + j + 1) * P], x, K("ident"))
                    mm.then_inc(rw_tr, 1)
                for q in range(8):
                    tt, j, hb = unit_of(q)
                    b = 64 * hb
                    for p in range(2):
                        c = 2 * tt + p
                        o = j * 256
                        rows = slice(64 * p, 64 * p + 64)
                        rhs = g_ar[b:b + 64, j, :, c * 64:c * 64 + 64]
                        pe.matmul(ps[rows, 4 + 2 * hb + tt, o:o + 128], g_kt[b:b + 64, j, c * 64:c * 64 + 64], rhs,
                                  start=True, stop=True, skip_group_check=True)
                        mm = pe.matmul(ps[rows, 4 + 2 * hb + tt, o + 128:o + 256], g_bt[b:b + 64, j, c * 64:c * 64 + 64], rhs,
                                       start=True, stop=True, skip_group_check=True)
                mm.then_inc(rw_gram, 1)
                pe.wait_ge(rw_taken, g + 1)
                for q in range(8):
                    tt, j, hb = unit_of(q)
                    b = 64 * hb
                    for p in range(2):
                        c = 2 * tt + p
                        o = (q // 2) * 64
                        mm = pe.matmul(ps[64 * p:64 * p + 64, 2 * hb, o:o + 64], g_ar[b:b + 64, j, 0, c * 64:c * 64 + 64],
                                       g_bt[b:b + 64, j, c * 64:c * 64 + 64], start=True, stop=True, skip_group_check=True)
                mm.then_inc(rw_aab, 1)
                meet["pe"]()
                for l in range(LEVELS - 1):
                    for half in range(2):
                        n = (g * (LEVELS - 1) + l) * 2 + half
                        if l >= 1:
                            pe.wait_ge(rw_T, n - 1)
                        for q in range(4 * half, 4 * half + 4):
                            for p in range(2):
                                rows = slice(64 * p, 64 * p + 64)
                                mm = pe.matmul(ps[rows, 4 + half, (q % 4) * 64:(q % 4) * 64 + 64], g_X[rows, l, q, :], g_T[rows, q, 0, :],
                                               start=True, stop=True, skip_group_check=True)
                        mm.then_inc(rw_P, 1)
                    for half in range(2):
                        n = (g * (LEVELS - 1) + l) * 2 + half
                        pe.wait_ge(rw_Pc, n + 1)
                        for q in range(4 * half, 4 * half + 4):
                            o = (q % 4) * 128
                            for p in range(2):
                                rows = slice(64 * p, 64 * p + 64)
                                pe.matmul(ps[rows, 6 + half, o:o + 64], g_T[rows, q, 1, :], g_P[rows, q, :],
                                          start=True, stop=True, skip_group_check=True)
                                mm = pe.matmul(ps[rows, 6 + half, o + 64:o + 128], g_P[rows, q, :], g_T[rows, q, 1, :],
                                               start=True, stop=True, skip_group_check=True)
                        mm.then_inc(rw_U, 1)
                for q in range(8):
                    for p in range(2):
                        rows = slice(64 * p, 64 * p + 64)
                        mm = pe.matmul(ps[rows, 0, q * 64:q * 64 + 64], g_gm[rows, q, 0:64], g_v[rows, q, :],
                                       start=True, stop=True, skip_group_check=True)
                mm.then_inc(rw_f, 1)
                pe.wait_ge(rw_T, (g + 1) * (LEVELS - 1) * 2)
                for q in range(8):
                    tt, j, hb = unit_of(q)
                    for p in range(2):
                        rows = slice(64 * p, 64 * p + 64)
                        o = (2 * j + tt) * 64
                        pe.matmul(ps[64 * hb:64 * hb + 64, 2 + p, o:o + 64], g_at[rows, q, :], g_T[rows, q, 1, :],
                                  start=True, stop=True, skip_group_check=True)
                pe.wait_ge(rw_fc, g + 1)
                for q in range(8):
                    for p in range(2):
                        rows = slice(64 * p, 64 * p + 64)
                        mm = pe.matmul(ps[rows, 1, q * 64:q * 64 + 64], g_T[rows, q, 1, :], g_F[rows, q, :],
                                       start=True, stop=True, skip_group_check=True)
                mm.then_inc(rw_z, 1)
                meet["pe"]()
                for c in range(4):
                    tt, p = c // 2, c % 2
                    rows = slice(64 * p, 64 * p + 64)
                    heads = [(4 * tt + x, x // 2, 64 * (x % 2)) for x in range(4)]
                    st = g_st[:, c % 2]
                    if c:
                        pe.wait_ge(rs_st, 3 * g + c)
                        for q, j, b in heads:
                            mm = pe.matmul(ps[rows, 7 if b else 3, j * 64:j * 64 + 64],
                                           g_TA[b:b + 64, j, c, :], st[b:b + 64, j, :], start=True, stop=True,
                                           skip_group_check=True)
                        mm.then_inc(rs_u, 1)
                        pe.wait_ge(rs_U, 3 * g + c)
                    if c < 3:
                        for q, j, b in heads:
                            o = (c % 2) * 128 + j * 64
                            pe.matmul(ps[b:b + 64, 4, o:o + 64], g_kh[rows, q, :], g_v[rows, q, :], start=True, stop=False,
                                      skip_group_check=True)
                            mm = pe.matmul(ps[b:b + 64, 4, o:o + 64], g_bh[rows, q, :], g_Z[rows, q, :], start=False,
                                           stop=True, skip_group_check=True)
                        mm.then_inc(rs_s, 1)
                    for q, j, b in heads:
                        o = ps[rows, 5, q * 64:q * 64 + 64]
                        pe.matmul(o, g_gm[rows, q, 64:128], g_v[rows, q, :], start=True, stop=False, skip_group_check=True)
                        pe.matmul(o, g_gm[rows, q, 192:256], g_Z[rows, q, :], start=False, stop=True, skip_group_check=True)
                        mm = pe.matmul(ps[rows, 0 if b else 6, (q // 2) * 64:(q // 2) * 64 + 64],
                                       g_ar[b:b + 64, j, 1, c * 64:c * 64 + 64], st[b:b + 64, j, :], start=True, stop=True,
                                       skip_group_check=True)
                mm.then_inc(rs_y, 1)
                pe.wait_ge(gn_n, g + 1)
                for tt in range(2):
                    for j in range(2):
                        mm = pe.transpose(ps[:, 6, j * T + tt * P:j * T + (tt + 1) * P],
                                          g_y[:, 4 * tt + 2 * j:4 * tt + 2 * j + 2, :].rearrange("p q t -> p (q t)"),
                                          K("ident"))
                mm.then_inc(gn_t, 1)
                meet["pe"]()

        def act_rwkv(act):
            meet["act"]()
            act.activation(rproj[0:64, RL, :], rproj[0:64, RL, :], ACT.Tanh)
            act.activation(rproj[:, RL + 1, :], rproj[:, RL + 1, :], ACT.Sigmoid)
            act.activation(rproj[0:32, RL + 2, :], rproj[0:32, RL + 2, :], ACT.Sigmoid)
            meet["act"]()
            for g in range(GROUPS):
                act.wait_ge(rw_lora, g + 1)
                for j in range(2):
                    act.activation(e_sg[:, j, :], ps[:, 4, j * T:(j + 1) * T], ACT.Sigmoid, bias=C("w0", 2 * g + j))
                    act.activation(e_ai[:, j, :], ps[:, 5, j * T:(j + 1) * T], ACT.Sigmoid, bias=C("a0", 2 * g + j))
                act.activation(g_gate, two(ps[:, 6, :]), ACT.Copy)
                meet["act"]()
                act.wait_ge(rw_kk, g + 1)
                act.activation(e_rn, e_kk, ACT.Square).then_inc(rw_sq, 1)
                act.wait_ge(rw_log, g + 1)
                act.activation(g_eW, e_ls, ACT.Exp, scale=-DECAY)
                act.activation(e_eWp, e_lp, ACT.Exp, scale=-DECAY)
                act.activation(e_eWi, e_ls, ACT.Exp, scale=DECAY)
                act.activation(e_eWe, e_le, ACT.Exp, scale=-DECAY).then_inc(rw_exp, 1)
                act.wait_ge(rw_mx, g + 1)
                act.activation(e_rn, e_rn, ACT.Sqrt).then_inc(rw_rt, 1)
                meet["act"]()
                act.wait_ge(rw_tr, 4 * g + 1)
                act.activation(g_at, ps[:, 0, :].rearrange("p (q d) -> p q d", d=HD), ACT.Copy)
                act.wait_ge(rw_tr, 4 * g + 3)
                act.activation(g_bh, ps[:, 2, :].rearrange("p (q d) -> p q d", d=HD), ACT.Copy).then_inc(rw_taken, 1)
                act.wait_ge(rw_tr, 4 * g + 4)
                act.activation(g_v, ps[:, 3, :].rearrange("p (q d) -> p q d", d=HD), ACT.Copy)
                meet["act"]()
                for l in range(LEVELS - 1):
                    for half in range(2):
                        n = (g * (LEVELS - 1) + l) * 2 + half
                        act.wait_ge(rw_P, n + 1)
                        act.activation(g_P[:, 4 * half:4 * half + 4, :],
                                       ps[:, 4 + half, 0:256].rearrange("p (q t) -> p q t", q=4), ACT.Copy)\
                            .then_inc(rw_Pc, 1)
                act.wait_ge(rw_f, g + 1)
                act.activation(g_F, ps[:, 0, :].rearrange("p (q t) -> p q t", q=8), ACT.Copy).then_inc(rw_fc, 1)
                act.wait_ge(rw_z, g + 1)
                for p in range(2):
                    act.activation(g_TA[:, :, p::2, :], ps[:, 2 + p, 0:256].rearrange("p (j c t) -> p j c t", j=2, c=2), ACT.Copy)
                meet["act"]()
                act.wait_ge(gn_c, g + 1)
                act.activation(g_F, g_y, ACT.Square, scale=0.125).then_inc(gn_sq, 1)
                act.wait_ge(gn_ss, g + 1)
                act.activation(g_small[:, 3, :], g_small[:, 2, :], ACT.Sqrt, bias=eps_col[:, 1:2]).then_inc(gn_rt, 1)
                meet["act"]()

        def pool_rwkv(pool):
            meet["pool"]()
            meet["pool"]()
            for g in range(GROUPS):
                shift(pool, plink, RV + 2 * g, 2, e_shp)
                meet["pool"]()
                pool.wait_ge(rw_b, g + 1)
                pool.wait_ge(rw_exp, g + 1)
                pool.tensor_tensor(e_kh, rproj[:, RK + 2 * g:RK + 2 * g + 2, :], e_eWe, ALU.mult)
                pool.tensor_tensor(e_bh, e_b, e_eWe, ALU.mult)
                meet["pool"]()
                pool.wait_ge(rw_gm, g + 1)
                for l in range(1, LEVELS):
                    pool.tensor_tensor(g_X[:, l - 1], g_gm[:, :, 128:192],
                                       K("levT")[:, l * 64:(l + 1) * 64].unsqueeze(1).broadcast_to([P, 8, 64]), ALU.mult)
                meet["pool"]()
                meet["pool"]()
                meet["pool"]()

        def dve_rwkv(dve):
            shift(dve, link, RL, 2, e_sh)
            shift(dve, link, RL + 2, 1, e_sh, 32)
            meet["dve"]()
            meet["dve"]()
            for g in range(GROUPS):
                r, k, v = (rproj[:, x + 2 * g:x + 2 * g + 2, :] for x in (RR, RK, RV))
                shift(dve, link, RR + 2 * g, 2, e_sh)
                shift(dve, link, RK + 2 * g, 2, e_sh)
                meet["dve"]()
                dve.tensor_tensor(e_kk, k, per_tile("k_k", g), ALU.mult).then_inc(rw_kk, 1)
                flat = lambda x: x.rearrange("p j t -> p (j t)")
                link(dve.tensor_tensor_scan(flat(e_ls), K("reset"), flat(e_sg), 0.0, ALU.mult, ALU.add))
                dve.tensor_tensor(e_lp, e_ls, e_sg, ALU.subtract)
                chunks = lambda x: flat(x).rearrange("p (n t) -> p n t", t=CHUNK)
                dve.tensor_tensor(chunks(e_le), chunks(e_ls)[:, :, CHUNK - 1:CHUNK].broadcast_to([P, 8, CHUNK]), chunks(e_ls),
                                  ALU.subtract).then_inc(rw_log, 1)
                link(dve.scalar_tensor_tensor(out=e_b, in0=e_ai, scalar=-1.0, in1=per_tile("k_a", g), op0=ALU.add, op1=ALU.mult))
                link(dve.scalar_tensor_tensor(out=k, in0=e_b, scalar=1.0, in1=k, op0=ALU.add, op1=ALU.mult))
                dve.wait_ge(rw_ss, g + 1)
                dve.tensor_scalar(flat(e_rn), ps[:, 7, :], 1e-24, None, ALU.max).then_inc(rw_mx, 1)
                dve.wait_ge(rw_rt, g + 1)
                link(dve.reciprocal(e_rn, e_rn))
                link(dve.tensor_tensor(e_kk, e_kk, e_rn, ALU.mult))
                dve.tensor_tensor(e_b, e_kk, e_ai, ALU.mult).then_inc(rw_b, 1)
                dve.wait_ge(rw_b, g + 1)
                dve.wait_ge(rw_exp, g + 1)
                link(dve.tensor_tensor(e_lp, r, k, ALU.mult))
                dve.tensor_tensor(e_le, e_lp, per_tile("r_k", g), ALU.mult).then_inc(rw_rk, 1)
                dve.scalar_tensor_tensor(out=g_ar[:, :, 0, :], in0=e_kk, scalar=-1.0, in1=e_eWp, op0=ALU.mult, op1=ALU.mult)
                dve.tensor_tensor(g_ar[:, :, 1, :], r, g_eW, ALU.mult)
                dve.tensor_tensor(g_kt, k, e_eWi, ALU.mult)
                dve.tensor_tensor(g_bt, e_b, e_eWi, ALU.mult)
                dve.wait_ge(rw_bon, g + 1)
                link(dve.tensor_tensor(g_bonus, two(ps[:, 3, :]), v, ALU.mult))
                meet["dve"]()
                dve.wait_ge(rw_tr, 4 * g + 2)
                dve.tensor_copy(g_kh, ps[:, 1, :].rearrange("p (q d) -> p q d", d=HD))
                dve.wait_ge(rw_gram, g + 1)
                for x in range(4):
                    q0 = 4 * (x % 2) + x // 2
                    ins = dve.tensor_tensor(g_gm[:, q0:q0 + 3:2, :], ps[:, 4 + x, :].rearrange("p (q n) -> p q n", q=2),
                                            K("gram").unsqueeze(1).broadcast_to([P, 2, 256]), ALU.mult)
                ins.then_inc(rw_gm, 1)
                dve.wait_ge(rw_gm, g + 1)
                all8 = lambda m: m.unsqueeze(1).broadcast_to([P, 8, 64])
                link(dve.tensor_tensor(g_T[:, :, 1, :], g_gm[:, :, 128:192], all8(K("levT")[:, 0:64]), ALU.mult))
                link(dve.tensor_tensor(g_T[:, :, 1, :], g_T[:, :, 1, :], all8(K("eye64")), ALU.add))
                dve.wait_ge(rw_aab, g + 1)
                for hb in range(2):
                    ins = dve.tensor_tensor(g_T[:, hb::2, 0, :], ps[:, 2 * hb, 0:256].rearrange("p (q t) -> p q t", q=4),
                                            K("lev0").unsqueeze(1).broadcast_to([P, 4, 64]), ALU.mult)
                link(ins)
                dve.memset(g_st[:, 0], 0.0)
                link(dve.tensor_tensor(g_T[:, :, 0, :], g_T[:, :, 0, :], all8(K("eye64")), ALU.add))
                meet["dve"]()
                for l in range(LEVELS - 1):
                    for half in range(2):
                        n = (g * (LEVELS - 1) + l) * 2 + half
                        dve.wait_ge(rw_U, n + 1)
                        t = g_T[:, 4 * half:4 * half + 4].rearrange("p q x t -> p (q x t)")
                        dve.tensor_tensor(t, t, ps[:, 6 + half, :], ALU.add).then_inc(rw_T, 1)
                dve.wait_ge(rw_z, g + 1)
                dve.tensor_copy(g_Z, ps[:, 1, :].rearrange("p (q t) -> p q t", q=8))
                meet["dve"]()
                for c in range(4):
                    tt, p = c // 2, c % 2
                    rows = slice(64 * p, 64 * p + 64)
                    if c:
                        dve.wait_ge(rs_u, 3 * g + c)
                        for hb in range(2):
                            u = g_Z[rows, 4 * tt + hb:4 * tt + 4:2, :]
                            ins = dve.tensor_tensor(u, u, ps[rows, 3 + 4 * hb, 0:128].rearrange("p (q t) -> p q t", q=2), ALU.add)
                        ins.then_inc(rs_U, 1)
                    if c < 3:
                        dve.wait_ge(rs_s, 3 * g + c + 1)
                        new = g_st[:, (c + 1) % 2]
                        o = ps[:, 4, (c % 2) * 128:(c % 2) * 128 + 128].rearrange("p (j v) -> p j v", j=2)
                        if c == 0:
                            dve.tensor_copy(new, o).then_inc(rs_st, 1)
                        else:
                            wc = g_eW[:, :, c * CHUNK + CHUNK - 1:c * CHUNK + CHUNK].broadcast_to([P, 2, HD])
                            link(dve.tensor_tensor(g_st2, g_st[:, c % 2], wc, ALU.mult))
                            dve.tensor_tensor(new, g_st2, o, ALU.add).then_inc(rs_st, 1)
                        dve.wait_ge(rs_st, 3 * g + c + 1)
                dve.wait_ge(rs_y, g + 1)
                link(dve.tensor_copy(g_y, ps[:, 5, :].rearrange("p (q t) -> p q t", q=8)))
                for hb in range(2):
                    y = g_y[:, hb::2, :]
                    ins = dve.tensor_tensor(y, y, ps[:, 0 if hb else 6, 0:256].rearrange("p (q t) -> p q t", q=4), ALU.add)
                link(ins)
                link(dve.tensor_reduce(g_small[:, 0, :], g_y, AX, ALU.add))
                link(dve.tensor_scalar(g_small[:, 1, :], g_small[:, 0, :], -1.0 / HD, None, ALU.mult))
                dve.tensor_tensor(g_y, g_y, g_small[:, 1, :].unsqueeze(2).broadcast_to([P, 8, HD]), ALU.add).then_inc(gn_c, 1)
                dve.wait_ge(gn_sq, g + 1)
                dve.wait_ge(gn_c, g + 1)
                dve.tensor_reduce(g_small[:, 2, :], g_F, AX, ALU.add).then_inc(gn_ss, 1)
                dve.wait_ge(gn_rt, g + 1)
                link(dve.reciprocal(g_small[:, 3, :], g_small[:, 3, :]))
                dve.tensor_tensor(g_y, g_y, g_small[:, 3, :].unsqueeze(2).broadcast_to([P, 8, HD]), ALU.mult).then_inc(gn_n, 1)
                dve.wait_ge(gn_t, g + 1)
                for j in range(2):
                    m = 2 * g + j
                    ins = dve.tensor_scalar(yT[:, m, :], ps[:, 6, j * T:(j + 1) * T], C("ln_w", m), C("ln_b", m),
                                            ALU.mult, ALU.add)
                link(ins)
                y = yT[:, 2 * g:2 * g + 2, :]
                link(dve.tensor_tensor(y, y, g_bonus, ALU.add))
                link(dve.tensor_tensor(y, y, g_gate, ALU.mult))
                meet["dve"]()

        g_st2 = g_P.rearrange("p q t -> p (q t)")[:, 0:128].rearrange("p (j v) -> p j v", j=2)

        sg_done = sem("sg_done")

        def act_gates(act):
            def body(j, u, i):
                act.wait_ge(unit_done, u + 1)
                act.wait_ge(dve_out, u - 1)
                for x in range(2):
                    ins = act.activation(stage_buf[:, j % 2, x * T:(x + 1) * T], ps[:, 2 * (j % 2) + x, 0:T], ACT.Sigmoid,
                                         bias=C("gate_bias", i + 8 * x))
                ins.then_inc(act_out, 1)
            straight_units("gates", body)

        def dve_gates(dve):
            def body(j, u, i):
                dve.wait_ge(act_out, u + 1)
                g = stage_buf[:, j % 2]
                dve.tensor_tensor(g[:, 0:T], g[:, 0:T], ya[:, i, :], ALU.mult)
                link(dve.tensor_tensor(g[:, T:2 * T], g[:, T:2 * T], yr[:, i, :], ALU.mult))
                dve.tensor_tensor(merged[:, i, :], g[:, 0:T], g[:, T:2 * T], ALU.add).then_inc(dve_out, 1)
            straight_units("gates", body)

        def gate_of(part):
            def gates(m, c0):
                return [(lo, hi, mod[:, bass.ds(m + part * KT, 1), s:s + 1].rearrange("p a b -> p (a b)"))
                        for s in range(2) for lo, hi in [(s * T - c0, s * T - c0 + T)] if lo >= 0]
            return lambda c0: (lambda m: gates(m, c0))

        half = lambda m: [(0, T, 0.5)]
        whole = lambda m: [(0, T, 1.0)]

        def scale_of(i, c0):
            return lambda m: segments(c0, None, lambda s: scl[:, i, m, s:s + 1])

        def shift_of(part, c0):
            return lambda m: segments(c0, None, lambda s: mod[:, part * KT + m, s:s + 1])

        def plain(name):
            return lambda m: [(0, T, C(name, m))]

        none = lambda m: [(0, T, None)]

        block = ctx.enter_context(nc.Block())

        @block.tensor
        def _(pe):
            meet["pe"] = Meet(pe, "pe")
            pe.wait_ge(params_in, 48)
            for layer in range(DEPTH):
                c0, n = unit_tokens(layer, False)
                meet["pe"]()
                pe_ada(pe, layer, cond)
                meet["pe"]()
                pe_norm(pe, 2 * layer, 0, TA)
                meet["pe"]()
                pe_project(pe, layer)
                meet["pe"]()
                pe_mlstm(pe, layer)
                meet["pe"]()
                pe_pool(pe, layer)
                meet["pe"]()
                pe_qk(pe, layer)
                meet["pe"]()
                pe_attention(pe, layer)
                meet["pe"]()
                pe_feature_tiles(pe, f"out{layer}", 2, mixT, c0, n)
                meet["pe"]()
                pe_norm(pe, 2 * layer + 1, c0, n)
                meet["pe"]()
                pe_ffn(pe, layer, c0, n)
                meet["pe"]()
            pe_norm(pe, 4, T, T)
            meet["pe"]()
            pe_norm(pe, 5, T, T)
            meet["pe"]()
            pe_ffn(pe, 2, T, T)
            meet["pe"]()
            pe_norm(pe, 6, T, T)
            meet["pe"]()
            pe_feature_tiles(pe, "qk", 3, hT, T, T)
            pe_values(pe)
            meet["pe"]()
            pe.wait_ge(second_in, 16)
            pe_rope(pe)
            meet["pe"]()
            pe_dilated(pe)
            meet["pe"]()
            pe_feature_tiles(pe, "rkv", 3, hT, T, T)
            pe_lora(pe)
            meet["pe"]()
            pe_rwkv(pe)
            pe_feature_tiles(pe, "attn_up", 4, attnT, 0, T, kt=2)
            pe_feature_tiles(pe, "rwkv_out", 2, yT, 0, T, per_bank=1)
            meet["pe"]()
            pe_feature_tiles(pe, "gates", 2, hT, T, T, per_bank=1, straight=True)
            meet["pe"]()
            pe_feature_tiles(pe, "w_o", 2, merged, 0, T)
            meet["pe"]()
            pe_norm(pe, 7, T, T)
            meet["pe"]()
            pe_ffn(pe, 3, T, T)
            meet["pe"]()
            pe_norm(pe, 8, T, T)
            meet["pe"]()

        @block.scalar
        def _(act):
            meet["act"] = Meet(act, "act")
            links["act"] = Chain(act, chains["act"])
            act.wait_ge(params_in, 48)
            for layer in range(DEPTH):
                c0, n = unit_tokens(layer, False)
                act.activation(cond[:, :, 0:2], C("cond", 0, 16).rearrange("p (k s) -> p k s", s=2), ACT.Silu)
                meet["act"]()
                copy_rows(act, act_copy(act), act_out, f"ada{layer}", 0)
                meet["act"]()
                act_norm(act, 2 * layer, 0, TA)
                meet["act"]()
                evacuate_project(act, act_copy(act), act_out, layer, 0)
                meet["act"]()
                act_mlstm(act, layer)
                meet["act"]()
                meet["act"]()
                act_qk(act, layer)
                meet["act"]()
                act_attention(act, layer)
                meet["act"]()
                act_residual(act, f"out{layer}", n, gate_of(2)(c0), 2)
                meet["act"]()
                act_norm(act, 2 * layer + 1, c0, n)
                meet["act"]()
                act_ffn(act, layer, c0, n, gate_of(5)(c0))
                meet["act"]()
            act.dma_start(const[:, COMMON_N:COMMON_N + TWO_N], dram["const2"]).then_inc(second_in, 16)
            act_norm(act, 4, T, T)
            meet["act"]()
            act_norm(act, 5, T, T)
            meet["act"]()
            act_ffn(act, 2, T, T, half)
            meet["act"]()
            act_norm(act, 6, T, T)
            meet["act"]()
            copy_out(act, act_copy(act), act_out, "qk", three_tiles(qkT, 0))
            copy_out(act, act_copy(act), act_out, "v", value_halves(0))
            meet["act"]()
            meet["act"]()
            act_dilated(act)
            meet["act"]()
            copy_out(act, act_copy(act), act_out, "rkv", three_tiles(rproj, 0))
            copy_out(act, act_copy(act), act_out, "lora", lora_tiles(0))
            meet["act"]()
            act_rwkv(act)
            copy_out(act, act_copy(act), act_out, "attn_up", bank_each(ya, 0, 2))
            copy_out(act, act_copy(act), act_out, "rwkv_out", bank_each(yr, 0, 1))
            meet["act"]()
            act_gates(act)
            meet["act"]()
            act_residual(act, "w_o", T, whole, 2)
            meet["act"]()
            act_norm(act, 7, T, T)
            meet["act"]()
            act_ffn(act, 3, T, T, half)
            meet["act"]()
            act_norm(act, 8, T, T)
            meet["act"]()

        @block.vector
        def _(dve):
            meet["dve"] = Meet(dve, "dve")
            links["dve"] = Chain(dve, chains["dve"])
            dve.memset(eps_col[:, 0:1], EPS)
            dve.memset(eps_col[:, 1:2], GN_EPS)
            copy = lambda o, s: dve.tensor_copy(o, s)
            for layer in range(DEPTH):
                c0, n = unit_tokens(layer, False)
                dve.memset(cond[:, :, 2:32], 0.0)
                dve.wait_ge(params_in, 48)
                meet["dve"]()
                copy_rows(dve, copy, dve_out, f"ada{layer}", 1)
                meet["dve"]()
                dve_mod(dve, layer)
                dve_norm(dve, 2 * layer, 0, TA, hT, scale_of(0, 0), shift_of(0, 0))
                meet["dve"]()
                evacuate_project(dve, copy, dve_out, layer, 1)
                meet["dve"]()
                dve_mlstm(dve, layer)
                meet["dve"]()
                dve_pool(dve, layer)
                meet["dve"]()
                dve_qk(dve, layer)
                meet["dve"]()
                dve_attention(dve, layer)
                meet["dve"]()
                dve_residual(dve, f"out{layer}", c0, n, 2)
                meet["dve"]()
                dve_norm(dve, 2 * layer + 1, c0, n, hT, scale_of(1, c0), shift_of(3, c0))
                meet["dve"]()
                dve_ffn(dve, layer, c0, n)
                meet["dve"]()
            dve_norm(dve, 4, T, T, xT, plain("final_norm"), none)
            meet["dve"]()
            dve_norm(dve, 5, T, T, hT, plain("ffn1_norm"), none)
            meet["dve"]()
            dve_ffn(dve, 2, T, T)
            meet["dve"]()
            dve_norm(dve, 6, T, T, hT, plain("mix_norm"), none)
            meet["dve"]()
            copy_out(dve, copy, dve_out, "qk", three_tiles(qkT, 1))
            copy_out(dve, copy, dve_out, "v", value_halves(1))
            meet["dve"]()
            dve.wait_ge(second_in, 16)
            dve_rope(dve)
            meet["dve"]()
            dve_dilated(dve)
            meet["dve"]()
            copy_out(dve, copy, dve_out, "rkv", three_tiles(rproj, 1))
            copy_out(dve, copy, dve_out, "lora", lora_tiles(1))
            meet["dve"]()
            dve_rwkv(dve)
            copy_out(dve, copy, dve_out, "attn_up", bank_each(ya, 1, 2))
            copy_out(dve, copy, dve_out, "rwkv_out", bank_each(yr, 1, 1))
            meet["dve"]()
            dve_gates(dve)
            meet["dve"]()
            dve_residual(dve, "w_o", T, T, 2)
            meet["dve"]()
            dve_norm(dve, 7, T, T, hT, plain("ffn2_norm"), none)
            meet["dve"]()
            dve_ffn(dve, 3, T, T)
            meet["dve"]()
            dve_norm(dve, 8, T, T, hT, plain("final_norm_2"), none)
            meet["dve"]()

        @block.gpsimd
        def _(pool):
            meet["pool"] = Meet(pool, "pool")
            links["pool"] = Chain(pool, chains["pool"])
            pool.wait_ge(params_in, 48)
            for layer in range(DEPTH):
                for _ in range(4):
                    meet["pool"]()
                pool_mlstm(pool, layer)
                meet["pool"]()
                meet["pool"]()
                pool_qk(pool, layer)
                for _ in range(6):
                    meet["pool"]()
            for _ in range(5):
                meet["pool"]()
            meet["pool"]()
            pool.wait_ge(second_in, 16)
            pool_rope(pool)
            meet["pool"]()
            meet["pool"]()
            meet["pool"]()
            pool_rwkv(pool)
            for _ in range(7):
                meet["pool"]()

        @block.sync
        def _(sp):
            sp.dma_start(par[:, :], dram["par"]).then_inc(params_in, 16)
            sp.dma_start(const[:, 0:COMMON_N + ONE_N], dram["const"]).then_inc(params_in, 16)
            sp.dma_start(xT[:, :, :].rearrange("p k t -> p (k t)"), dram["x"]).then_inc(params_in, 16)
            load_weights(sp)
            sp.wait_ge(met["dve"], meet["dve"].n)
            sp.dma_start(out, hT[:, :, T:TA]).then_inc(stored, 16)
            sp.wait_ge(stored, 16)
        assert len({m.n for m in meet.values()}) == 1, {k: m.n for k, m in meet.items()}


def feature_columns(v):
    return np.asarray(v).reshape(-1, P).T


def tiles(w, cols):
    k, m = w.shape
    return w.reshape(k // P, P, m // cols, cols).transpose(2, 1, 0, 3).reshape(m // cols, P, -1)


def joined(t, n):
    u = t.shape[0] // n
    return t.reshape(u, n, P, -1).transpose(0, 2, 1, 3).reshape(u, P, -1)


def layout(i):
    i = {k: np.asarray(v) for k, v in i.items()}
    w = {}
    heads = [h for j in range(4) for h in (j, 4 + j)]
    for l in range(DEPTH):
        w[f"ada{l}"] = tiles(i["w_ada"][l], ADA_COLS)
        offs = np.cumsum([0, 512, 128, 128, 256, 256, 256, 256, 16, 256])
        aq, ak, av, mq, mk, mv, mo, mg, pp = (i["w_in"][l][:, a:b] for a, b in zip(offs[:-1], offs[1:]))
        aq = aq.reshape(D, 8, HD)[:, heads].reshape(D, 512)
        fm = tiles(np.concatenate([aq, mq, mo, mk, ak, np.zeros_like(ak)], 1), P)
        w[f"fm{l}"] = joined(fm, 2)
        w[f"tma{l}"] = tiles(np.concatenate([mv, mg], 1), 272)
        w[f"tmb{l}"] = tiles(np.concatenate([av, pp], 1), 384)
        wo = i["w_out"][l]
        wo = np.concatenate([wo[:512].reshape(8, HD, D)[heads].reshape(512, D), wo[512:]], 0)
        w[f"out{l}"] = joined(tiles(wo, P), 2)
        for r, g, u, d in ((l, i["w_ffn_gate"][l], i["w_ffn_up"][l], i["w_ffn_down"][l]),
                           (2 + l, *(i[f"ffn{1 + l}_w_{x}_2"][0] for x in ("gate", "up", "down")))):
            w[f"up{r}"] = np.concatenate([tiles(g, P), tiles(u, P)], 2)
            w[f"down{r}"] = tiles(d, P)
    w2 = i["w_in_2"][0]
    w["qk"] = joined(tiles(w2[:, :1536], P), 3)
    w["v"] = tiles(w2[:, 1536:2304], 384)
    w["rkv"] = joined(tiles(w2[:, 2304:2304 + 3072], P), 3)
    w["lora"] = tiles(w2[:, 5376:5664], 288)
    w["attn_up"] = joined(tiles(i["attn_w_up_2"][0], P), 4)
    w["rwkv_out"] = joined(tiles(i["rwkv_w_out_2"][0], P), 2)
    gt = tiles(w2[:, 5664:], P)
    w["gates"] = np.concatenate([gt[:8], gt[8:]], 2)
    w["w_o"] = joined(tiles(i["w_o_2"][0], P), 2)

    par = np.zeros((P, PAR_N), np.float32)

    def put(name, v, rows=slice(0, P)):
        at, n = PAR_AT[name]
        par[rows, at:at + n] = v
    for l in range(DEPTH):
        for name in ("norm_mix", "norm_ffn", "b_ada", "ml_norm", "pool_scale"):
            put(f"{name}{l}", feature_columns(i[name][l]))
        for name in ("q_norm", "k_norm"):
            put(f"{name}{l}", np.tile(i[name][l], 2)[:, None])
        put(f"b_gates{l}", i["b_gates"][l].reshape(4, 4).T, slice(0, 4))
        put(f"pool_w{l}", i["pool_w"][l].reshape(2, 2, HD, HD).transpose(1, 2, 0, 3).reshape(P, -1))
    put("final_norm", feature_columns(i["final_norm"]))
    put("final_norm_2", feature_columns(i["final_norm_2"]))
    for name in ("ffn1_norm", "mix_norm", "ffn2_norm", "gate_bias"):
        put(name, feature_columns(i[name + "_2"][0]))
    mu = np.concatenate([i["rwkv_mu_2"][0], np.zeros(R_TILES * P - 3360, np.float32)])
    put("mu", feature_columns(mu))
    for name in ("w0", "a0", "k_k", "k_a", "r_k", "ln_w", "ln_b"):
        put(name, feature_columns(i[f"rwkv_{name}_2"][0].reshape(-1)))
    put("cond", np.stack([feature_columns(i["c_ctx"]), feature_columns(i["c"][0])], 2).reshape(P, -1))
    x = np.concatenate([i["ctx"][0], i["x"][0]], 0)
    x = x.reshape(TA, KT, P).transpose(2, 1, 0).reshape(P, -1)
    wa2 = np.concatenate([i["rwkv_w2_2"][0], i["rwkv_a2_2"][0]], 0)
    g2 = i["rwkv_g2_2"][0]
    g2b = np.concatenate([g2[P:], np.zeros((2 * P - len(g2), D), np.float32)], 0)
    const = np.concatenate([CONSTS[k] for k in COMMON + BLOCK1], 1)
    const2 = np.concatenate([CONSTS[k] for k in BLOCK2] + [wa2, g2[:P], g2b], 1)
    return {"par": par, "const": const, "const2": const2, "x": x, **{f"w_{k}": v for k, v in w.items()}}


def kernel(**inputs):
    import concourse.bacc as bacc
    from concourse.bass_utils import run_bass_kernel_spmd

    nc = bacc.Bacc("TRN2", target_bir_lowering=False, num_devices=1)
    arrays, dram = {}, {}
    for name, a in layout(inputs).items():
        arrays[f"{name}_dram"] = a = np.ascontiguousarray(a, dtype=np.float32)
        dram[name] = nc.dram_tensor(f"{name}_dram", a.shape, F32, kind="ExternalInput").ap()
    out = nc.dram_tensor("out_dram", (P, KT, T), F32, kind="ExternalOutput").ap()
    build(nc, dram, out)
    r = run_bass_kernel_spmd(nc, [arrays], core_ids=[0])
    y = r.results[0]["out_dram"]
    return np.ascontiguousarray(y.transpose(2, 1, 0).reshape(1, T, D))
```

```python
from contextlib import ExitStack

import numpy as np
import concourse.bass as bass
from concourse import mybir

F32 = mybir.dt.float32
ALU = mybir.AluOpType
ACT = mybir.ActivationFunctionType
AX = mybir.AxisListType.X

P = 128
D = 1024
KT = D // P
T = 256
TA = 2 * T
HD = 64
DEPTH = 2
FF = 2816
FT = FF // P
ADA_UNITS, ADA_COLS = 16, 384
ADA_FIRST = -(-2 * D // ADA_COLS)
ADA_TILES = ADA_FIRST * ADA_COLS // P
SLOTS, SLOT = 4, 3072
EPS = 1e-6
GN_EPS = 64e-5
POOL_WINDOWS = (2, 4, 8, 16)
GRID_W = 64
CHUNK = 64
DECAY = float(np.exp(-0.5))
LEVELS = 6

AQ, MQ, MO, MK, AK, FM_TILES = 0, 4, 6, 8, 10, 11
MV, MG, AV, PP, TM = 0, 256, 272, 400, 656
RR, RK, RV, RL, R_TILES = 0, 8, 16, 24, 27


def constant_table():
    c = {}
    i = np.arange(P)
    c["ident"] = np.eye(P)
    c["ones"] = np.ones((P, P))
    c["blockones"] = (i[:, None] // HD == i[None] // HD) * 1.0
    rot = np.zeros((P, P))
    for o in range(P):
        if o % 32 < 16:
            rot[o + 16, o] = -1
        else:
            rot[o - 16, o] = 1
    c["rot1"] = rot
    rot = np.zeros((P, P))
    for o in range(P):
        d = o % HD
        if d < 8:
            rot[o + 8, o] = -1
        elif d < 16:
            rot[o - 8, o] = 1
    c["rot2"] = rot
    half = HD // 2
    f32 = np.float32
    inv = (1.0 / (f32(10000.0) ** (np.arange(0, half, 2, dtype=f32) / f32(half)))).astype(f32)
    row = np.repeat(np.arange(T // GRID_W, dtype=f32), GRID_W)
    col = np.tile(np.arange(GRID_W, dtype=f32), T // GRID_W)
    ar, ac = row[:, None] * inv, col[:, None] * inv
    ang = np.concatenate([ar, ar, ac, ac], 1).astype(f32)
    cos1, sin1 = np.ones((P, TA)), np.zeros((P, TA))
    cos1[:, T:] = np.tile(np.cos(ang).T, (2, 1))
    sin1[:, T:] = np.tile(np.sin(ang).T, (2, 1))
    c["cos1"], c["sin1"] = cos1, sin1
    inv2 = np.power(f32(500000.0), -np.arange(8, dtype=f32) * f32(2.0 / 16)).astype(f32)
    a2 = (np.arange(T, dtype=f32)[:, None] * inv2[None]).astype(f32)
    cos2, sin2 = np.ones((HD, T)), np.zeros((HD, T))
    cos2[0:16] = np.tile(np.cos(a2).T, (2, 1))
    sin2[0:16] = np.tile(np.sin(a2).T, (2, 1))
    c["cos2"], c["sin2"] = np.tile(cos2, (2, 1)), np.tile(sin2, (2, 1))
    c["tri0"] = (i[:, None] <= i[None]) * 1.0
    c["tri1"] = (i[:, None] >= i[None]) * 1.0
    for qt in range(2):
        nk = (qt + 1) * P
        t = qt * P + i[:, None]
        s = np.arange(nk)[None]
        see = [(s <= t) & (t - s <= P), (s <= t) & ((t - s) % 4 == 0), (s <= t) & ((t - s) % 16 == 0)]
        c[f"see{qt}"] = np.concatenate([np.where(m, 0.0, -1e30) for m in see], 1)
    t = np.arange(T)
    band = np.zeros((T, 4, T))
    for g, w in enumerate(POOL_WINDOWS):
        lo, hi = np.maximum(t - w // 2, 0), np.minimum(t + w // 2, T)
        s = t[:, None]
        band[:, g] = ((s >= lo) & (s < hi)) / (hi - lo).astype(f32)[None] - (s == t[None])
    c["band"] = band.reshape(2, P, 4, T).transpose(1, 0, 2, 3).reshape(P, -1)
    sel = np.zeros((P, 4, P))
    for h in range(4):
        sel[h, h] = 1
    c["sel"] = sel.reshape(P, -1)
    fold = np.zeros((P, 2))
    for j in range(4):
        fold[32 * j, 0] = fold[32 * j + 1, 1] = 1
    c["fold"] = fold
    s, t = i[:, None] % CHUNK, np.arange(CHUNK)[None]
    c["gram"] = np.concatenate([s < t, s <= t, s < t, s <= t], 1) * 1.0
    c["eye64"] = (s == t) * 1.0
    lev, levT = [], []
    for l in range(LEVELS):
        b = 1 << l
        low = (s // (2 * b) == t // (2 * b)) & (s % (2 * b) >= b) & (t % (2 * b) < b)
        lev.append(low)
        levT.append((s // (2 * b) == t // (2 * b)) & (t % (2 * b) >= b) & (s % (2 * b) < b))
    c["lev0"] = lev[0] * 1.0
    c["levT"] = np.concatenate(levT, 1) * 1.0
    reset = np.ones((P, TA))
    reset[:, ::CHUNK] = 0
    c["reset"] = reset
    return {k: np.ascontiguousarray(v, dtype=f32) for k, v in c.items()}


def column_map(groups):
    at, out = 0, {}
    for name, n in groups:
        out[name] = (at, n)
        at += n
    return out, at


CONSTS = constant_table()
COMMON = ("ident", "ones", "blockones")
BLOCK1 = ("rot1", "cos1", "sin1", "tri0", "tri1", "band", "sel", "fold")
BLOCK2 = tuple(k for k in CONSTS if k not in COMMON + BLOCK1)
CONST_AT, COMMON_N = column_map([(k, CONSTS[k].shape[1]) for k in COMMON])
_one, ONE_N = column_map([(k, CONSTS[k].shape[1]) for k in BLOCK1])
_two, TWO_N = column_map([(k, CONSTS[k].shape[1]) for k in BLOCK2] + [("wa2", D), ("g2a", D), ("g2b", D)])
CONST_AT.update({k: (COMMON_N + at, n) for m in (_one, _two) for k, (at, n) in m.items()})
CONST_N = COMMON_N + max(ONE_N, TWO_N)

PAR1 = [("norm_mix", 8), ("norm_ffn", 8), ("b_ada", 48), ("q_norm", 1), ("k_norm", 1), ("ml_norm", 2),
        ("pool_scale", 2), ("b_gates", 4), ("pool_w", 2 * HD)]
PAR2 = [("final_norm", 8), ("ffn1_norm", 8), ("mix_norm", 8), ("ffn2_norm", 8), ("final_norm_2", 8),
        ("gate_bias", 16), ("mu", R_TILES), ("w0", 8), ("a0", 8), ("k_k", 8), ("k_a", 8), ("r_k", 8),
        ("ln_w", 8), ("ln_b", 8), ("cond", 16)]
PAR_AT, PAR_N = column_map([(f"{n}{l}", k) for l in range(DEPTH) for n, k in PAR1] + PAR2)

PHASES = []
PHASES += [("ada0a", ADA_FIRST, KT * ADA_COLS)]
for _l in range(DEPTH):
    PHASES += [(f"tma{_l}", 1, KT * 272), (f"fm{_l}", 6, 2 * D), (f"tmb{_l}", 1, KT * 384)]
    PHASES += [(f"ada{_l}b", ADA_UNITS - ADA_FIRST, KT * ADA_COLS)]
    if _l + 1 < DEPTH:
        PHASES += [(f"ada{_l + 1}a", ADA_FIRST, KT * ADA_COLS)]
    PHASES += [(f"out{_l}", 4, 2 * D), (f"up{_l}", FT, 2 * D), (f"down{_l}", 8, FT * P)]
PHASES += [("up2", FT, 2 * D), ("down2", 8, FT * P), ("qk", 4, 3 * D), ("v", 2, KT * 384), ("rkv", 8, 3 * D),
           ("lora", 1, KT * 288), ("gates", 8, 2 * D), ("attn_up", 2, D), ("rwkv_out", 4, 2 * D), ("w_o", 4, 2 * D),
           ("up3", FT, 2 * D), ("down3", 8, FT * P)]
FIRST = {}
_u = 0
for _n, _k, _ in PHASES:
    FIRST[_n] = _u
    _u += _k
UNITS = _u


class Chain:

    def __init__(self, eng, sem):
        self.eng, self.sem, self.n, self.reg = eng, sem, 0, None

    def __call__(self, ins):
        ins.then_inc(self.sem, 1)
        self.n += 1
        self.eng.wait_ge(self.sem, self.n if self.reg is None else self.reg + self.n)


def over_units(eng, phase, body, chain=None):
    first, n = FIRST[phase], dict((a, b) for a, b, _ in PHASES)[phase]
    i = 0
    if first == 0:
        while i < SLOTS:
            body(i % SLOTS, i, i)
            i += 1
    trips = (n - i) // SLOTS
    if trips > 1:
        per = 0
        n0 = chain.n if chain else 0
        with eng.Fori(0, trips) as r:
            if chain:
                chain.reg = r * chain.per
            for j in range(SLOTS):
                body((first + i + j) % SLOTS, r * SLOTS + (first + i + j), r * SLOTS + (i + j))
        if chain:
            assert chain.n - n0 == chain.per, (chain.n, n0, chain.per)
            chain.n = n0 + chain.per * trips
            chain.reg = None
        i += trips * SLOTS
    while i < n:
        body((first + i) % SLOTS, first + i, i)
        i += 1


def build(nc, dram, out):
    ctx = ExitStack()
    with ctx:
        def sb(name, *shape):
            return ctx.enter_context(nc.sbuf_tensor(name, [P, *shape], F32))

        def sem(name):
            return ctx.enter_context(nc.semaphore(name))

        xT = sb("xT", KT, TA)
        hT = sb("hT", KT, TA)
        ring = sb("ring", SLOTS, SLOT)
        const = sb("const", CONST_N)
        par = sb("par", PAR_N)
        mod = [sb(f"mod{x}", 48, 2) for x in range(DEPTH)]
        scl = [sb(f"scl{x}", 2, KT, 2) for x in range(DEPTH)]
        eps_col = sb("eps_col", 2)
        WORK = 25200
        work = sb("work", WORK)
        ps = ctx.enter_context(nc.psum_tensor("ps", [P, 8, 512], F32))

        def K(name):
            at, n = CONST_AT[name]
            return const[:, at:at + n]

        def C(name, j=0, n=1, rows=slice(0, P)):
            at, _ = PAR_AT[name]
            return par[rows, at + j:at + j + n]

        class Area:

            def __init__(self, at=0):
                self.at = at

            def __call__(self, n):
                self.at += n
                assert self.at <= WORK, self.at
                return work[:, self.at - n:self.at]

        a = Area()
        proj = a(FM_TILES * TA).rearrange("p (m t) -> p m t", t=TA)
        tm = a(4 * TM).rearrange("p (k c) -> p k c", c=TM)
        mixT = a(KT * TA).rearrange("p (m t) -> p m t", t=TA)
        mixer_free = a.at
        hidden = work[:, 0:FT * TA].rearrange("p (m t) -> p m t", t=TA)
        stage_buf = work[:, WORK - 2048:WORK].rearrange("p (b n) -> p b n", b=2)

        params_in = sem("params_in")
        second_in = sem("second_in")
        loaded = [sem(f"loaded{j}") for j in range(SLOTS)]
        unit_done = sem("unit_done")
        act_out = sem("act_out")
        dve_out = sem("dve_out")
        chains = {e: sem(f"{e}_chain") for e in ("act", "dve", "pool")}
        met = {e: sem(f"{e}_met") for e in ("pe", "act", "dve", "pool")}
        stored = sem("stored")

        class Meet:

            def __init__(self, eng, me):
                self.eng, self.me, self.n = eng, me, 0

            def __call__(self):
                self.n += 1
                self.eng.drain().then_inc(met[self.me], 1)
                for other in met:
                    if other != self.me:
                        self.eng.wait_ge(met[other], self.n)

        def load_weights(sp):
            for phase, n, size in PHASES:
                src = dram[f"w_{phase}"]

                def body(j, u, i):
                    if not (isinstance(u, int) and u < SLOTS):
                        sp.wait_ge(unit_done, u - (SLOTS - 1))
                    sp.dma_start(ring[:, j, 0:size], src[bass.ds(i, 1), :, :].rearrange("a p n -> p (a n)"))\
                        .then_inc(loaded[j], 16)
                over_units(sp, phase, body)

        def pe_unit_ready(pe, j, u):
            pe.wait_ge(loaded[j], (u - j) * (16 // SLOTS) + 16)
            if not (isinstance(u, int) and u < 2):
                pe.wait_ge(act_out, u - 1)
                pe.wait_ge(dve_out, u - 1)

        def pe_feature_tiles(pe, phase, tiles, rhs, c0, n, kt=KT, per_bank=None, straight=False):
            per_bank = per_bank or 512 // n

            def body(j, u, i):
                pe_unit_ready(pe, j, u)
                for m in range(tiles):
                    bank = 2 * (j % 2) + m // per_bank
                    o = (m % per_bank) * n
                    for k in range(kt):
                        w = ring[:, j, (m * kt + k) * P:(m * kt + k + 1) * P]
                        mm = pe.matmul(ps[:, bank, o:o + n], w, rhs[:, k, c0:c0 + n], start=(k == 0), stop=(k == kt - 1))
                mm.then_inc(unit_done, 1)
            if straight:
                straight_units(phase, body)
            else:
                over_units(pe, phase, body)

        def pe_ada(pe):
            def body(j, u, i):
                pe_unit_ready(pe, j, u)
                ada_products(pe, j, 2 * (j % 2))
                pe.wait_ge(act_out, u + 1)
                pe.wait_ge(dve_out, u + 1)
                ada_fold(pe, j, i, 4, 0)
            over_units(pe, "ada0a", body)

        ADA_HALF = ADA_COLS // 2

        def ada_products(pe, j, bank):
            for x in range(2):
                for k in range(KT):
                    g, o = k % 4, k * ADA_COLS + x * ADA_HALF
                    mm = pe.matmul(ps[32 * g:32 * g + 32, bank + x, 0:ADA_HALF], cond[:, k, :],
                                   ring[:, j, o:o + ADA_HALF], start=(k < 4), stop=(k >= 4),
                                   tile_position=(0, 32 * g), skip_group_check=True)
            mm.then_inc(unit_done, 1)

        def ada_fold(pe, j, i, bank, at):
            for m in range(3):
                mm = pe.matmul(ps[:, bank, bass.ds(i * 6 + 2 * m + at, 2)], stage_buf[:, j % 2, m * P:(m + 1) * P],
                               K("fold"), start=True, stop=True)
            return mm

        def copy_rows(eng, copy, my_out, me):
            def body(j, u, i):
                eng.wait_ge(unit_done, u + 1)
                copy(stage_buf[:, j % 2, me * ADA_HALF:(me + 1) * ADA_HALF], ps[:, 2 * (j % 2) + me, 0:ADA_HALF])\
                    .then_inc(my_out, 1)
            over_units(eng, "ada0a", body)

        ada_cols = sem("ada_cols")

        def later_ada(layer):
            units = list(range(ADA_FIRST, ADA_UNITS)) + (list(range(ADA_FIRST)) if layer + 1 < DEPTH else [])
            return FIRST[f"ada{layer}b"], units

        def pe_ada_unit(pe, layer, n):
            first, units = later_ada(layer)
            u = first + n
            if 1 <= n <= len(units):
                pe.wait_ge(act_out, u)
                pe.wait_ge(dve_out, u)
                mm = ada_fold(pe, (u - 1) % SLOTS, units[n - 1], 7, ADA_HALF)
                if n == len(units):
                    mm.then_inc(ada_cols, 1)
            if n < len(units):
                pe.wait_ge(loaded[u % SLOTS], 16 * (u // SLOTS + 1))
                ada_products(pe, u % SLOTS, 6)

        def take_ada_rows(eng, copy, my_out, me, layer, n):
            first, units = later_ada(layer)
            if 0 <= n < len(units):
                u = first + n
                eng.wait_ge(unit_done, u + 1)
                copy(stage_buf[:, u % 2, me * ADA_HALF:(me + 1) * ADA_HALF], ps[:, 6 + me, 0:ADA_HALF]).then_inc(my_out, 1)

        def act_copy(act):
            return lambda o, i: act.activation(o, i, ACT.Copy)

        def act_residual(act, phase, n, gates, tiles):
            def body(j, u, i):
                act.wait_ge(unit_done, u + 1)
                act.wait_ge(dve_out, u - 1)
                for m in range(tiles):
                    for lo, hi, s in gates(i * tiles + m):
                        ins = act.activation(stage_buf[:, j % 2, m * n + lo:m * n + hi],
                                             ps[:, 2 * (j % 2) + (m * n) // 512, (m * n) % 512 + lo:(m * n) % 512 + hi],
                                             ACT.Copy, scale=s)
                ins.then_inc(act_out, 1)
            over_units(act, phase, body)

        def dve_residual(dve, phase, c0, n, tiles):
            def body(j, u, i):
                dve.wait_ge(act_out, u + 1)
                x = xT[:, bass.ds(i * tiles, tiles), c0:c0 + n]
                dve.tensor_tensor(x, x, stage_buf[:, j % 2, 0:tiles * n].rearrange("p (m t) -> p m t", t=n), ALU.add)\
                    .then_inc(dve_out, 1)
            over_units(dve, phase, body)

        def pe_ffn(pe, r, c0, n):
            pe_feature_tiles(pe, f"up{r}", 2, hT, c0, n, per_bank=1)
            meet["pe"]()
            pe_feature_tiles(pe, f"down{r}", 1, hidden, 0, n, kt=FT)

        def act_ffn(act, r, c0, n, gates):
            def body(j, u, i):
                act.wait_ge(unit_done, u + 1)
                act.wait_ge(dve_out, u - 1)
                act.activation(stage_buf[:, j % 2, 0:n], ps[:, 2 * (j % 2), 0:n], ACT.Silu).then_inc(act_out, 1)
            over_units(act, f"up{r}", body)
            meet["act"]()
            act_residual(act, f"down{r}", n, gates, 1)

        def dve_ffn(dve, r, c0, n):
            def body(j, u, i):
                dve.wait_ge(act_out, u + 1)
                dve.tensor_tensor(hidden[:, bass.ds(i, 1), 0:n].rearrange("p a n -> p (a n)"),
                                  stage_buf[:, j % 2, 0:n], ps[:, 2 * (j % 2) + 1, 0:n], ALU.mult).then_inc(dve_out, 1)
            over_units(dve, f"up{r}", body)
            meet["dve"]()
            dve_residual(dve, f"down{r}", c0, n, 1)

        norm_sq, norm_sum, norm_rt = sem("norm_sq"), sem("norm_sum"), sem("norm_rt")
        square = work[:, WORK - 4096 - 2048 - 512:WORK - 2048 - 512].rearrange("p (m t) -> p m t", t=TA)
        rstd = work[:, WORK - 2048 - 512:WORK - 2048]

        def pe_norm(pe, r, c0, n):
            for k in range(KT):
                if k % 2 == 0:
                    pe.wait_ge(norm_sq, 4 * r + k // 2 + 1)
                mm = pe.matmul(ps[:, 5, 0:n], K("ones"), square[:, k, 0:n], start=(k == 0), stop=(k == KT - 1))
            mm.then_inc(norm_sum, 1)

        def act_norm(act, r, c0, n):
            for k in range(0, KT, 2):
                act.activation(square[:, k:k + 2, 0:n], xT[:, k:k + 2, c0:c0 + n], ACT.Square, scale=1.0 / 32)\
                    .then_inc(norm_sq, 1)
            act.wait_ge(norm_sum, r + 1)
            act.activation(rstd[:, 0:n], ps[:, 5, 0:n], ACT.Sqrt, bias=eps_col[:, 0:1]).then_inc(norm_rt, 1)

        def dve_norm(dve, r, c0, n, dst, scale, shift):
            dve.wait_ge(norm_rt, r + 1)
            link(dve.reciprocal(rstd[:, 0:n], rstd[:, 0:n]))
            for m in range(KT):
                for lo, hi, s in scale(m):
                    dve.scalar_tensor_tensor(out=dst[:, m, c0 + lo:c0 + hi], in0=xT[:, m, c0 + lo:c0 + hi], scalar=s,
                                             in1=rstd[:, lo:hi], op0=ALU.mult, op1=ALU.mult).then_inc(norm_x, 1)
            if shift is not None:
                pieces = [(m, piece) for m in range(KT) for piece in shift(m)]
                for i, (m, (lo, hi, b)) in enumerate(pieces):
                    dve.wait_ge(norm_x, norm_done[0] + i + 1)
                    dst_m = dst[:, m, c0 + lo:c0 + hi]
                    dve.tensor_scalar(dst_m, dst_m, b, None, ALU.add)
            norm_done[0] += sum(len(scale(m)) for m in range(KT))

        norm_x = sem("norm_x")
        norm_done = [0]

        def segments(c0, n, col):
            return [(s * T - c0, s * T - c0 + T, col(s)) for s in range(2) if c0 <= s * T]

        from_blocks = {"pe": [], "act": [], "dve": [], "pool": []}
        meet, links = {}, {}

        def link(ins):
            links["dve"](ins)

        def alink(ins):
            links["act"](ins)

        def plink(ins):
            links["pool"](ins)

        cond_at = COMMON_N + ONE_N
        assert cond_at + KT * 32 <= CONST_N
        cond = const[:, cond_at:cond_at + KT * 32].rearrange("p (k c) -> p k c", c=32)

        def dve_mod(dve, layer, first, bank, at):
            lo, hi = (0, ADA_TILES) if first else (ADA_TILES, 48)
            link(dve.tensor_tensor(mod[layer][:, lo:hi, :], ps[:, bank, at + 2 * lo:at + 2 * hi].rearrange("p (m s) -> p m s", s=2),
                                   C(f"b_ada{layer}", lo, hi - lo).unsqueeze(2).broadcast_to([P, hi - lo, 2]), ALU.add))
            part, i, name = (1, 0, "norm_mix") if first else (4, 1, "norm_ffn")
            link(dve.scalar_tensor_tensor(out=scl[layer][:, i], in0=mod[layer][:, part * KT:(part + 1) * KT, :], scalar=1.0,
                                          in1=C(f"{name}{layer}", 0, 8).unsqueeze(2).broadcast_to([P, KT, 2]),
                                          op0=ALU.add, op1=ALU.mult))

        FM_ORDER = [(AQ, False), (MK, True), (AQ + 2, False), (MQ, False), (MO, False), (AK, True)]

        def unit_tokens(layer, full):
            return (0, TA) if full or layer < DEPTH - 1 else (T, T)

        def pe_project(pe, layer):
            def token_major(cols, spare):
                def body(j, u, i):
                    pe_unit_ready(pe, j, u)
                    for tt in range(4):
                        bank = 2 * (j % 2) + tt if tt < 2 else spare + tt - 2
                        for k in range(KT):
                            mm = pe.matmul(ps[:, bank, 0:cols], hT[:, k, tt * P:(tt + 1) * P],
                                           ring[:, j, k * cols:(k + 1) * cols], start=(k == 0), stop=(k == KT - 1))
                    mm.then_inc(unit_done, 1)
                return body

            def feature_major(j, u, i):
                tile, full = FM_ORDER[i]
                c0, n = unit_tokens(layer, full)
                pe_unit_ready(pe, j, u)
                for m in range(min(2, FM_TILES - tile)):
                    for k in range(KT):
                        mm = pe.matmul(ps[:, 2 * (j % 2) + m, 0:n], ring[:, j, (m * KT + k) * P:(m * KT + k + 1) * P],
                                       hT[:, k, c0:c0 + n], start=(k == 0), stop=(k == KT - 1))
                mm.then_inc(unit_done, 1)
            straight_units(f"tma{layer}", token_major(272, 4))
            straight_units(f"fm{layer}", feature_major, after=(0, lambda: pe_gate_rows(pe, layer)))
            pe_gate_columns(pe, layer)
            straight_units(f"tmb{layer}", token_major(384, 6))

        def straight_units(phase, body, after=None):
            first, n = FIRST[phase], dict((a, b) for a, b, _ in PHASES)[phase]
            for i in range(n):
                body((first + i) % SLOTS, first + i, i)
                if after and after[0] == i:
                    after[1]()

        def evacuate_project(eng, copy, my_out, layer, me, gate_rows):
            def token_major(cols, at, spare):
                def body(j, u, i):
                    eng.wait_ge(unit_done, u + 1)
                    bank = spare if me else 2 * (j % 2)
                    copy(tm[:, 2 * me:2 * me + 2, at:at + cols], ps[:, bank:bank + 2, 0:cols]).then_inc(my_out, 1)
                return body

            def feature_major(j, u, i):
                tile, full = FM_ORDER[i]
                c0, n = unit_tokens(layer, full)
                eng.wait_ge(unit_done, u + 1)
                if tile + 1 < FM_TILES:
                    ins = copy(proj[:, tile + me, c0:c0 + n], ps[:, 2 * (j % 2) + me, 0:n])
                else:
                    if me:
                        eng.wait_ge(act_out, u + 1)
                    ins = copy(proj[:, tile, me * T:(me + 1) * T], ps[:, 2 * (j % 2), me * T:(me + 1) * T])
                ins.then_inc(my_out, 1)
            straight_units(f"tma{layer}", token_major(272, MV, 4))
            straight_units(f"fm{layer}", feature_major, after=(0, lambda: gate_rows(eng, layer)))
            straight_units(f"tmb{layer}", token_major(384, AV, 6))

        qk_sq, qk_sum, qk_rt, qk_n, qk_rot, qk_cos, qk_r = (
            sem(f"qk_{x}") for x in ("sq", "sum", "rt", "n", "rot", "cos", "r"))
        qa = Area(mixer_free)
        qk_buf = [[qa(TA) for _ in range(2)] for _ in range(4)]

        def qk_tiles(layer):
            c0, n = unit_tokens(layer, False)
            return [(AQ + m, c0, n, f"q_norm{layer}") for m in range(4)] + [(AK, 0, TA, f"k_norm{layer}")]

        def pe_qk(pe, layer):
            for i, (m, c0, n, _) in enumerate(qk_tiles(layer), 5 * layer):
                pe.wait_ge(qk_sq, i + 1)
                if i >= 2:
                    pe.wait_ge(qk_rt, i - 1)
                pe.matmul(ps[:, 4 + i % 2, 0:n], K("blockones"), qk_buf[0][i % 2][:, 0:n], start=True, stop=True)\
                    .then_inc(qk_sum, 1)
                if i > 5 * layer:
                    rotate(pe, i - 1, qk_tiles(layer)[i - 1 - 5 * layer])
            rotate(pe, 5 * layer + 4, qk_tiles(layer)[4])

        def rotate(pe, i, tile):
            m, c0, n, _ = tile
            pe.wait_ge(qk_n, i + 1)
            if i >= 2:
                pe.wait_ge(qk_r, i - 1)
            pe.matmul(ps[:, 6 + i % 2, 0:n], K("rot1"), qk_buf[1][i % 2][:, 0:n], start=True, stop=True)\
                .then_inc(qk_rot, 1)

        def act_qk(act, layer):
            for i, (m, c0, n, _) in enumerate(qk_tiles(layer), 5 * layer):
                if i >= 2:
                    act.wait_ge(qk_sum, i - 1)
                act.activation(qk_buf[0][i % 2][:, 0:n], proj[:, m, c0:c0 + n], ACT.Square, scale=0.125)\
                    .then_inc(qk_sq, 1)
                if i > 5 * layer:
                    root(act, i - 1, qk_tiles(layer)[i - 1 - 5 * layer][2])
            root(act, 5 * layer + 4, qk_tiles(layer)[4][2])

        def root(act, i, n):
            act.wait_ge(qk_sum, i + 1)
            if i >= 2:
                act.wait_ge(qk_r, i - 1)
            act.activation(qk_buf[3][i % 2][:, 0:n], ps[:, 4 + i % 2, 0:n], ACT.Sqrt, bias=eps_col[:, 0:1]).then_inc(qk_rt, 1)

        def dve_qk(dve, layer):
            def finish(i, tile):
                m, c0, n, _ = tile
                dve.wait_ge(qk_rot, i + 1)
                link(dve.tensor_tensor(qk_buf[3][i % 2][:, 0:n], ps[:, 6 + i % 2, 0:n], K("sin1")[:, c0:c0 + n], ALU.mult))
                dve.wait_ge(qk_cos, i + 1)
                dve.tensor_tensor(proj[:, m, c0:c0 + n], qk_buf[2][i % 2][:, 0:n], qk_buf[3][i % 2][:, 0:n], ALU.add)\
                    .then_inc(qk_r, 1)
                dve.wait_ge(qk_r, i + 1)
            tiles = qk_tiles(layer)
            for i, (m, c0, n, gain) in enumerate(tiles, 5 * layer):
                dve.wait_ge(qk_rt, i + 1)
                link(dve.reciprocal(qk_buf[3][i % 2][:, 0:n], qk_buf[3][i % 2][:, 0:n]))
                if i >= 2:
                    dve.wait_ge(qk_cos, i - 1)
                dve.scalar_tensor_tensor(out=qk_buf[1][i % 2][:, 0:n], in0=proj[:, m, c0:c0 + n], scalar=C(gain),
                                         in1=qk_buf[3][i % 2][:, 0:n], op0=ALU.mult, op1=ALU.mult).then_inc(qk_n, 1)
                dve.wait_ge(qk_n, i + 1)
                if i > 5 * layer:
                    finish(i - 1, tiles[i - 1 - 5 * layer])
            finish(5 * layer + 4, tiles[4])

        def pool_qk(pool, layer):
            for i, (m, c0, n, _) in enumerate(qk_tiles(layer), 5 * layer):
                pool.wait_ge(qk_n, i + 1)
                if i >= 2:
                    pool.wait_ge(qk_r, i - 1)
                pool.tensor_tensor(qk_buf[2][i % 2][:, 0:n], qk_buf[1][i % 2][:, 0:n], K("cos1")[:, c0:c0 + n], ALU.mult)\
                    .then_inc(qk_cos, 1)

        at_s, at_max, at_exp, at_p, at_t, at_pt, at_o, at_out = (
            sem(f"at_{x}") for x in ("scores", "max", "exp", "probs", "turned", "probsT", "o", "out"))
        aa = Area(mixer_free)
        probs = [aa(TA) for _ in range(3)]
        probsT = [aa(TA) for _ in range(2)]
        at_small = aa(4 * 64).rearrange("p (k n) -> p k n", k=4)

        def attention_units(layer):
            tiles = range(4) if layer < DEPTH - 1 else range(2, 4)
            return [(qt, h // 2, h % 2, (2 if qt < 2 else 4) * P) for qt in tiles for h in range(8)]

        AT_BASE = [0, 32, 48]

        def pe_attention(pe, layer):
            units, base = attention_units(layer), AT_BASE[layer]
            n = len(units)
            for i in range(n + 3):
                if i < n:
                    qt, j, b, nk = units[i]
                    if i >= 3:
                        pe.wait_ge(at_exp, base + i - 2)
                    pe.matmul(ps[:, 3 + i % 3, 0:nk], proj[64 * b:64 * b + 64, AQ + j, qt * P:(qt + 1) * P],
                              proj[64 * b:64 * b + 64, AK, 0:nk], start=True, stop=True).then_inc(at_s, 1)
                if 2 <= i < n + 2:
                    x = i - 2
                    nk = units[x][3]
                    pe.wait_ge(at_p, base + x + 1)
                    if x >= 2:
                        pe.wait_ge(at_pt, base + x - 1)
                    for s in range(nk // P):
                        mm = pe.transpose(ps[:, 6 + x % 2, s * P:(s + 1) * P], probs[x % 3][:, s * P:(s + 1) * P], K("ident"))
                    mm.then_inc(at_t, 1)
                if i >= 3:
                    x = i - 3
                    qt, j, b, nk = units[x]
                    pe.wait_ge(at_pt, base + x + 1)
                    if x >= 6 and b == 0:
                        pe.wait_ge(at_out, (base + x) // 2 - 2)
                    for s in range(nk // P):
                        mm = pe.matmul(ps[64 * b:64 * b + 64, (x // 2) % 3, 0:P], tm[:, s, AV + 64 * b:AV + 64 * b + 64],
                                       probsT[x % 2][:, s * P:(s + 1) * P], start=(s == 0), stop=(s == nk // P - 1),
                                       skip_group_check=True)
                    mm.then_inc(at_o, 1)

        def act_attention(act, layer):
            units, base = attention_units(layer), AT_BASE[layer]
            n = len(units)
            for i in range(n + 2):
                if i < n:
                    nk = units[i][3]
                    act.wait_ge(at_max, base + i + 1)
                    if i >= 3:
                        act.wait_ge(at_t, base + i - 2)
                    act.activation(probs[i % 3][:, 0:nk], ps[:, 3 + i % 3, 0:nk], ACT.Exp, scale=0.125,
                                   bias=at_small[:, 1, i:i + 1], accum_out=at_small[:, 2, i:i + 1]).then_inc(at_exp, 1)
                if i >= 2:
                    x = i - 2
                    nk = units[x][3]
                    act.wait_ge(at_t, base + x + 1)
                    if x >= 2:
                        act.wait_ge(at_o, base + x - 1)
                    act.activation(probsT[x % 2][:, 0:nk], ps[:, 6 + x % 2, 0:nk], ACT.Copy).then_inc(at_pt, 1)

        def dve_attention(dve, layer):
            units, base = attention_units(layer), AT_BASE[layer]
            n = len(units)
            for i in range(n + 4):
                if i < n:
                    nk = units[i][3]
                    dve.wait_ge(at_s, base + i + 1)
                    link(dve.tensor_reduce(at_small[:, 0, i:i + 1], ps[:, 3 + i % 3, 0:nk], AX, ALU.max))
                    dve.tensor_scalar(at_small[:, 1, i:i + 1], at_small[:, 0, i:i + 1], -0.125, None, ALU.mult)\
                        .then_inc(at_max, 1)
                if 1 <= i <= n:
                    x = i - 1
                    dve.wait_ge(at_exp, base + x + 1)
                    link(dve.reciprocal(at_small[:, 3, x:x + 1], at_small[:, 2, x:x + 1]))
                    pr = probs[x % 3][:, 0:units[x][3]]
                    dve.tensor_scalar(pr, pr, at_small[:, 3, x:x + 1], None, ALU.mult).then_inc(at_p, 1)
                if i >= 4:
                    x = i - 4
                    qt, j, b, nk = units[x]
                    if b == 1:
                        dve.wait_ge(at_o, base + x + 1)
                        dve.tensor_copy(mixT[:, j, qt * P:(qt + 1) * P], ps[:, (x // 2) % 3, 0:P]).then_inc(at_out, 1)

        pl_mean, pl_in, pl_y, pl_out = (sem(f"pl_{x}") for x in ("mean", "in", "y", "out"))
        pa = Area(mixer_free)
        pooled = pa(2 * TA).rearrange("p (g t) -> p g t", t=TA)

        def pool_segments(layer):
            return (0, 1) if layer < DEPTH - 1 else (1,)

        def pe_pool(pe, layer):
            for seg in pool_segments(layer):
                for g in range(4):
                    b = 64 * (g % 2)
                    for s in range(2):
                        mm = pe.matmul(ps[b:b + 64, seg, (g // 2) * T:(g // 2 + 1) * T],
                                       tm[:, 2 * seg + s, PP + 64 * g:PP + 64 * g + 64],
                                       K("band")[:, (s * 4 + g) * T:(s * 4 + g + 1) * T], start=(s == 0), stop=(s == 1),
                                       skip_group_check=True)
            mm.then_inc(pl_mean, 1)
            pe.wait_ge(pl_in, layer + 1)
            c0, n = unit_tokens(layer, False)
            for g in range(4):
                b = 64 * (g % 2)
                mm = pe.matmul(ps[b:b + 64, 2 + g // 2, 0:n], C(f"pool_w{layer}", 64 * (g // 2), 64, slice(b, b + 64)),
                               pooled[b:b + 64, g // 2, c0:c0 + n], start=True, stop=True, skip_group_check=True)
            mm.then_inc(pl_y, 1)

        def dve_pool(dve, layer):
            dve.wait_ge(pl_mean, layer + 1)
            for seg in pool_segments(layer):
                ins = dve.tensor_copy(pooled[:, :, seg * T:(seg + 1) * T], ps[:, seg, :].rearrange("p (g t) -> p g t", g=2))
            ins.then_inc(pl_in, 1)
            dve.wait_ge(pl_y, layer + 1)
            c0, n = unit_tokens(layer, False)
            for g in range(2):
                dve.tensor_scalar(mixT[:, 6 + g, c0:c0 + n], ps[:, 2 + g, 0:n], C(f"pool_scale{layer}", g), None, ALU.mult)

        ml_t, ml_abs, ml_ln, ml_rows, ml_cols, ml_d, ml_enm = (
            sem(f"ml_{x}") for x in ("gates_t", "abs", "ln", "rows", "cols", "dcols", "enm"))
        ml_nb, ml_nbs, ml_s, ml_z, ml_e, ml_ez, ml_p, ml_num, ml_h = (
            sem(f"ml_{x}") for x in ("nb", "nb_sb", "s", "z", "e", "masked", "p", "num", "h"))
        ml_sq, ml_hn, ml_hT, ml_one = (sem(f"ml_{x}") for x in ("sq", "hn", "hT", "vones"))
        ml_cols_taken = sem("ml_cols_taken")
        ma = Area(mixer_free)
        vones = ma(4 * 4 * 65).rearrange("p (t h c) -> p t h c", t=4, h=4)
        ml_pre = mixT[0:4, 0:4, :]
        ml_neg = mixT[0:4, 4:6, :]
        ml_e1 = mixT[0:4, 6:8, :]
        zero_row = ma(TA)
        cols = ma(64).rearrange("p (k d t h) -> p k d t h", k=2, d=2, t=4)
        nb = ma(2 * 2 * TA).rearrange("p (b d t) -> p b d t", b=2, d=2)
        pbuf = ma(8 * TA).rearrange("p (s d t) -> p s d t", s=4, d=2)
        ml_row = pbuf[0:4, 0:3, :, :].rearrange("p s d t -> p (s d) t")
        ebuf = ma(4 * TA).rearrange("p (b d t) -> p b d t", b=2, d=2)
        hsum = hT[:, 0:2, :].rearrange("p a (t h v) -> p (a t) h v", h=4, v=64)
        hnum = hT[:, 2:6, :].rearrange("p (d a) (t h v) -> p d (a t) h v", d=2, h=4, v=64)
        hden = ma(3 * 2 * 4).rearrange("p (k d t) -> p k d t", k=3, d=2)
        hss = ma(2 * 16).rearrange("p (k n) -> p k n", k=2)

        def ml_range(s, d, c0):
            lo, hi = (s * P, TA) if d == 0 else ((0, TA) if s < 2 else (T, T + P) if s == 2 else (T, TA))
            return max(lo, c0), hi

        def ml_sources(tt, d):
            if d == 0:
                return range(0, tt + 1)
            return range(tt, 2) if tt < 2 else [0, 1] + list(range(tt, 4))

        def ml_tiles(layer):
            return range(0, 4) if layer < DEPTH - 1 else range(2, 4)

        def pe_gate_rows(pe, layer):
            pe.wait_ge(act_out, FIRST[f"tma{layer}"] + 1)
            pe.wait_ge(dve_out, FIRST[f"tma{layer}"] + 1)
            for ty in range(4):
                for tt in range(4):
                    mm = pe.transpose(ps[0:4, 4 + ty, tt * P:(tt + 1) * P], tm[:, tt, MG + 4 * ty:MG + 4 * ty + 4], K("ident"))
            mm.then_inc(ml_t, 1)

        def pe_gate_columns(pe, layer):
            pe.wait_ge(ml_rows, layer + 1)
            for k, row in enumerate((2, 0)):
                for d in range(2):
                    for tt in range(4):
                        mm = pe.transpose(ps[:, 4, 4 * ((k * 2 + d) * 4 + tt):4 * ((k * 2 + d) * 4 + tt) + 4],
                                          ml_row[:, row + d, tt * P:(tt + 1) * P], K("ident")[0:4, 0:4])
            mm.then_inc(ml_cols, 1)

        def pe_mlstm(pe, layer):
            c0, _ = unit_tokens(layer, False)

            def running_max(h):
                for d in range(2):
                    n = 2 * (4 * layer + h) + d
                    if h:
                        pe.wait_ge(ml_nbs, n - 1)
                    elif d == 1:
                        pe.wait_ge(ml_cols_taken, layer + 1)
                    pe.matmul(ps[:, 5 - d, 0:TA], K("sel")[0:4, h * P:(h + 1) * P], ml_neg[:, d, :], start=True, stop=True)\
                        .then_inc(ml_nb, 1)
            def sums(h):
                hh = 4 * layer + h
                pe.wait_ge(ml_p, 4 * hh + 4)
                if h >= 1:
                    pe.wait_ge(ml_h, hh)
                for d in range(2):
                    for tt in ml_tiles(layer):
                        src = list(ml_sources(tt, d))
                        for s in src:
                            mm = pe.matmul(ps[:, 2 + d, 65 * tt:65 * tt + 65], pbuf[:, s, d, tt * P:(tt + 1) * P],
                                           vones[:, s, h, :], start=(s == src[0]), stop=(s == src[-1]))
                mm.then_inc(ml_num, 1)

            running_max(0)
            for h in range(4):
                hh = 4 * layer + h
                b = 64 * (h % 2)
                for s in range(4):
                    n = 4 * hh + s
                    if n >= 2 + 16 * layer:
                        pe.wait_ge(ml_p, n - 1)
                    pe.matmul(ps[:, n % 2, c0:TA], proj[b:b + 64, MK + h // 2, s * P:(s + 1) * P],
                              proj[b:b + 64, MQ + h // 2, c0:TA], start=True, stop=True).then_inc(ml_s, 1)
                    if s == 3 and h < 3:
                        running_max(h + 1)
                    pe_ada_unit(pe, layer, 4 * h + s)
                    if s == 0 and h >= 1:
                        sums(h - 1)
            sums(3)
            pe_ada_unit(pe, layer, 16)
            pe.wait_ge(ml_hn, layer + 1)
            for tt in ml_tiles(layer):
                for f in range(2):
                    mm = pe.transpose(ps[:, f, tt * P:(tt + 1) * P],
                                      hsum[:, tt, 2 * f:2 * f + 2, :].rearrange("p h v -> p (h v)"), K("ident"))
            mm.then_inc(ml_hT, 1)

        def act_gate_rows(act, layer):
            act.wait_ge(ml_abs, layer + 1)
            alink(act.activation(ml_e1, ml_e1, ACT.Exp, scale=-1.0))
            act.activation(ml_e1, ml_e1, ACT.Ln, bias=1.0).then_inc(ml_ln, 1)

        def act_mlstm(act, layer):
            c0, n = unit_tokens(layer, False)
            act.wait_ge(ml_cols, layer + 1)
            act.activation(cols[:, 1].rearrange("p d t h -> p (d t h)"), ps[:, 4, 32:64], ACT.Exp, scale=-1.0)\
                .then_inc(ml_enm, 1)

            def take_running_max(h):
                hh = 4 * layer + h
                for d in range(2):
                    act.wait_ge(ml_nb, 2 * hh + d + 1)
                    if h >= 2:
                        act.wait_ge(ml_z, 8 * (hh - 1))
                    act.activation(nb[:, h % 2, d, :], ps[:, 5 - d, 0:TA], ACT.Copy).then_inc(ml_nbs, 1)
            take_running_max(0)
            for h in range(4):
                for s in range(4):
                    for d in range(2):
                        lo, hi = ml_range(s, d, c0)
                        m = 8 * (4 * layer + h) + 2 * s + d
                        act.wait_ge(ml_z, m + 1)
                        act.activation(ebuf[:, s % 2, d, lo:hi], ebuf[:, s % 2, d, lo:hi], ACT.Exp).then_inc(ml_e, 1)
                    take_ada_rows(act, act_copy(act), act_out, 0, layer, 4 * h + s - 1)
                    if s == 2 and h < 3:
                        take_running_max(h + 1)
            take_ada_rows(act, act_copy(act), act_out, 0, layer, 15)
            act.wait_ge(ml_h, 4 * layer + 4)
            act.wait_ge(ml_hsum, layer + 1)
            t0 = ml_tiles(layer)[0]
            act.activation(hnum[:, 0, t0:4], hsum[:, t0:4], ACT.Square, scale=0.125).then_inc(ml_sq, 1)
            act.activation(proj[:, MO:MO + 2, c0:TA], proj[:, MO:MO + 2, c0:TA], ACT.Sigmoid).then_inc(ml_sig, 1)
            act.wait_ge(ml_ss, layer + 1)
            nn = (4 - t0) * 4
            act.activation(hss[:, 1, 0:nn], hss[:, 0, 0:nn], ACT.Sqrt, bias=eps_col[:, 0:1]).then_inc(ml_rt, 1)

        ml_hsum, ml_sig, ml_ss, ml_rt = sem("ml_hsum"), sem("ml_sig"), sem("ml_ss"), sem("ml_rt")

        def pool_mlstm(pool, layer):
            c0, _ = unit_tokens(layer, False)
            pool.memset(vones[:, :, :, 64:65], 1.0)
            for tt in range(4):
                ins = pool.tensor_copy(vones[:, tt, :, 0:64], tm[:, tt, MV:MV + 256].rearrange("p (h v) -> p h v", h=4))
            ins.then_inc(ml_one, 1)
            for h in range(4):
                for s in range(4):
                    for d in range(2):
                        m = 8 * (4 * layer + h) + 2 * s + d
                        pool.wait_ge(ml_e, m + 1)
                        lo, hi = ml_range(s, d, c0)
                        if lo <= s * P < hi:
                            diag = ebuf[:, s % 2, d, s * P:(s + 1) * P]
                            pool.tensor_tensor(diag, diag, K(f"tri{d}"), ALU.mult).then_inc(ml_ez, 1)

        def dve_gate_rows(dve, layer):
            dve.memset(zero_row, 0.0)
            dve.wait_ge(ml_t, layer + 1)
            for ty in range(4):
                ins = dve.tensor_scalar(ml_pre[:, ty, :], ps[0:4, 4 + ty, :], C(f"b_gates{layer}", ty, 1, slice(0, 4)), None, ALU.add)
            link(ins)
            lf, li = ml_pre[:, 1:4:2, :], ml_pre[:, 0:4:2, :]
            dve.scalar_tensor_tensor(out=ml_e1, in0=lf, scalar=-1.0, in1=lf, op0=ALU.mult, op1=ALU.max).then_inc(ml_abs, 1)
            dve.wait_ge(ml_ln, layer + 1)
            link(dve.scalar_tensor_tensor(out=lf, in0=lf, scalar=0.0, in1=ml_e1, op0=ALU.min, op1=ALU.subtract))
            z = zero_row[0:4, :]
            B, Dr, M = (ml_row[:, 2 * k:2 * k + 2, :] for k in range(3))

            def scans(dst, a, b, op):
                dve.tensor_tensor_scan(dst[:, 0, :], a[:, 0, :], b[:, 0, :], 0.0, op, op)
                link(dve.tensor_tensor_scan(dst[:, 1, 0:T][:, ::-1], a[:, 1, 0:T][:, ::-1], b[:, 1, 0:T][:, ::-1], 0.0, op, op))
                link(dve.tensor_tensor_scan(dst[:, 1, T:TA][:, ::-1], a[:, 1, T:TA][:, ::-1], b[:, 1, T:TA][:, ::-1],
                                            dst[:, 1, 0:1], op, op))
            scans(B, lf, z.unsqueeze(1).broadcast_to([4, 2, TA]), ALU.add)
            link(dve.tensor_tensor(Dr, li, B, ALU.subtract))
            scans(M, Dr, Dr, ALU.max)
            dve.tensor_scalar(ml_neg, M, -1.0, None, ALU.mult)
            dve.tensor_tensor(B, B, M, ALU.add).then_inc(ml_rows, 1)

        def dve_mlstm(dve, layer):
            c0, _ = unit_tokens(layer, False)
            dve.wait_ge(ml_enm, layer + 1)
            dve.tensor_copy(cols[:, 0].rearrange("p d t h -> p (d t h)"), ps[:, 4, 0:32]).then_inc(ml_cols_taken, 1)
            dve.wait_ge(ml_cols_taken, layer + 1)
            t0 = ml_tiles(layer)[0]

            def log_weights(n):
                h, s = n // 4, n % 4
                for d in range(2):
                    lo, hi = ml_range(s, d, c0)
                    dve.wait_ge(ml_nbs, 2 * (4 * layer + h) + d + 1)
                    dve.tensor_scalar(ebuf[:, s % 2, d, lo:hi], nb[:, h % 2, d, lo:hi], cols[:, 0, d, s, h:h + 1], 0.0,
                                      ALU.add, ALU.min).then_inc(ml_z, 1)

            def outputs(h):
                hh = 4 * layer + h
                dve.wait_ge(ml_num, hh + 1)
                both = ps[:, 2:4, 0:260].rearrange("p d (t c) -> p d t c", c=65)[:, :, t0:4]
                link(dve.tensor_copy(hden[:, 0, :, t0:4], both[:, :, :, 64]))
                link(dve.scalar_tensor_tensor(out=hden[:, 1, :, t0:4], in0=hden[:, 0, :, t0:4], scalar=-1.0,
                                              in1=hden[:, 0, :, t0:4], op0=ALU.mult, op1=ALU.max))
                link(dve.tensor_tensor(hden[:, 1, :, t0:4], hden[:, 1, :, t0:4], cols[:, 1, :, t0:4, h], ALU.max))
                link(dve.reciprocal(hden[:, 2, :, t0:4], hden[:, 1, :, t0:4]))
                for d in range(2):
                    ins = dve.tensor_tensor(hnum[:, d, t0:4, h, :], both[:, d, :, 0:64],
                                            hden[:, 2, d, t0:4].unsqueeze(2).broadcast_to([P, 4 - t0, 64]), ALU.mult)
                ins.then_inc(ml_h, 1)
                dve.wait_ge(ml_h, hh + 1)

            copy = lambda o, i: dve.tensor_copy(o, i)
            ez = ML_EZ[layer]
            log_weights(0)
            for n in range(16):
                h, s = n // 4, n % 4
                hh, m = 4 * layer + h, 16 * layer + n
                if n + 1 < 16:
                    log_weights(n + 1)
                take_ada_rows(dve, copy, dve_out, 1, layer, n - 1)
                dve.wait_ge(ml_s, m + 1)
                if s == 0 and h >= 1:
                    dve.wait_ge(ml_num, hh)
                for d in range(2):
                    lo, hi = ml_range(s, d, c0)
                    dve.wait_ge(ml_e, 2 * m + d + 1)
                    if lo <= s * P < hi:
                        ez += 1
                        dve.wait_ge(ml_ez, ez)
                    ins = dve.scalar_tensor_tensor(out=pbuf[:, s, d, lo:hi], in0=ps[:, m % 2, lo:hi], scalar=0.125,
                                                   in1=ebuf[:, s % 2, d, lo:hi], op0=ALU.mult, op1=ALU.mult)
                ins.then_inc(ml_p, 1)
                dve.wait_ge(ml_p, m + 1)
                if s == 1 and h >= 1:
                    outputs(h - 1)
            take_ada_rows(dve, copy, dve_out, 1, layer, 15)
            outputs(3)
            dve.tensor_tensor(hsum[:, t0:4], hnum[:, 0, t0:4], hnum[:, 1, t0:4], ALU.add).then_inc(ml_hsum, 1)
            dve.wait_ge(ml_sq, layer + 1)
            nn = (4 - t0) * 4
            dve.tensor_reduce(hss[:, 0, 0:nn], hnum[:, 0, t0:4].rearrange("p t h v -> p (t h) v"), AX, ALU.add)\
                .then_inc(ml_ss, 1)
            dve.wait_ge(ml_rt, layer + 1)
            link(dve.reciprocal(hss[:, 1, 0:nn], hss[:, 1, 0:nn]))
            hs = hsum[:, t0:4].rearrange("p t h v -> p (t h) v")
            dve.tensor_tensor(hs, hs, hss[:, 1, 0:nn].unsqueeze(2).broadcast_to([P, nn, 64]), ALU.mult).then_inc(ml_hn, 1)
            dve.wait_ge(ml_hT, layer + 1)
            dve.wait_ge(ml_sig, layer + 1)
            for f in range(2):
                dve.scalar_tensor_tensor(out=mixT[:, 4 + f, c0:TA], in0=ps[:, f, c0:TA], scalar=C(f"ml_norm{layer}", f),
                                         in1=proj[:, MO + f, c0:TA], op0=ALU.mult, op1=ALU.mult)
            dve.wait_ge(ada_cols, layer + 1)
            dve_mod(dve, layer, False, 7, ADA_HALF)
            if layer + 1 < DEPTH:
                dve_mod(dve, layer + 1, True, 7, ADA_HALF)

        def ez_total(layer):
            c0 = unit_tokens(layer, False)[0]
            return 4 * sum(ml_range(s, d, c0)[0] <= s * P < ml_range(s, d, c0)[1] for s in range(4) for d in range(2))

        ML_EZ = [0, ez_total(0)]

        a = Area()
        rproj = a(R_TILES * T).rearrange("p (m t) -> p m t", t=T)
        attnT = a(2 * T).rearrange("p (m t) -> p m t", t=T)
        yT = a(KT * T).rearrange("p (m t) -> p m t", t=T)
        second_free = a.at
        a = Area(second_free)
        qkT = a(12 * T).rearrange("p (m t) -> p m t", t=T)
        vtm = a(2 * 768).rearrange("p (k c) -> p k c", c=768)
        s_probs = [a(768) for _ in range(2)]
        s_probsT = [a(768) for _ in range(2)]
        s_masked = [a(768) for _ in range(2)]
        s_small = a(64).rearrange("p (k n) -> p k n", k=4)
        s_cos = [a(2 * T) for _ in range(2)]
        s_sin = [a(2 * T) for _ in range(2)]
        a = Area(second_free)
        ya = a(KT * T).rearrange("p (m t) -> p m t", t=T)
        yr = a(KT * T).rearrange("p (m t) -> p m t", t=T)
        merged = a(KT * T).rearrange("p (m t) -> p m t", t=T)

        def copy_out(eng, copy, my_out, phase, pieces):
            def body(j, u, i):
                eng.wait_ge(unit_done, u + 1)
                for o, s in pieces(j, i):
                    ins = copy(o, s)
                ins.then_inc(my_out, 1)
            over_units(eng, phase, body)

        def three_tiles(dst, me):
            def pieces(j, i):
                if me == 0:
                    return [(dst[:, bass.ds(i * 3, 2), :], ps[:, 2 * (j % 2), :].rearrange("p (m t) -> p m t", t=T))]
                return [(dst[:, bass.ds(i * 3 + 2, 1), :], ps[:, 2 * (j % 2) + 1, 0:T].unsqueeze(1))]
            return pieces

        def value_halves(me):
            def pieces(j, i):
                return [(vtm[:, me, i * 384:(i + 1) * 384], ps[:, 2 * (j % 2) + me, 0:384])]
            return pieces

        def lora_tiles(me):
            def pieces(j, i):
                if me == 0:
                    return [(rproj[:, RL:RL + 2, :], ps[:, 2 * (j % 2), :].rearrange("p (m t) -> p m t", t=T))]
                return [(rproj[0:32, RL + 2, :], ps[0:32, 2 * (j % 2) + 1, 0:T])]
            return pieces

        def bank_each(dst, me, per):
            def pieces(j, i):
                return [(dst[:, i * 2 * per + me * per:i * 2 * per + (me + 1) * per, :],
                         ps[:, 2 * (j % 2) + me, 0:per * T].rearrange("p (m t) -> p m t", t=T))]
            return pieces

        def pe_values(pe):
            def body(j, u, i):
                pe_unit_ready(pe, j, u)
                for tt in range(2):
                    for k in range(KT):
                        mm = pe.matmul(ps[:, 2 * (j % 2) + tt, 0:384], hT[:, k, T + tt * P:T + (tt + 1) * P],
                                       ring[:, j, k * 384:(k + 1) * 384], start=(k == 0), stop=(k == KT - 1))
                mm.then_inc(unit_done, 1)
            straight_units("v", body)

        def pe_lora(pe):
            def body(j, u, i):
                pe_unit_ready(pe, j, u)
                for at, m, bank, o in ((0, P, 0, 0), (P, P, 0, T), (2 * P, 32, 1, 0)):
                    for k in range(KT):
                        w = ring[:, j, k * 288 + at:k * 288 + at + m]
                        mm = pe.matmul(ps[0:m, 2 * (j % 2) + bank, o:o + T], w, hT[:, k, T:TA],
                                       start=(k == 0), stop=(k == KT - 1))
                mm.then_inc(unit_done, 1)
            straight_units("lora", body)

        sr_rot, sr_cos, sr_out = (sem(f"sr_{x}") for x in ("rot", "cos", "out"))
        two = lambda v: v.rearrange("p (m t) -> p m t", t=T)

        def pe_rope(pe):
            for i in range(6):
                if i >= 2:
                    pe.wait_ge(sr_out, i - 1)
                pe.matmul(ps[:, 4 + i % 2, :], K("rot2"), qkT[:, 2 * i:2 * i + 2, :].rearrange("p m t -> p (m t)"),
                          start=True, stop=True).then_inc(sr_rot, 1)

        def pool_rope(pool):
            for i in range(6):
                if i >= 2:
                    pool.wait_ge(sr_out, i - 1)
                pool.tensor_tensor(two(s_cos[i % 2]), qkT[:, 2 * i:2 * i + 2, :],
                                   K("cos2").unsqueeze(1).broadcast_to([P, 2, T]), ALU.mult).then_inc(sr_cos, 1)

        def dve_rope(dve):
            for i in range(6):
                dve.wait_ge(sr_rot, i + 1)
                link(dve.tensor_tensor(two(s_sin[i % 2]), two(ps[:, 4 + i % 2, :]),
                                       K("sin2").unsqueeze(1).broadcast_to([P, 2, T]), ALU.mult))
                dve.wait_ge(sr_cos, i + 1)
                dve.tensor_tensor(qkT[:, 2 * i:2 * i + 2, :], two(s_cos[i % 2]), two(s_sin[i % 2]), ALU.add)\
                    .then_inc(sr_out, 1)

        S_UNITS = [(qt, hh) for qt in range(2) for hh in range(4)]
        s_max, s_copied = sem("s_max"), sem("s_copied")
        SB = 48

        def score_banks(i):
            return 4 if i % 2 == 0 else 2

        def s_scores(i, w):
            return ps[:, score_banks(i):score_banks(i) + 2, :].rearrange("p b n -> p (b n)")[:, 0:w]

        def pe_dilated(pe):
            n = len(S_UNITS)
            for i in range(n + 2):
                if i < n:
                    qt, hh = S_UNITS[i]
                    nk = (qt + 1) * P
                    b = 64 * (hh % 2)
                    if i >= 2:
                        pe.wait_ge(s_max, i - 1)
                    for g in range(3):
                        m = (4 * g + hh) // 2
                        o = score_banks(i) * 512 + g * nk
                        mm = pe.matmul(ps[:, o // 512, o % 512:o % 512 + nk], qkT[b:b + 64, m, qt * P:(qt + 1) * P],
                                       qkT[b:b + 64, 6 + m, 0:nk], start=True, stop=True)
                    mm.then_inc(at_s, 1)
                if 1 <= i <= n:
                    qt, hh = S_UNITS[i - 1]
                    blocks = 3 * (qt + 1)
                    pe.wait_ge(at_p, SB + i)
                    if i >= 2:
                        pe.wait_ge(at_pt, SB + i - 1)
                    for s in range(blocks):
                        mm = pe.transpose(ps[:, 6 + s // 4, (s % 4) * P:(s % 4 + 1) * P],
                                          s_probs[(i - 1) % 2][:, s * P:(s + 1) * P], K("ident"))
                    mm.then_inc(at_t, 1)
                if i >= 2:
                    qt, hh = S_UNITS[i - 2]
                    b = 64 * (hh % 2)
                    pe.wait_ge(at_pt, SB + i - 1)
                    blocks = [(g, s) for g in range(3) for s in range(qt + 1)]
                    for x, (g, s) in enumerate(blocks):
                        v = vtm[:, s, (4 * g + hh) * 64:(4 * g + hh + 1) * 64]
                        o = ((i - 2) // 2) * P
                        mm = pe.matmul(ps[b:b + 64, 0, o:o + P], v, s_probsT[i % 2][:, x * P:(x + 1) * P],
                                       start=(x == 0), stop=(x == len(blocks) - 1), skip_group_check=True)
                    mm.then_inc(at_o, 1)

        def act_dilated(act):
            def turn(i):
                w = 3 * (S_UNITS[i][0] + 1) * P
                act.wait_ge(at_t, SB + i + 1)
                if i >= 2:
                    act.wait_ge(at_o, SB + i - 1)
                act.activation(s_probsT[i % 2][:, 0:w], ps[:, 6:8, :].rearrange("p b n -> p (b n)")[:, 0:w], ACT.Copy)\
                    .then_inc(at_pt, 1)
            for i, (qt, hh) in enumerate(S_UNITS):
                w = 3 * (qt + 1) * P
                act.wait_ge(at_max, SB + i + 1)
                if i >= 2:
                    act.wait_ge(at_t, SB + i - 1)
                act.activation(s_probs[i % 2][:, 0:w], s_masked[i % 2][:, 0:w], ACT.Exp, scale=0.125,
                               bias=s_small[:, 1, i:i + 1], accum_out=s_small[:, 2, i:i + 1]).then_inc(at_exp, 1)
                if i >= 1:
                    turn(i - 1)
            turn(len(S_UNITS) - 1)

        def dve_dilated(dve):
            n = len(S_UNITS)
            for i in range(n + 1):
                if i < n:
                    qt, hh = S_UNITS[i]
                    w = 3 * (qt + 1) * P
                    dve.wait_ge(at_s, SB + i + 1)
                    if i >= 2:
                        dve.wait_ge(at_exp, SB + i - 1)
                    dve.tensor_tensor(s_masked[i % 2][:, 0:w], s_scores(i, w), K(f"see{qt}"), ALU.add).then_inc(s_max, 1)
                    dve.wait_ge(s_max, i + 1)
                    link(dve.tensor_reduce(s_small[:, 0, i:i + 1], s_masked[i % 2][:, 0:w], AX, ALU.max))
                    dve.tensor_scalar(s_small[:, 1, i:i + 1], s_small[:, 0, i:i + 1], -0.125, None, ALU.mult)\
                        .then_inc(at_max, 1)
                if i >= 1:
                    w = 3 * (S_UNITS[i - 1][0] + 1) * P
                    dve.wait_ge(at_exp, SB + i)
                    link(dve.reciprocal(s_small[:, 3, i - 1:i], s_small[:, 2, i - 1:i]))
                    pr = s_probs[(i - 1) % 2][:, 0:w]
                    dve.tensor_scalar(pr, pr, s_small[:, 3, i - 1:i], None, ALU.mult).then_inc(at_p, 1)
            dve.wait_ge(at_o, SB + n)
            dve.tensor_copy(attnT.rearrange("p m (q t) -> p q m t", q=2),
                            ps[:, 0, :].rearrange("p (q m t) -> p q m t", q=2, m=2))

        GROUPS = KT // 2
        (rw_log, rw_exp, rw_kk, rw_sq, rw_ss, rw_mx, rw_rt, rw_rk, rw_bon, rw_b, rw_lora) = (
            sem(f"rw_{x}") for x in ("log", "exp", "kk", "sq", "ss", "mx", "rt", "rk", "bonus", "b", "lora"))
        (rw_tr, rw_taken, rw_gram, rw_gm, rw_aab, rw_T0, rw_X, rw_P, rw_Pc, rw_U, rw_T, rw_f, rw_fc, rw_z) = (
            sem(f"rw_{x}") for x in ("turned", "taken", "gram", "masked", "aab", "t0", "x", "p", "p_sb", "tp", "t", "f",
                                     "f_sb", "z"))
        (rs_u, rs_U, rs_s, rs_st, rs_y, gn_c, gn_sq, gn_ss, gn_rt, gn_n, gn_t) = (
            sem(f"rs_{x}") for x in ("u", "u_sb", "s", "state", "y", "centred", "sq", "ss", "rt", "normed", "turned"))
        a = Area(second_free)
        pair = lambda: a(2 * T).rearrange("p (j t) -> p j t", j=2)
        g_gate, g_bonus, g_eW = pair(), pair(), pair()
        g_ar = a(4 * T).rearrange("p (j x t) -> p j x t", j=2, x=2)
        g_kt, g_bt = pair(), pair()
        g_at, g_kh, g_bh, g_v = (a(2 * T).rearrange("p (q d) -> p q d", d=HD) for _ in range(4))
        later = a.at
        g_gm = a(8 * 4 * CHUNK).rearrange("p (q x) -> p q x", q=8)
        g_T = a(8 * 2 * CHUNK).rearrange("p (q x t) -> p q x t", q=8, x=2)
        g_X = a((LEVELS - 1) * 8 * CHUNK).rearrange("p (l q t) -> p l q t", l=LEVELS - 1, q=8)
        g_P, g_F, g_Z = (a(8 * CHUNK).rearrange("p (q t) -> p q t", q=8) for _ in range(3))
        g_TA = a(8 * CHUNK).rearrange("p (j c t) -> p j c t", j=2, c=4)
        g_y = a(8 * CHUNK).rearrange("p (q t) -> p q t", q=8)
        g_st = a(2 * 2 * HD).rearrange("p (b j v) -> p b j v", b=2, j=2)
        g_small = a(32).rearrange("p (k n) -> p k n", k=4)
        a = Area(later)
        e_sg, e_ai, e_ls, e_lp, e_le, e_eWp, e_eWi, e_eWe, e_kk, e_rn, e_b, e_kh, e_bh = (pair() for _ in range(13))
        e_sh = a(4 * T).rearrange("p (m t) -> p m t", t=T)
        e_shp = e_kh

        def shift(eng, lk, tile, n, buf, rows=P):
            z, d = rproj[0:rows, tile:tile + n, :], buf[0:rows, 0:n, :]
            eng.tensor_tensor(d[:, :, 1:T], z[:, :, 0:T - 1], z[:, :, 1:T], ALU.subtract)
            lk(eng.tensor_scalar(d[:, :, 0:1], z[:, :, 0:1], -1.0, None, ALU.mult))
            lk(eng.tensor_tensor(d, d, C("mu", tile, n, slice(0, rows)).unsqueeze(2).broadcast_to([rows, n, T]), ALU.mult))
            lk(eng.tensor_tensor(z, z, d, ALU.add))

        def per_tile(name, g):
            return C(name, 2 * g, 2).unsqueeze(2).broadcast_to([P, 2, T])

        def unit_of(q):
            return q // 4, (q // 2) % 2, q % 2

        def pe_rwkv(pe):
            meet["pe"]()
            meet["pe"]()
            for g in range(GROUPS):
                for j in range(2):
                    m = (2 * g + j) * P
                    o = j * T
                    pe.matmul(ps[:, 4, o:o + T], K("wa2")[0:64, m:m + P], rproj[0:64, RL, :], start=True, stop=True)
                    pe.matmul(ps[:, 5, o:o + T], K("wa2")[64:P, m:m + P], rproj[64:P, RL, :], start=True, stop=True)
                    pe.matmul(ps[:, 6, o:o + T], K("g2a")[:, m:m + P], rproj[:, RL + 1, :], start=True, stop=False)
                    mm = pe.matmul(ps[:, 6, o:o + T], K("g2b")[0:32, m:m + P], rproj[0:32, RL + 2, :],
                                   start=False, stop=True)
                mm.then_inc(rw_lora, 1)
                meet["pe"]()
                pe.wait_ge(rw_sq, g + 1)
                pe.matmul(ps[:, 7, :], K("blockones"), e_rn.rearrange("p j t -> p (j t)"), start=True, stop=True)\
                    .then_inc(rw_ss, 1)
                pe_gate(pe, 2 * g)
                pe.wait_ge(rw_rk, g + 1)
                pe.matmul(ps[:, 3, :], K("blockones"), e_le.rearrange("p j t -> p (j t)"), start=True, stop=True)\
                    .then_inc(rw_bon, 1)
                meet["pe"]()
                for bank, src in enumerate((None, e_kh, e_bh, rproj[:, RV + 2 * g:RV + 2 * g + 2, :])):
                    for tt in range(2):
                        for j in range(2):
                            x = (g_ar[:, j, 0] if src is None else src[:, j])[:, tt * P:(tt + 1) * P]
                            mm = pe.transpose(ps[:, bank, (2 * tt + j) * P:(2 * tt + j + 1) * P], x, K("ident"))
                    mm.then_inc(rw_tr, 1)
                for q in range(8):
                    tt, j, hb = unit_of(q)
                    b = 64 * hb
                    for p in range(2):
                        c = 2 * tt + p
                        o = j * 256
                        rows = slice(64 * p, 64 * p + 64)
                        rhs = g_ar[b:b + 64, j, :, c * 64:c * 64 + 64]
                        pe.matmul(ps[rows, 4 + 2 * hb + tt, o:o + 128], g_kt[b:b + 64, j, c * 64:c * 64 + 64], rhs,
                                  start=True, stop=True, skip_group_check=True)
                        mm = pe.matmul(ps[rows, 4 + 2 * hb + tt, o + 128:o + 256], g_bt[b:b + 64, j, c * 64:c * 64 + 64], rhs,
                                       start=True, stop=True, skip_group_check=True)
                mm.then_inc(rw_gram, 1)
                pe.wait_ge(rw_taken, g + 1)
                for q in range(8):
                    tt, j, hb = unit_of(q)
                    b = 64 * hb
                    for p in range(2):
                        c = 2 * tt + p
                        o = (q // 2) * 64
                        mm = pe.matmul(ps[64 * p:64 * p + 64, 2 * hb, o:o + 64], g_ar[b:b + 64, j, 0, c * 64:c * 64 + 64],
                                       g_bt[b:b + 64, j, c * 64:c * 64 + 64], start=True, stop=True, skip_group_check=True)
                mm.then_inc(rw_aab, 1)
                meet["pe"]()
                for l in range(LEVELS - 1):
                    for half in range(2):
                        n = (g * (LEVELS - 1) + l) * 2 + half
                        if l >= 1:
                            pe.wait_ge(rw_T, n - 1)
                        for q in range(4 * half, 4 * half + 4):
                            for p in range(2):
                                rows = slice(64 * p, 64 * p + 64)
                                mm = pe.matmul(ps[rows, 4 + half, (q % 4) * 64:(q % 4) * 64 + 64], g_X[rows, l, q, :], g_T[rows, q, 0, :],
                                               start=True, stop=True, skip_group_check=True)
                        mm.then_inc(rw_P, 1)
                    for half in range(2):
                        n = (g * (LEVELS - 1) + l) * 2 + half
                        pe.wait_ge(rw_Pc, n + 1)
                        for q in range(4 * half, 4 * half + 4):
                            o = (q % 4) * 128
                            for p in range(2):
                                rows = slice(64 * p, 64 * p + 64)
                                pe.matmul(ps[rows, 6 + half, o:o + 64], g_T[rows, q, 1, :], g_P[rows, q, :],
                                          start=True, stop=True, skip_group_check=True)
                                mm = pe.matmul(ps[rows, 6 + half, o + 64:o + 128], g_P[rows, q, :], g_T[rows, q, 1, :],
                                               start=True, stop=True, skip_group_check=True)
                        mm.then_inc(rw_U, 1)
                for q in range(8):
                    for p in range(2):
                        rows = slice(64 * p, 64 * p + 64)
                        mm = pe.matmul(ps[rows, 0, q * 64:q * 64 + 64], g_gm[rows, q, 0:64], g_v[rows, q, :],
                                       start=True, stop=True, skip_group_check=True)
                mm.then_inc(rw_f, 1)
                pe.wait_ge(rw_T, (g + 1) * (LEVELS - 1) * 2)
                for q in range(8):
                    tt, j, hb = unit_of(q)
                    for p in range(2):
                        rows = slice(64 * p, 64 * p + 64)
                        o = (2 * j + tt) * 64
                        pe.matmul(ps[64 * hb:64 * hb + 64, 2 + p, o:o + 64], g_at[rows, q, :], g_T[rows, q, 1, :],
                                  start=True, stop=True, skip_group_check=True)
                pe.wait_ge(rw_fc, g + 1)
                for q in range(8):
                    for p in range(2):
                        rows = slice(64 * p, 64 * p + 64)
                        mm = pe.matmul(ps[rows, 1, q * 64:q * 64 + 64], g_T[rows, q, 1, :], g_F[rows, q, :],
                                       start=True, stop=True, skip_group_check=True)
                mm.then_inc(rw_z, 1)
                meet["pe"]()
                for c in range(4):
                    tt, p = c // 2, c % 2
                    rows = slice(64 * p, 64 * p + 64)
                    heads = [(4 * tt + x, x // 2, 64 * (x % 2)) for x in range(4)]
                    st = g_st[:, c % 2]
                    if c:
                        pe.wait_ge(rs_st, 3 * g + c)
                        for q, j, b in heads:
                            mm = pe.matmul(ps[rows, 7 if b else 3, j * 64:j * 64 + 64],
                                           g_TA[b:b + 64, j, c, :], st[b:b + 64, j, :], start=True, stop=True,
                                           skip_group_check=True)
                        mm.then_inc(rs_u, 1)
                        pe.wait_ge(rs_U, 3 * g + c)
                    if c < 3:
                        for q, j, b in heads:
                            o = (c % 2) * 128 + j * 64
                            pe.matmul(ps[b:b + 64, 4, o:o + 64], g_kh[rows, q, :], g_v[rows, q, :], start=True, stop=False,
                                      skip_group_check=True)
                            mm = pe.matmul(ps[b:b + 64, 4, o:o + 64], g_bh[rows, q, :], g_Z[rows, q, :], start=False,
                                           stop=True, skip_group_check=True)
                        mm.then_inc(rs_s, 1)
                    for q, j, b in heads:
                        o = ps[rows, 5, q * 64:q * 64 + 64]
                        pe.matmul(o, g_gm[rows, q, 64:128], g_v[rows, q, :], start=True, stop=False, skip_group_check=True)
                        pe.matmul(o, g_gm[rows, q, 192:256], g_Z[rows, q, :], start=False, stop=True, skip_group_check=True)
                        mm = pe.matmul(ps[rows, 0 if b else 6, (q // 2) * 64:(q // 2) * 64 + 64],
                                       g_ar[b:b + 64, j, 1, c * 64:c * 64 + 64], st[b:b + 64, j, :], start=True, stop=True,
                                       skip_group_check=True)
                mm.then_inc(rs_y, 1)
                pe_gate(pe, 2 * g + 1)
                pe.wait_ge(gn_n, g + 1)
                for tt in range(2):
                    for j in range(2):
                        mm = pe.transpose(ps[:, 6, j * T + tt * P:j * T + (tt + 1) * P],
                                          g_y[:, 4 * tt + 2 * j:4 * tt + 2 * j + 2, :].rearrange("p q t -> p (q t)"),
                                          K("ident"))
                mm.then_inc(gn_t, 1)
                meet["pe"]()

        def act_rwkv(act):
            meet["act"]()
            act.activation(rproj[0:64, RL, :], rproj[0:64, RL, :], ACT.Tanh)
            act.activation(rproj[:, RL + 1, :], rproj[:, RL + 1, :], ACT.Sigmoid)
            act.activation(rproj[0:32, RL + 2, :], rproj[0:32, RL + 2, :], ACT.Sigmoid)
            meet["act"]()
            for g in range(GROUPS):
                act.wait_ge(rw_lora, g + 1)
                for j in range(2):
                    act.activation(e_sg[:, j, :], ps[:, 4, j * T:(j + 1) * T], ACT.Sigmoid, bias=C("w0", 2 * g + j))
                    act.activation(e_ai[:, j, :], ps[:, 5, j * T:(j + 1) * T], ACT.Sigmoid, bias=C("a0", 2 * g + j))
                act.activation(g_gate, two(ps[:, 6, :]), ACT.Copy)
                meet["act"]()
                act.wait_ge(rw_kk, g + 1)
                act.activation(e_rn, e_kk, ACT.Square).then_inc(rw_sq, 1)
                act.wait_ge(rw_log, g + 1)
                act.activation(g_eW, e_ls, ACT.Exp, scale=-DECAY)
                act.activation(e_eWp, e_lp, ACT.Exp, scale=-DECAY)
                act.activation(e_eWi, e_ls, ACT.Exp, scale=DECAY)
                act.activation(e_eWe, e_le, ACT.Exp, scale=-DECAY).then_inc(rw_exp, 1)
                act.wait_ge(rw_mx, g + 1)
                act.activation(e_rn, e_rn, ACT.Sqrt).then_inc(rw_rt, 1)
                act_gate(act, 2 * g)
                meet["act"]()
                act.wait_ge(rw_tr, 4 * g + 1)
                act.activation(g_at, ps[:, 0, :].rearrange("p (q d) -> p q d", d=HD), ACT.Copy)
                act.wait_ge(rw_tr, 4 * g + 3)
                act.activation(g_bh, ps[:, 2, :].rearrange("p (q d) -> p q d", d=HD), ACT.Copy).then_inc(rw_taken, 1)
                act.wait_ge(rw_tr, 4 * g + 4)
                act.activation(g_v, ps[:, 3, :].rearrange("p (q d) -> p q d", d=HD), ACT.Copy)
                meet["act"]()
                for l in range(LEVELS - 1):
                    for half in range(2):
                        n = (g * (LEVELS - 1) + l) * 2 + half
                        act.wait_ge(rw_P, n + 1)
                        act.activation(g_P[:, 4 * half:4 * half + 4, :],
                                       ps[:, 4 + half, 0:256].rearrange("p (q t) -> p q t", q=4), ACT.Copy)\
                            .then_inc(rw_Pc, 1)
                act.wait_ge(rw_f, g + 1)
                act.activation(g_F, ps[:, 0, :].rearrange("p (q t) -> p q t", q=8), ACT.Copy).then_inc(rw_fc, 1)
                act.wait_ge(rw_z, g + 1)
                for p in range(2):
                    act.activation(g_TA[:, :, p::2, :], ps[:, 2 + p, 0:256].rearrange("p (j c t) -> p j c t", j=2, c=2), ACT.Copy)
                meet["act"]()
                act.wait_ge(gn_c, g + 1)
                act.activation(g_F, g_y, ACT.Square, scale=0.125).then_inc(gn_sq, 1)
                act.wait_ge(gn_ss, g + 1)
                act.activation(g_small[:, 3, :], g_small[:, 2, :], ACT.Sqrt, bias=eps_col[:, 1:2]).then_inc(gn_rt, 1)
                act_gate(act, 2 * g + 1)
                meet["act"]()

        def pool_rwkv(pool):
            meet["pool"]()
            meet["pool"]()
            for g in range(GROUPS):
                shift(pool, plink, RV + 2 * g, 2, e_shp)
                meet["pool"]()
                pool.wait_ge(rw_b, g + 1)
                pool.wait_ge(rw_exp, g + 1)
                pool.tensor_tensor(e_kh, rproj[:, RK + 2 * g:RK + 2 * g + 2, :], e_eWe, ALU.mult)
                pool.tensor_tensor(e_bh, e_b, e_eWe, ALU.mult)
                meet["pool"]()
                pool.wait_ge(rw_gm, g + 1)
                for l in range(1, LEVELS):
                    pool.tensor_tensor(g_X[:, l - 1], g_gm[:, :, 128:192],
                                       K("levT")[:, l * 64:(l + 1) * 64].unsqueeze(1).broadcast_to([P, 8, 64]), ALU.mult)
                meet["pool"]()
                meet["pool"]()
                meet["pool"]()

        def dve_rwkv(dve):
            shift(dve, link, RL, 2, e_sh)
            shift(dve, link, RL + 2, 1, e_sh, 32)
            meet["dve"]()
            meet["dve"]()
            for g in range(GROUPS):
                r, k, v = (rproj[:, x + 2 * g:x + 2 * g + 2, :] for x in (RR, RK, RV))
                shift(dve, link, RR + 2 * g, 2, e_sh)
                shift(dve, link, RK + 2 * g, 2, e_sh)
                meet["dve"]()
                dve.tensor_tensor(e_kk, k, per_tile("k_k", g), ALU.mult).then_inc(rw_kk, 1)
                flat = lambda x: x.rearrange("p j t -> p (j t)")
                link(dve.tensor_tensor_scan(flat(e_ls), K("reset"), flat(e_sg), 0.0, ALU.mult, ALU.add))
                dve.tensor_tensor(e_lp, e_ls, e_sg, ALU.subtract)
                chunks = lambda x: flat(x).rearrange("p (n t) -> p n t", t=CHUNK)
                dve.tensor_tensor(chunks(e_le), chunks(e_ls)[:, :, CHUNK - 1:CHUNK].broadcast_to([P, 8, CHUNK]), chunks(e_ls),
                                  ALU.subtract).then_inc(rw_log, 1)
                link(dve.scalar_tensor_tensor(out=e_b, in0=e_ai, scalar=-1.0, in1=per_tile("k_a", g), op0=ALU.add, op1=ALU.mult))
                link(dve.scalar_tensor_tensor(out=k, in0=e_b, scalar=1.0, in1=k, op0=ALU.add, op1=ALU.mult))
                dve.wait_ge(rw_ss, g + 1)
                dve.tensor_scalar(flat(e_rn), ps[:, 7, :], 1e-24, None, ALU.max).then_inc(rw_mx, 1)
                dve.wait_ge(rw_rt, g + 1)
                link(dve.reciprocal(e_rn, e_rn))
                link(dve.tensor_tensor(e_kk, e_kk, e_rn, ALU.mult))
                dve.tensor_tensor(e_b, e_kk, e_ai, ALU.mult).then_inc(rw_b, 1)
                dve.wait_ge(rw_b, g + 1)
                dve.wait_ge(rw_exp, g + 1)
                link(dve.tensor_tensor(e_lp, r, k, ALU.mult))
                dve.tensor_tensor(e_le, e_lp, per_tile("r_k", g), ALU.mult).then_inc(rw_rk, 1)
                dve.scalar_tensor_tensor(out=g_ar[:, :, 0, :], in0=e_kk, scalar=-1.0, in1=e_eWp, op0=ALU.mult, op1=ALU.mult)
                dve.tensor_tensor(g_ar[:, :, 1, :], r, g_eW, ALU.mult)
                dve.tensor_tensor(g_kt, k, e_eWi, ALU.mult)
                dve.tensor_tensor(g_bt, e_b, e_eWi, ALU.mult)
                dve.wait_ge(rw_bon, g + 1)
                link(dve.tensor_tensor(g_bonus, two(ps[:, 3, :]), v, ALU.mult))
                meet["dve"]()
                dve.wait_ge(rw_tr, 4 * g + 2)
                dve.tensor_copy(g_kh, ps[:, 1, :].rearrange("p (q d) -> p q d", d=HD))
                dve.wait_ge(rw_gram, g + 1)
                for x in range(4):
                    q0 = 4 * (x % 2) + x // 2
                    ins = dve.tensor_tensor(g_gm[:, q0:q0 + 3:2, :], ps[:, 4 + x, :].rearrange("p (q n) -> p q n", q=2),
                                            K("gram").unsqueeze(1).broadcast_to([P, 2, 256]), ALU.mult)
                ins.then_inc(rw_gm, 1)
                dve.wait_ge(rw_gm, g + 1)
                all8 = lambda m: m.unsqueeze(1).broadcast_to([P, 8, 64])
                link(dve.tensor_tensor(g_T[:, :, 1, :], g_gm[:, :, 128:192], all8(K("levT")[:, 0:64]), ALU.mult))
                link(dve.tensor_tensor(g_T[:, :, 1, :], g_T[:, :, 1, :], all8(K("eye64")), ALU.add))
                dve.wait_ge(rw_aab, g + 1)
                for hb in range(2):
                    ins = dve.tensor_tensor(g_T[:, hb::2, 0, :], ps[:, 2 * hb, 0:256].rearrange("p (q t) -> p q t", q=4),
                                            K("lev0").unsqueeze(1).broadcast_to([P, 4, 64]), ALU.mult)
                link(ins)
                dve.memset(g_st[:, 0], 0.0)
                link(dve.tensor_tensor(g_T[:, :, 0, :], g_T[:, :, 0, :], all8(K("eye64")), ALU.add))
                meet["dve"]()
                for l in range(LEVELS - 1):
                    for half in range(2):
                        n = (g * (LEVELS - 1) + l) * 2 + half
                        dve.wait_ge(rw_U, n + 1)
                        t = g_T[:, 4 * half:4 * half + 4].rearrange("p q x t -> p (q x t)")
                        dve.tensor_tensor(t, t, ps[:, 6 + half, :], ALU.add).then_inc(rw_T, 1)
                dve.wait_ge(rw_z, g + 1)
                dve.tensor_copy(g_Z, ps[:, 1, :].rearrange("p (q t) -> p q t", q=8))
                meet["dve"]()
                for c in range(4):
                    tt, p = c // 2, c % 2
                    rows = slice(64 * p, 64 * p + 64)
                    if c:
                        dve.wait_ge(rs_u, 3 * g + c)
                        for hb in range(2):
                            u = g_Z[rows, 4 * tt + hb:4 * tt + 4:2, :]
                            ins = dve.tensor_tensor(u, u, ps[rows, 3 + 4 * hb, 0:128].rearrange("p (q t) -> p q t", q=2), ALU.add)
                        ins.then_inc(rs_U, 1)
                    if c < 3:
                        dve.wait_ge(rs_s, 3 * g + c + 1)
                        new = g_st[:, (c + 1) % 2]
                        o = ps[:, 4, (c % 2) * 128:(c % 2) * 128 + 128].rearrange("p (j v) -> p j v", j=2)
                        if c == 0:
                            dve.tensor_copy(new, o).then_inc(rs_st, 1)
                        else:
                            wc = g_eW[:, :, c * CHUNK + CHUNK - 1:c * CHUNK + CHUNK].broadcast_to([P, 2, HD])
                            link(dve.tensor_tensor(g_st2, g_st[:, c % 2], wc, ALU.mult))
                            dve.tensor_tensor(new, g_st2, o, ALU.add).then_inc(rs_st, 1)
                        dve.wait_ge(rs_st, 3 * g + c + 1)
                dve.wait_ge(rs_y, g + 1)
                link(dve.tensor_copy(g_y, ps[:, 5, :].rearrange("p (q t) -> p q t", q=8)))
                for hb in range(2):
                    y = g_y[:, hb::2, :]
                    ins = dve.tensor_tensor(y, y, ps[:, 0 if hb else 6, 0:256].rearrange("p (q t) -> p q t", q=4), ALU.add)
                link(ins)
                link(dve.tensor_reduce(g_small[:, 0, :], g_y, AX, ALU.add))
                link(dve.tensor_scalar(g_small[:, 1, :], g_small[:, 0, :], -1.0 / HD, None, ALU.mult))
                dve.tensor_tensor(g_y, g_y, g_small[:, 1, :].unsqueeze(2).broadcast_to([P, 8, HD]), ALU.add).then_inc(gn_c, 1)
                dve.wait_ge(gn_sq, g + 1)
                dve.wait_ge(gn_c, g + 1)
                dve.tensor_reduce(g_small[:, 2, :], g_F, AX, ALU.add).then_inc(gn_ss, 1)
                dve.wait_ge(gn_rt, g + 1)
                link(dve.reciprocal(g_small[:, 3, :], g_small[:, 3, :]))
                dve.tensor_tensor(g_y, g_y, g_small[:, 3, :].unsqueeze(2).broadcast_to([P, 8, HD]), ALU.mult).then_inc(gn_n, 1)
                dve.wait_ge(gn_t, g + 1)
                for j in range(2):
                    m = 2 * g + j
                    ins = dve.tensor_scalar(yT[:, m, :], ps[:, 6, j * T:(j + 1) * T], C("ln_w", m), C("ln_b", m),
                                            ALU.mult, ALU.add)
                link(ins)
                y = yT[:, 2 * g:2 * g + 2, :]
                link(dve.tensor_tensor(y, y, g_bonus, ALU.add))
                link(dve.tensor_tensor(y, y, g_gate, ALU.mult))
                meet["dve"]()
                dve.drain().then_inc(dve_out, 2)

        g_st2 = g_P.rearrange("p q t -> p (q t)")[:, 0:128].rearrange("p (j v) -> p j v", j=2)

        y_gated = sem("y_gated")

        def pe_gate(pe, i):
            u = FIRST["gates"] + i
            j = u % SLOTS
            pe_unit_ready(pe, j, u)
            for m in range(2):
                for k in range(KT):
                    mm = pe.matmul(ps[:, 1 + i % 2, m * T:(m + 1) * T], ring[:, j, (m * KT + k) * P:(m * KT + k + 1) * P],
                                   hT[:, k, T:TA], start=(k == 0), stop=(k == KT - 1))
            mm.then_inc(unit_done, 1)

        def act_gate(act, i):
            act.wait_ge(unit_done, FIRST["gates"] + i + 1)
            for m, dst in enumerate((xT, hT)):
                ins = act.activation(dst[:, i, 0:T], ps[:, 1 + i % 2, m * T:(m + 1) * T], ACT.Sigmoid,
                                     bias=C("gate_bias", i + 8 * m))
            ins.then_inc(act_out, 1)

        def pool_merge(pool):
            pool.wait_ge(act_out, FIRST["attn_up"] + 2)
            pool.wait_ge(dve_out, FIRST["attn_up"] + 2)
            pool.tensor_tensor(ya, ya, xT[:, :, 0:T], ALU.mult).then_inc(y_gated, 1)

        def dve_merge(dve):
            dve.wait_ge(act_out, FIRST["rwkv_out"] + 4)
            dve.wait_ge(dve_out, FIRST["rwkv_out"] + 4)
            link(dve.tensor_tensor(yr, yr, hT[:, :, 0:T], ALU.mult))
            dve.wait_ge(y_gated, 1)
            dve.tensor_tensor(merged, ya, yr, ALU.add)

        def gate_of(layer, part):
            def gates(m, c0):
                return [(lo, hi, mod[layer][:, bass.ds(m + part * KT, 1), s:s + 1].rearrange("p a b -> p (a b)"))
                        for s in range(2) for lo, hi in [(s * T - c0, s * T - c0 + T)] if lo >= 0]
            return lambda c0: (lambda m: gates(m, c0))

        half = lambda m: [(0, T, 0.5)]
        whole = lambda m: [(0, T, 1.0)]

        def scale_of(layer, i, c0):
            return lambda m: segments(c0, None, lambda s: scl[layer][:, i, m, s:s + 1])

        def shift_of(layer, part, c0):
            return lambda m: segments(c0, None, lambda s: mod[layer][:, part * KT + m, s:s + 1])

        def plain(name):
            return lambda m: [(0, T, C(name, m))]

        block = ctx.enter_context(nc.Block())

        @block.tensor
        def _(pe):
            meet["pe"] = Meet(pe, "pe")
            pe.wait_ge(params_in, 48)
            for layer in range(DEPTH):
                c0, n = unit_tokens(layer, False)
                if layer == 0:
                    meet["pe"]()
                    pe_ada(pe)
                    meet["pe"]()
                pe_norm(pe, 2 * layer, 0, TA)
                meet["pe"]()
                pe_project(pe, layer)
                meet["pe"]()
                pe_mlstm(pe, layer)
                meet["pe"]()
                pe_pool(pe, layer)
                meet["pe"]()
                pe_qk(pe, layer)
                meet["pe"]()
                pe_attention(pe, layer)
                meet["pe"]()
                pe_feature_tiles(pe, f"out{layer}", 2, mixT, c0, n)
                meet["pe"]()
                pe_norm(pe, 2 * layer + 1, c0, n)
                meet["pe"]()
                pe_ffn(pe, layer, c0, n)
                meet["pe"]()
            pe_norm(pe, 4, T, T)
            meet["pe"]()
            pe_norm(pe, 5, T, T)
            meet["pe"]()
            pe_ffn(pe, 2, T, T)
            meet["pe"]()
            pe_norm(pe, 6, T, T)
            meet["pe"]()
            pe_feature_tiles(pe, "qk", 3, hT, T, T)
            pe_values(pe)
            meet["pe"]()
            pe.wait_ge(second_in, 16)
            pe_rope(pe)
            meet["pe"]()
            pe_dilated(pe)
            meet["pe"]()
            pe_feature_tiles(pe, "rkv", 3, hT, T, T)
            pe_lora(pe)
            meet["pe"]()
            pe_rwkv(pe)
            pe_feature_tiles(pe, "attn_up", 4, attnT, 0, T, kt=2)
            pe_feature_tiles(pe, "rwkv_out", 2, yT, 0, T, per_bank=1)
            meet["pe"]()
            pe_feature_tiles(pe, "w_o", 2, merged, 0, T)
            meet["pe"]()
            pe_norm(pe, 7, T, T)
            meet["pe"]()
            pe_ffn(pe, 3, T, T)
            meet["pe"]()
            pe_norm(pe, 8, T, T)
            meet["pe"]()

        @block.scalar
        def _(act):
            meet["act"] = Meet(act, "act")
            links["act"] = Chain(act, chains["act"])
            act.wait_ge(params_in, 48)
            for layer in range(DEPTH):
                c0, n = unit_tokens(layer, False)
                if layer == 0:
                    act.activation(cond[:, :, 0:2], C("cond", 0, 16).rearrange("p (k s) -> p k s", s=2), ACT.Silu)
                    meet["act"]()
                    copy_rows(act, act_copy(act), act_out, 0)
                    meet["act"]()
                act_norm(act, 2 * layer, 0, TA)
                meet["act"]()
                evacuate_project(act, act_copy(act), act_out, layer, 0, act_gate_rows)
                meet["act"]()
                act_mlstm(act, layer)
                meet["act"]()
                meet["act"]()
                act_qk(act, layer)
                meet["act"]()
                act_attention(act, layer)
                meet["act"]()
                act_residual(act, f"out{layer}", n, gate_of(layer, 2)(c0), 2)
                meet["act"]()
                act_norm(act, 2 * layer + 1, c0, n)
                meet["act"]()
                act_ffn(act, layer, c0, n, gate_of(layer, 5)(c0))
                meet["act"]()
            act.dma_start(const[:, COMMON_N:COMMON_N + TWO_N], dram["const2"]).then_inc(second_in, 16)
            act_norm(act, 4, T, T)
            meet["act"]()
            act_norm(act, 5, T, T)
            meet["act"]()
            act_ffn(act, 2, T, T, half)
            meet["act"]()
            act_norm(act, 6, T, T)
            meet["act"]()
            copy_out(act, act_copy(act), act_out, "qk", three_tiles(qkT, 0))
            copy_out(act, act_copy(act), act_out, "v", value_halves(0))
            meet["act"]()
            meet["act"]()
            act_dilated(act)
            meet["act"]()
            copy_out(act, act_copy(act), act_out, "rkv", three_tiles(rproj, 0))
            copy_out(act, act_copy(act), act_out, "lora", lora_tiles(0))
            meet["act"]()
            act_rwkv(act)
            copy_out(act, act_copy(act), act_out, "attn_up", bank_each(ya, 0, 2))
            copy_out(act, act_copy(act), act_out, "rwkv_out", bank_each(yr, 0, 1))
            meet["act"]()
            act_residual(act, "w_o", T, whole, 2)
            meet["act"]()
            act_norm(act, 7, T, T)
            meet["act"]()
            act_ffn(act, 3, T, T, half)
            meet["act"]()
            act_norm(act, 8, T, T)
            meet["act"]()

        @block.vector
        def _(dve):
            meet["dve"] = Meet(dve, "dve")
            links["dve"] = Chain(dve, chains["dve"])
            dve.memset(eps_col[:, 0:1], EPS)
            dve.memset(eps_col[:, 1:2], GN_EPS)
            copy = lambda o, s: dve.tensor_copy(o, s)
            for layer in range(DEPTH):
                c0, n = unit_tokens(layer, False)
                if layer == 0:
                    dve.memset(cond[:, :, 2:32], 0.0)
                    dve.wait_ge(params_in, 48)
                    meet["dve"]()
                    copy_rows(dve, copy, dve_out, 1)
                    meet["dve"]()
                    dve_mod(dve, 0, True, 4, 0)
                dve_norm(dve, 2 * layer, 0, TA, hT, scale_of(layer, 0, 0), shift_of(layer, 0, 0))
                meet["dve"]()
                evacuate_project(dve, copy, dve_out, layer, 1, dve_gate_rows)
                meet["dve"]()
                dve_mlstm(dve, layer)
                meet["dve"]()
                dve_pool(dve, layer)
                meet["dve"]()
                dve_qk(dve, layer)
                meet["dve"]()
                dve_attention(dve, layer)
                meet["dve"]()
                dve_residual(dve, f"out{layer}", c0, n, 2)
                meet["dve"]()
                dve_norm(dve, 2 * layer + 1, c0, n, hT, scale_of(layer, 1, c0), shift_of(layer, 3, c0))
                meet["dve"]()
                dve_ffn(dve, layer, c0, n)
                meet["dve"]()
            dve_norm(dve, 4, T, T, xT, plain("final_norm"), None)
            meet["dve"]()
            dve_norm(dve, 5, T, T, hT, plain("ffn1_norm"), None)
            meet["dve"]()
            dve_ffn(dve, 2, T, T)
            meet["dve"]()
            dve_norm(dve, 6, T, T, hT, plain("mix_norm"), None)
            meet["dve"]()
            copy_out(dve, copy, dve_out, "qk", three_tiles(qkT, 1))
            copy_out(dve, copy, dve_out, "v", value_halves(1))
            meet["dve"]()
            dve.wait_ge(second_in, 16)
            dve_rope(dve)
            meet["dve"]()
            dve_dilated(dve)
            meet["dve"]()
            copy_out(dve, copy, dve_out, "rkv", three_tiles(rproj, 1))
            copy_out(dve, copy, dve_out, "lora", lora_tiles(1))
            meet["dve"]()
            dve_rwkv(dve)
            copy_out(dve, copy, dve_out, "attn_up", bank_each(ya, 1, 2))
            copy_out(dve, copy, dve_out, "rwkv_out", bank_each(yr, 1, 1))
            dve_merge(dve)
            meet["dve"]()
            dve_residual(dve, "w_o", T, T, 2)
            meet["dve"]()
            dve_norm(dve, 7, T, T, hT, plain("ffn2_norm"), None)
            meet["dve"]()
            dve_ffn(dve, 3, T, T)
            meet["dve"]()
            dve_norm(dve, 8, T, T, hT, plain("final_norm_2"), None)
            meet["dve"]()

        @block.gpsimd
        def _(pool):
            meet["pool"] = Meet(pool, "pool")
            links["pool"] = Chain(pool, chains["pool"])
            pool.wait_ge(params_in, 48)
            for layer in range(DEPTH):
                for _ in range(2 if layer else 4):
                    meet["pool"]()
                pool_mlstm(pool, layer)
                meet["pool"]()
                meet["pool"]()
                pool_qk(pool, layer)
                for _ in range(6):
                    meet["pool"]()
            for _ in range(5):
                meet["pool"]()
            meet["pool"]()
            pool.wait_ge(second_in, 16)
            pool_rope(pool)
            meet["pool"]()
            meet["pool"]()
            meet["pool"]()
            pool_rwkv(pool)
            pool_merge(pool)
            for _ in range(6):
                meet["pool"]()

        @block.sync
        def _(sp):
            sp.dma_start(par[:, :], dram["par"]).then_inc(params_in, 16)
            sp.dma_start(const[:, 0:COMMON_N + ONE_N], dram["const"]).then_inc(params_in, 16)
            sp.dma_start(xT[:, :, :].rearrange("p k t -> p (k t)"), dram["x"]).then_inc(params_in, 16)
            load_weights(sp)
            sp.wait_ge(met["dve"], meet["dve"].n)
            sp.dma_start(out, hT[:, :, T:TA]).then_inc(stored, 16)
            sp.wait_ge(stored, 16)
        assert len({m.n for m in meet.values()}) == 1, {k: m.n for k, m in meet.items()}


def feature_columns(v):
    return np.asarray(v).reshape(-1, P).T


def tiles(w, cols):
    k, m = w.shape
    return w.reshape(k // P, P, m // cols, cols).transpose(2, 1, 0, 3).reshape(m // cols, P, -1)


def joined(t, n):
    u = t.shape[0] // n
    return t.reshape(u, n, P, -1).transpose(0, 2, 1, 3).reshape(u, P, -1)


def layout(i):
    i = {k: np.asarray(v) for k, v in i.items()}
    w = {}
    heads = [h for j in range(4) for h in (j, 4 + j)]
    for l in range(DEPTH):
        ada = tiles(i["w_ada"][l], ADA_COLS)
        w[f"ada{l}a"], w[f"ada{l}b"] = ada[:ADA_FIRST], ada[ADA_FIRST:]
        offs = np.cumsum([0, 512, 128, 128, 256, 256, 256, 256, 16, 256])
        aq, ak, av, mq, mk, mv, mo, mg, pp = (i["w_in"][l][:, a:b] for a, b in zip(offs[:-1], offs[1:]))
        aq = aq.reshape(D, 8, HD)[:, heads].reshape(D, 512)
        fm = tiles(np.concatenate([aq[:, :256], mk, aq[:, 256:], mq, mo, ak, np.zeros_like(ak)], 1), P)
        w[f"fm{l}"] = joined(fm, 2)
        w[f"tma{l}"] = tiles(np.concatenate([mv, mg], 1), 272)
        w[f"tmb{l}"] = tiles(np.concatenate([av, pp], 1), 384)
        wo = i["w_out"][l]
        wo = np.concatenate([wo[:512].reshape(8, HD, D)[heads].reshape(512, D), wo[512:]], 0)
        w[f"out{l}"] = joined(tiles(wo, P), 2)
        for r, g, u, d in ((l, i["w_ffn_gate"][l], i["w_ffn_up"][l], i["w_ffn_down"][l]),
                           (2 + l, *(i[f"ffn{1 + l}_w_{x}_2"][0] for x in ("gate", "up", "down")))):
            w[f"up{r}"] = np.concatenate([tiles(g, P), tiles(u, P)], 2)
            w[f"down{r}"] = tiles(d, P)
    w2 = i["w_in_2"][0]
    w["qk"] = joined(tiles(w2[:, :1536], P), 3)
    w["v"] = tiles(w2[:, 1536:2304], 384)
    w["rkv"] = joined(tiles(w2[:, 2304:2304 + 3072], P), 3)
    w["lora"] = tiles(w2[:, 5376:5664], 288)
    w["attn_up"] = joined(tiles(i["attn_w_up_2"][0], P), 4)
    w["rwkv_out"] = joined(tiles(i["rwkv_w_out_2"][0], P), 2)
    gt = tiles(w2[:, 5664:], P)
    w["gates"] = np.concatenate([gt[:8], gt[8:]], 2)
    w["w_o"] = joined(tiles(i["w_o_2"][0], P), 2)

    par = np.zeros((P, PAR_N), np.float32)

    def put(name, v, rows=slice(0, P)):
        at, n = PAR_AT[name]
        par[rows, at:at + n] = v
    for l in range(DEPTH):
        for name in ("norm_mix", "norm_ffn", "b_ada", "ml_norm", "pool_scale"):
            put(f"{name}{l}", feature_columns(i[name][l]))
        for name in ("q_norm", "k_norm"):
            put(f"{name}{l}", np.tile(i[name][l], 2)[:, None])
        put(f"b_gates{l}", i["b_gates"][l].reshape(4, 4).T, slice(0, 4))
        put(f"pool_w{l}", i["pool_w"][l].reshape(2, 2, HD, HD).transpose(1, 2, 0, 3).reshape(P, -1))
    put("final_norm", feature_columns(i["final_norm"]))
    put("final_norm_2", feature_columns(i["final_norm_2"]))
    for name in ("ffn1_norm", "mix_norm", "ffn2_norm", "gate_bias"):
        put(name, feature_columns(i[name + "_2"][0]))
    mu = np.concatenate([i["rwkv_mu_2"][0], np.zeros(R_TILES * P - 3360, np.float32)])
    put("mu", feature_columns(mu))
    for name in ("w0", "a0", "k_k", "k_a", "r_k", "ln_w", "ln_b"):
        put(name, feature_columns(i[f"rwkv_{name}_2"][0].reshape(-1)))
    put("cond", np.stack([feature_columns(i["c_ctx"]), feature_columns(i["c"][0])], 2).reshape(P, -1))
    x = np.concatenate([i["ctx"][0], i["x"][0]], 0)
    x = x.reshape(TA, KT, P).transpose(2, 1, 0).reshape(P, -1)
    wa2 = np.concatenate([i["rwkv_w2_2"][0], i["rwkv_a2_2"][0]], 0)
    g2 = i["rwkv_g2_2"][0]
    g2b = np.concatenate([g2[P:], np.zeros((2 * P - len(g2), D), np.float32)], 0)
    const = np.concatenate([CONSTS[k] for k in COMMON + BLOCK1], 1)
    const2 = np.concatenate([CONSTS[k] for k in BLOCK2] + [wa2, g2[:P], g2b], 1)
    return {"par": par, "const": const, "const2": const2, "x": x, **{f"w_{k}": v for k, v in w.items()}}


def kernel(**inputs):
    import concourse.bacc as bacc
    from concourse.bass_utils import run_bass_kernel_spmd

    nc = bacc.Bacc("TRN2", target_bir_lowering=False, num_devices=1)
    arrays, dram = {}, {}
    for name, a in layout(inputs).items():
        arrays[f"{name}_dram"] = a = np.ascontiguousarray(a, dtype=np.float32)
        dram[name] = nc.dram_tensor(f"{name}_dram", a.shape, F32, kind="ExternalInput").ap()
    out = nc.dram_tensor("out_dram", (P, KT, T), F32, kind="ExternalOutput").ap()
    build(nc, dram, out)
    r = run_bass_kernel_spmd(nc, [arrays], core_ids=[0])
    y = r.results[0]["out_dram"]
    return np.ascontiguousarray(y.transpose(2, 1, 0).reshape(1, T, D))
```

```python
from contextlib import ExitStack

import numpy as np
import concourse.bass as bass
from concourse import mybir

F32 = mybir.dt.float32
F32R = mybir.dt.float32r
ALU = mybir.AluOpType
ACT = mybir.ActivationFunctionType
AX = mybir.AxisListType.X

P = 128
D = 1024
KT = D // P
T = 256
TA = 2 * T
HD = 64
DEPTH = 2
FF = 2816
FT = FF // P
ADA_UNITS, ADA_COLS = 16, 384
ADA_FIRST = -(-2 * D // ADA_COLS)
ADA_TILES = ADA_FIRST * ADA_COLS // P
SLOTS, SLOT = 4, 3072
EPS = 1e-6
GN_EPS = 64e-5
POOL_WINDOWS = (2, 4, 8, 16)
GRID_W = 64
CHUNK = 64
DECAY = float(np.exp(-0.5))
LEVELS = 6

AQ, MQ, MO, MK, AK, FM_TILES = 0, 4, 6, 8, 10, 11
MV, MG, AV, PP, TM = 0, 256, 272, 400, 656
RR, RK, RV, RL, R_TILES = 0, 8, 16, 24, 27


def constant_table():
    c = {}
    i = np.arange(P)
    c["ident"] = np.eye(P)
    c["ones"] = np.ones((P, P))
    c["blockones"] = (i[:, None] // HD == i[None] // HD) * 1.0
    rot = np.zeros((P, P))
    for o in range(P):
        if o % 32 < 16:
            rot[o + 16, o] = -1
        else:
            rot[o - 16, o] = 1
    c["rot1"] = rot
    rot = np.zeros((P, P))
    for o in range(P):
        d = o % HD
        if d < 8:
            rot[o + 8, o] = -1
        elif d < 16:
            rot[o - 8, o] = 1
    c["rot2"] = rot
    half = HD // 2
    f32 = np.float32
    inv = (1.0 / (f32(10000.0) ** (np.arange(0, half, 2, dtype=f32) / f32(half)))).astype(f32)
    row = np.repeat(np.arange(T // GRID_W, dtype=f32), GRID_W)
    col = np.tile(np.arange(GRID_W, dtype=f32), T // GRID_W)
    ar, ac = row[:, None] * inv, col[:, None] * inv
    ang = np.concatenate([ar, ar, ac, ac], 1).astype(f32)
    cos1, sin1 = np.ones((P, TA)), np.zeros((P, TA))
    cos1[:, T:] = np.tile(np.cos(ang).T, (2, 1))
    sin1[:, T:] = np.tile(np.sin(ang).T, (2, 1))
    c["cos1"], c["sin1"] = cos1, sin1
    inv2 = np.power(f32(500000.0), -np.arange(8, dtype=f32) * f32(2.0 / 16)).astype(f32)
    a2 = (np.arange(T, dtype=f32)[:, None] * inv2[None]).astype(f32)
    cos2, sin2 = np.ones((HD, T)), np.zeros((HD, T))
    cos2[0:16] = np.tile(np.cos(a2).T, (2, 1))
    sin2[0:16] = np.tile(np.sin(a2).T, (2, 1))
    c["cos2"], c["sin2"] = np.tile(cos2, (2, 1)), np.tile(sin2, (2, 1))
    c["tri0"] = (i[:, None] <= i[None]) * 1.0
    c["tri1"] = (i[:, None] >= i[None]) * 1.0
    for qt in range(2):
        nk = (qt + 1) * P
        t = qt * P + i[:, None]
        s = np.arange(nk)[None]
        see = [(s <= t) & (t - s <= P), (s <= t) & ((t - s) % 4 == 0), (s <= t) & ((t - s) % 16 == 0)]
        c[f"see{qt}"] = np.concatenate([np.where(m, 0.0, -1e30) for m in see], 1)
    t = np.arange(T)
    band = np.zeros((T, 4, T))
    for g, w in enumerate(POOL_WINDOWS):
        lo, hi = np.maximum(t - w // 2, 0), np.minimum(t + w // 2, T)
        s = t[:, None]
        band[:, g] = ((s >= lo) & (s < hi)) / (hi - lo).astype(f32)[None] - (s == t[None])
    c["band"] = band.reshape(2, P, 4, T).transpose(1, 0, 2, 3).reshape(P, -1)
    sel = np.zeros((P, 4, P))
    for h in range(4):
        sel[h, h] = 1
    c["sel"] = sel.reshape(P, -1)
    fold = np.zeros((P, 2))
    for j in range(4):
        fold[32 * j, 0] = fold[32 * j + 1, 1] = 1
    c["fold"] = fold
    s, t = i[:, None] % CHUNK, np.arange(CHUNK)[None]
    c["gram"] = np.concatenate([s < t, s <= t, s < t, s <= t], 1) * 1.0
    c["eye64"] = (s == t) * 1.0
    lev, levT = [], []
    for l in range(LEVELS):
        b = 1 << l
        low = (s // (2 * b) == t // (2 * b)) & (s % (2 * b) >= b) & (t % (2 * b) < b)
        lev.append(low)
        levT.append((s // (2 * b) == t // (2 * b)) & (t % (2 * b) >= b) & (s % (2 * b) < b))
    c["lev0"] = lev[0] * 1.0
    c["levT"] = np.concatenate(levT, 1) * 1.0
    reset = np.ones((P, TA))
    reset[:, ::CHUNK] = 0
    c["reset"] = reset
    return {k: np.ascontiguousarray(v, dtype=f32) for k, v in c.items()}


def column_map(groups):
    at, out = 0, {}
    for name, n in groups:
        out[name] = (at, n)
        at += n
    return out, at


CONSTS = constant_table()
COMMON = ("ident", "ones", "blockones")
BLOCK1 = ("rot1", "cos1", "sin1", "tri0", "tri1", "band", "sel", "fold")
BLOCK2 = tuple(k for k in CONSTS if k not in COMMON + BLOCK1)
CONST_AT, COMMON_N = column_map([(k, CONSTS[k].shape[1]) for k in COMMON])
_one, ONE_N = column_map([(k, CONSTS[k].shape[1]) for k in BLOCK1])
_two, TWO_N = column_map([(k, CONSTS[k].shape[1]) for k in BLOCK2] + [("wa2", D), ("g2a", D), ("g2b", D)])
CONST_AT.update({k: (COMMON_N + at, n) for m in (_one, _two) for k, (at, n) in m.items()})
CONST_N = COMMON_N + max(ONE_N, TWO_N)

PAR1 = [("norm_mix", 8), ("norm_ffn", 8), ("b_ada", 48), ("q_norm", 1), ("k_norm", 1), ("ml_norm", 2),
        ("pool_scale", 2), ("b_gates", 4), ("pool_w", 2 * HD)]
PAR2 = [("final_norm", 8), ("ffn1_norm", 8), ("mix_norm", 8), ("ffn2_norm", 8), ("final_norm_2", 8),
        ("gate_bias", 16), ("mu", R_TILES), ("w0", 8), ("a0", 8), ("k_k", 8), ("k_a", 8), ("r_k", 8),
        ("ln_w", 8), ("ln_b", 8), ("cond", 16)]
PAR_AT, PAR_N = column_map([(f"{n}{l}", k) for l in range(DEPTH) for n, k in PAR1] + PAR2)

FFN_PARTS = ((8, 7, 7), (FT,), (FT,), (FT,))
DOWN_TILES = (2, 1, 1, 1)


def ffn_phases(r):
    out = []
    for x, f in enumerate(FFN_PARTS[r]):
        out += [(f"up{r}_{x}", f, 2 * D), (f"down{r}_{x}", KT // DOWN_TILES[r], DOWN_TILES[r] * f * P)]
    return out


NORM_SEGMENTS = (2, 2, 2, 1, 1, 1, 1, 1, 1)

PHASES = []
PHASES += [("ada0a", ADA_FIRST, KT * ADA_COLS)]
for _l in range(DEPTH):
    PHASES += [(f"tma{_l}", 1, KT * 272), (f"fm{_l}", 6, 2 * D), (f"tmb{_l}", 1, KT * 384)]
    PHASES += [(f"ada{_l}b", ADA_UNITS - ADA_FIRST, KT * ADA_COLS)]
    if _l + 1 < DEPTH:
        PHASES += [(f"ada{_l + 1}a", ADA_FIRST, KT * ADA_COLS)]
    PHASES += [(f"out{_l}", 4, 2 * D)] + ffn_phases(_l)
PHASES += ffn_phases(2) + [("qk", 4, 3 * D), ("v", 2, KT * 384), ("rkv", 8, 3 * D),
           ("lora", 1, KT * 288), ("gates", 8, 2 * D), ("attn_up", 2, D), ("rwkv_out", 4, 2 * D), ("w_o", 4, 2 * D),
           ] + ffn_phases(3)
FIRST = {}
_u = 0
for _n, _k, _ in PHASES:
    FIRST[_n] = _u
    _u += _k


class Chain:

    def __init__(self, eng, sem):
        self.eng, self.sem, self.n, self.reg = eng, sem, 0, None

    def __call__(self, ins):
        ins.then_inc(self.sem, 1)
        self.n += 1
        self.eng.wait_ge(self.sem, self.n if self.reg is None else self.reg + self.n)


def over_units(eng, phase, body, chain=None, peel=0):
    first, n = FIRST[phase], dict((a, b) for a, b, _ in PHASES)[phase]
    i = 0
    while i < (SLOTS if first == 0 else peel):
        body((first + i) % SLOTS, first + i, i)
        i += 1
    trips = (n - i) // SLOTS
    if trips > 1:
        per = 0
        n0 = chain.n if chain else 0
        with eng.Fori(0, trips) as r:
            if chain:
                chain.reg = r * chain.per
            for j in range(SLOTS):
                body((first + i + j) % SLOTS, r * SLOTS + (first + i + j), r * SLOTS + (i + j))
        if chain:
            assert chain.n - n0 == chain.per, (chain.n, n0, chain.per)
            chain.n = n0 + chain.per * trips
            chain.reg = None
        i += trips * SLOTS
    while i < n:
        body((first + i) % SLOTS, first + i, i)
        i += 1


def build(nc, dram, out):
    ctx = ExitStack()
    with ctx:
        def sb(name, *shape):
            return ctx.enter_context(nc.sbuf_tensor(name, [P, *shape], F32))

        def sem(name):
            return ctx.enter_context(nc.semaphore(name))

        xT = sb("xT", KT, TA)
        ring = sb("ring", SLOTS, SLOT)
        const = sb("const", CONST_N)
        par = sb("par", PAR_N)
        mod = [sb(f"mod{x}", 48, 2) for x in range(DEPTH)]
        scl = [sb(f"scl{x}", 2, KT, 2) for x in range(DEPTH)]
        eps_col = sb("eps_col", 2)
        WORK = 25200
        with ExitStack() as first_use:
            hT = first_use.enter_context(nc.sbuf_tensor("hT", [P, KT, TA], F32))
            work = first_use.enter_context(nc.sbuf_tensor("work", [P, WORK], F32))
        def ffn_operands(scope, name, size, tiles, n):
            assert 4 * size + 2 * tiles * n + 2 * KT * n <= KT * TA + WORK - 2048
            return [scope.enter_context(nc.sbuf_tensor(f"{name}_{x}", shape, F32R)) for x, shape in (
                ("hidden", [P, 2, tiles, n]),
                ("w", [P, 2, 2, size]),
                ("h", [P, 2, KT, n]))]
        with ExitStack() as first_use:
            both_operands = ffn_operands(first_use, "both", max(z for _, _, z in ffn_phases(0)), max(FFN_PARTS[0]), TA)
        latent_operands = ffn_operands(ctx, "latent", FT * P, FT, T)
        ps = ctx.enter_context(nc.psum_tensor("ps", [P, 8, 512], F32))

        def K(name):
            at, n = CONST_AT[name]
            return const[:, at:at + n]

        def C(name, j=0, n=1, rows=slice(0, P)):
            at, _ = PAR_AT[name]
            return par[rows, at + j:at + j + n]

        class Area:

            def __init__(self, at=0):
                self.at = at

            def __call__(self, n):
                self.at += n
                assert self.at <= WORK, self.at
                return work[:, self.at - n:self.at]

        a = Area()
        proj = a(FM_TILES * TA).rearrange("p (m t) -> p m t", t=TA)
        tm = a(4 * TM).rearrange("p (k c) -> p k c", c=TM)
        mixT = a(KT * TA).rearrange("p (m t) -> p m t", t=TA)
        mixer_free = a.at
        stage_buf = work[:, WORK - 2048:WORK].rearrange("p (b n) -> p b n", b=2)

        params_in = sem("params_in")
        second_in = sem("second_in")
        loaded = [sem(f"loaded{j}") for j in range(SLOTS)]
        unit_done = sem("unit_done")
        act_out = sem("act_out")
        dve_out = sem("dve_out")
        chains = {e: sem(f"{e}_chain") for e in ("act", "dve", "pool")}
        met = {e: sem(f"{e}_met") for e in ("pe", "act", "dve", "pool")}
        stored = sem("stored")

        class Meet:

            def __init__(self, eng, me):
                self.eng, self.me, self.n = eng, me, 0

            def __call__(self):
                self.n += 1
                self.eng.drain().then_inc(met[self.me], 1)
                for other in met:
                    if other != self.me:
                        self.eng.wait_ge(met[other], self.n)

        def load_weights(sp):
            for phase, n, size in PHASES:
                src = dram[f"w_{phase}"]

                def body(j, u, i):
                    if not (isinstance(u, int) and u < SLOTS):
                        sp.wait_ge(unit_done, u - (SLOTS - 1))
                    sp.dma_start(ring[:, j, 0:size], src[bass.ds(i, 1), :, :].rearrange("a p n -> p (a n)"))\
                        .then_inc(loaded[j], 16)
                over_units(sp, phase, body)

        def pe_unit_ready(pe, j, u):
            pe.wait_ge(loaded[j], (u - j) * (16 // SLOTS) + 16)
            if not (isinstance(u, int) and u < 2):
                pe.wait_ge(act_out, u - 1)
                pe.wait_ge(dve_out, u - 1)

        def pe_feature_tiles(pe, phase, tiles, rhs, c0, n, kt=KT, per_bank=None):
            per_bank = per_bank or 512 // n

            def body(j, u, i):
                pe_unit_ready(pe, j, u)
                for m in range(tiles):
                    bank = 2 * (j % 2) + m // per_bank
                    o = (m % per_bank) * n
                    for k in range(kt):
                        w = ring[:, j, (m * kt + k) * P:(m * kt + k + 1) * P]
                        mm = pe.matmul(ps[:, bank, o:o + n], w, rhs[:, k, c0:c0 + n], start=(k == 0), stop=(k == kt - 1))
                mm.then_inc(unit_done, 1)
            over_units(pe, phase, body)

        def pe_ada(pe):
            def body(j, u, i):
                pe_unit_ready(pe, j, u)
                ada_products(pe, j, 2 * (j % 2))
                pe.wait_ge(act_out, u + 1)
                pe.wait_ge(dve_out, u + 1)
                ada_fold(pe, j, i, 4, 0)
            over_units(pe, "ada0a", body)

        ADA_HALF = ADA_COLS // 2

        def ada_products(pe, j, bank):
            for x in range(2):
                for k in range(KT):
                    g, o = k % 4, k * ADA_COLS + x * ADA_HALF
                    mm = pe.matmul(ps[32 * g:32 * g + 32, bank + x, 0:ADA_HALF], cond[:, k, :],
                                   ring[:, j, o:o + ADA_HALF], start=(k < 4), stop=(k >= 4),
                                   tile_position=(0, 32 * g), skip_group_check=True)
            mm.then_inc(unit_done, 1)

        def ada_fold(pe, j, i, bank, at):
            for m in range(3):
                mm = pe.matmul(ps[:, bank, bass.ds(i * 6 + 2 * m + at, 2)], stage_buf[:, j % 2, m * P:(m + 1) * P],
                               K("fold"), start=True, stop=True)
            return mm

        def copy_rows(eng, copy, my_out, me):
            def body(j, u, i):
                eng.wait_ge(unit_done, u + 1)
                copy(stage_buf[:, j % 2, me * ADA_HALF:(me + 1) * ADA_HALF], ps[:, 2 * (j % 2) + me, 0:ADA_HALF])\
                    .then_inc(my_out, 1)
            over_units(eng, "ada0a", body)

        ada_cols = sem("ada_cols")

        def later_ada(layer):
            units = list(range(ADA_FIRST, ADA_UNITS)) + (list(range(ADA_FIRST)) if layer + 1 < DEPTH else [])
            return FIRST[f"ada{layer}b"], units

        def pe_ada_unit(pe, layer, n):
            first, units = later_ada(layer)
            u = first + n
            if 1 <= n <= len(units):
                pe.wait_ge(act_out, u)
                pe.wait_ge(dve_out, u)
                mm = ada_fold(pe, (u - 1) % SLOTS, units[n - 1], 7, ADA_HALF)
                if n == len(units):
                    mm.then_inc(ada_cols, 1)
            if n < len(units):
                pe.wait_ge(loaded[u % SLOTS], 16 * (u // SLOTS + 1))
                ada_products(pe, u % SLOTS, 6)

        def take_ada_rows(eng, copy, my_out, me, layer, n):
            first, units = later_ada(layer)
            if 0 <= n < len(units):
                u = first + n
                eng.wait_ge(unit_done, u + 1)
                copy(stage_buf[:, u % 2, me * ADA_HALF:(me + 1) * ADA_HALF], ps[:, 6 + me, 0:ADA_HALF]).then_inc(my_out, 1)

        def act_copy(act):
            return lambda o, i: act.activation(o, i, ACT.Copy)

        def act_residual(act, phase, n, gates, tiles):
            def body(j, u, i):
                act.wait_ge(unit_done, u + 1)
                act.wait_ge(dve_out, u - 1)
                for m in range(tiles):
                    for lo, hi, s in gates(i * tiles + m):
                        ins = act.activation(stage_buf[:, j % 2, m * n + lo:m * n + hi],
                                             ps[:, 2 * (j % 2) + (m * n) // 512, (m * n) % 512 + lo:(m * n) % 512 + hi],
                                             ACT.Copy, scale=s)
                ins.then_inc(act_out, 1)
            over_units(act, phase, body)

        def dve_residual(dve, phase, c0, n, tiles):
            def body(j, u, i):
                dve.wait_ge(act_out, u + 1)
                x = xT[:, bass.ds(i * tiles, tiles), c0:c0 + n]
                dve.tensor_tensor(x, x, stage_buf[:, j % 2, 0:tiles * n].rearrange("p (m t) -> p m t", t=n), ALU.add)\
                    .then_inc(dve_out, 1)
            over_units(dve, phase, body)

        w_high, w_low, h_high, h_low = (sem(x) for x in ("w_high", "w_low", "h_high", "h_low"))

        def ffn_tokens(r):
            return (0, TA) if r == 0 else (T, T)

        def ffn_operands_of(r):
            return both_operands if r == 0 else latent_operands

        def split_count(u, r):
            return u - FIRST[f"up{r}_0"] + sum(n for x in range(r) for _, n, _ in ffn_phases(x))

        def h_pieces(r, shift):
            _, n = ffn_tokens(r)
            tiles = [(m, piece) for m in range(KT) for piece in (shift(m) if shift else [(0, n, None)])]
            base = sum(KT * ffn_tokens(x)[1] // T for x in range(r))
            return [(base + x + 1, m, *piece) for x, (m, piece) in enumerate(tiles)]

        def act_norm_parts(act, norm, r, shift):
            c0, n = ffn_tokens(r)
            h = ffn_operands_of(r)[2]
            act_squares(act, c0, n)
            act_split_w(act, r, FIRST[f"up{r}_0"] % SLOTS, FIRST[f"up{r}_0"], 2 * D)
            act_root(act, norm, n)
            scaled = NORM_SCALED[norm]
            for x, (count, m, lo, hi, b) in enumerate(h_pieces(r, shift)):
                act.wait_ge(norm_x, scaled + x + 1)
                src = hT[:, m, c0 + lo:c0 + hi]
                if b is None:
                    ins = act.activation(h[:, 0, m, lo:hi], src, ACT.Copy)
                else:
                    ins = act.activation(h[:, 0, m, lo:hi], src, ACT.Identity, bias=b)
                ins.then_inc(h_high, 1)

        def dve_norm_parts(dve, norm, r, scale, shift):
            c0, n = ffn_tokens(r)
            h = ffn_operands_of(r)[2]
            dve_split_w(dve, r, FIRST[f"up{r}_0"] % SLOTS, FIRST[f"up{r}_0"], 2 * D)
            dve_norm(dve, norm, c0, n, hT, scale)
            for count, m, lo, hi, b in h_pieces(r, shift):
                dve.wait_ge(h_high, count)
                src, high, low = hT[:, m, c0 + lo:c0 + hi], h[:, 0, m, lo:hi], h[:, 1, m, lo:hi]
                if b is None:
                    ins = dve.tensor_tensor(low, src, high, ALU.subtract)
                else:
                    ins = dve.scalar_tensor_tensor(out=low, in0=src, scalar=b, in1=high, op0=ALU.add, op1=ALU.subtract)
                ins.then_inc(h_low, 1)

        def act_split_w(act, r, j, u, size):
            w = ffn_operands_of(r)[1]
            act.wait_ge(loaded[j], (u - j) * (16 // SLOTS) + 16)
            act.wait_ge(unit_done, u - 1)
            act.activation(w[:, j % 2, 0, 0:size], ring[:, j, 0:size], ACT.Copy).then_inc(w_high, 1)

        def dve_split_w(dve, r, j, u, size):
            w = ffn_operands_of(r)[1]
            dve.wait_ge(w_high, split_count(u, r) + 1)
            dve.wait_ge(unit_done, u - 1)
            dve.tensor_tensor(w[:, j % 2, 1, 0:size], ring[:, j, 0:size], w[:, j % 2, 0, 0:size], ALU.subtract)\
                .then_inc(w_low, 1)

        def pe_ffn(pe, r):
            _, n = ffn_tokens(r)
            hidden, w, h = ffn_operands_of(r)
            segments_n = n // T
            h_base = h_pieces(r, None)[0][0] - 1

            def products(phase, tiles, rhs, kt, first=False):
                def body(j, u, i):
                    pe.wait_ge(w_low, split_count(u, r) + 1)
                    pe.wait_ge(act_out, u - 1)
                    pe.wait_ge(dve_out, u - 1)
                    for m in range(tiles):
                        for k in range(kt):
                            at = (m * kt + k) * P
                            if first and m == 0 and isinstance(i, int) and i == 0:
                                pe.wait_ge(h_low, h_base + segments_n * (k + 1))
                            for x, (a, b) in enumerate(((0, 0), (0, 1), (1, 0))):
                                mm = pe.matmul(ps[:, 2 * (j % 2) + m, 0:n], w[:, j % 2, a, at:at + P], rhs[:, b, k, :],
                                               start=(k == 0 and x == 0), stop=(k == kt - 1 and x == 2))
                    mm.then_inc(unit_done, 1)
                over_units(pe, phase, body, peel=int(first))
            for x, f in enumerate(FFN_PARTS[r]):
                products(f"up{r}_{x}", 2, h, KT, first=(x == 0))
                pe.wait_ge(dve_out, FIRST[f"down{r}_{x}"])
                products(f"down{r}_{x}", DOWN_TILES[r], hidden, f)

        def behind_split(eng, r, split, evacuate, chain=None):
            last = []
            for x, (phase, n, size) in enumerate(ffn_phases(r)):
                def body(j, u, i):
                    if not (isinstance(i, int) and i == 0 and x == 0):
                        split(eng, r, j, u, size)
                    if not (isinstance(i, int) and i == 0):
                        evacuate[x % 2]((j - 1) % SLOTS, u - 1, i - 1)
                    elif last:
                        last.pop()()
                over_units(eng, phase, body, chain if x % 2 == 0 else None, peel=SLOTS)
                u = FIRST[phase] + n - 1
                last.append(lambda x=x, u=u, n=n: evacuate[x % 2](u % SLOTS, u, n - 1))
            last.pop()()

        def act_ffn(act, r, gates):
            _, n = ffn_tokens(r)

            def silu(j, u, i):
                act.wait_ge(unit_done, u + 1)
                act.wait_ge(dve_out, u - 1)
                act.activation(stage_buf[:, j % 2, 0:n], ps[:, 2 * (j % 2), 0:n], ACT.Silu).then_inc(act_out, 1)

            def scaled(j, u, i):
                act.wait_ge(unit_done, u + 1)
                act.wait_ge(dve_out, u - 1)
                for m in range(DOWN_TILES[r]):
                    for lo, hi, s in gates(i * DOWN_TILES[r] + m):
                        ins = act.activation(stage_buf[:, j % 2, m * n + lo:m * n + hi], ps[:, 2 * (j % 2) + m, lo:hi],
                                             ACT.Copy, scale=s)
                ins.then_inc(act_out, 1)
            behind_split(act, r, act_split_w, (silu, scaled))

        def dve_ffn(dve, r):
            c0, n = ffn_tokens(r)
            hidden = ffn_operands_of(r)[0]

            def gated(j, u, i):
                t = stage_buf[:, j % 2, 0:n]
                high, low = (hidden[:, x, bass.ds(i, 1), :].rearrange("p a n -> p (a n)") for x in range(2))
                dve.wait_ge(act_out, u + 1)
                link(dve.tensor_tensor(t, t, ps[:, 2 * (j % 2) + 1, 0:n], ALU.mult))
                link(dve.tensor_copy(high, t))
                dve.tensor_tensor(low, t, high, ALU.subtract).then_inc(dve_out, 1)

            def add(j, u, i):
                dve.wait_ge(act_out, u + 1)
                x = xT[:, bass.ds(i * DOWN_TILES[r], DOWN_TILES[r]), c0:c0 + n]
                dve.tensor_tensor(x, x, stage_buf[:, j % 2, 0:DOWN_TILES[r] * n].rearrange("p (m t) -> p m t", t=n), ALU.add)\
                    .then_inc(dve_out, 1)
            links["dve"].per = 2 * SLOTS
            behind_split(dve, r, dve_split_w, (gated, add), chain=links["dve"])

        norm_sq, norm_sum, norm_rt = sem("norm_sq"), sem("norm_sum"), sem("norm_rt")
        square = work[:, WORK - 4096 - 2048 - 512:WORK - 2048 - 512].rearrange("p (m t) -> p m t", t=TA)
        rstd = work[:, WORK - 2048 - 512:WORK - 2048]

        def pe_norm(pe, r, c0, n):
            for k in range(KT):
                if k % 2 == 0:
                    pe.wait_ge(norm_sq, 4 * r + k // 2 + 1)
                mm = pe.matmul(ps[:, 5, 0:n], K("ones"), square[:, k, 0:n], start=(k == 0), stop=(k == KT - 1))
            mm.then_inc(norm_sum, 1)

        def act_norm(act, r, c0, n):
            act_squares(act, c0, n)
            act_root(act, r, n)

        def act_squares(act, c0, n):
            for k in range(0, KT, 2):
                act.activation(square[:, k:k + 2, 0:n], xT[:, k:k + 2, c0:c0 + n], ACT.Square, scale=1.0 / 32)\
                    .then_inc(norm_sq, 1)

        def act_root(act, r, n):
            act.wait_ge(norm_sum, r + 1)
            act.activation(rstd[:, 0:n], ps[:, 5, 0:n], ACT.Sqrt, bias=eps_col[:, 0:1]).then_inc(norm_rt, 1)

        def dve_norm(dve, r, c0, n, dst, scale):
            dve.wait_ge(norm_rt, r + 1)
            link(dve.reciprocal(rstd[:, 0:n], rstd[:, 0:n]))
            for m in range(KT):
                for lo, hi, s in scale(m):
                    dve.scalar_tensor_tensor(out=dst[:, m, c0 + lo:c0 + hi], in0=xT[:, m, c0 + lo:c0 + hi], scalar=s,
                                             in1=rstd[:, lo:hi], op0=ALU.mult, op1=ALU.mult).then_inc(norm_x, 1)

        def act_shift_h(act, layer, shift):
            pieces = [(m, piece) for m in range(KT) for piece in shift(m)]
            for x, (m, (lo, hi, b)) in enumerate(pieces):
                act.wait_ge(norm_x, NORM_SCALED[2 * layer] + x + 1)
                act.activation(hT[:, m, lo:hi], hT[:, m, lo:hi], ACT.Identity, bias=b).then_inc(h_shifted, 1)

        h_shifted = sem("h_shifted")
        norm_x = sem("norm_x")
        NORM_SCALED = [KT * sum(NORM_SEGMENTS[:x]) for x in range(len(NORM_SEGMENTS))]

        def segments(c0, n, col):
            return [(s * T - c0, s * T - c0 + T, col(s)) for s in range(2) if c0 <= s * T]

        meet, links = {}, {}

        def link(ins):
            links["dve"](ins)

        def alink(ins):
            links["act"](ins)

        cond_at = COMMON_N + ONE_N
        assert cond_at + KT * 32 <= CONST_N
        cond = const[:, cond_at:cond_at + KT * 32].rearrange("p (k c) -> p k c", c=32)

        def dve_mod(dve, layer, first, bank, at):
            lo, hi = (0, ADA_TILES) if first else (ADA_TILES, 48)
            link(dve.tensor_tensor(mod[layer][:, lo:hi, :], ps[:, bank, at + 2 * lo:at + 2 * hi].rearrange("p (m s) -> p m s", s=2),
                                   C(f"b_ada{layer}", lo, hi - lo).unsqueeze(2).broadcast_to([P, hi - lo, 2]), ALU.add))
            part, i, name = (1, 0, "norm_mix") if first else (4, 1, "norm_ffn")
            link(dve.scalar_tensor_tensor(out=scl[layer][:, i], in0=mod[layer][:, part * KT:(part + 1) * KT, :], scalar=1.0,
                                          in1=C(f"{name}{layer}", 0, 8).unsqueeze(2).broadcast_to([P, KT, 2]),
                                          op0=ALU.add, op1=ALU.mult))

        FM_ORDER = [(AQ, False), (MK, True), (AQ + 2, False), (MQ, False), (MO, False), (AK, True)]

        def unit_tokens(layer, full):
            return (0, TA) if full or layer < DEPTH - 1 else (T, T)

        def pe_project(pe, layer):
            def token_major(cols, spare):
                def body(j, u, i):
                    pe_unit_ready(pe, j, u)
                    for tt in range(4):
                        bank = 2 * (j % 2) + tt if tt < 2 else spare + tt - 2
                        for k in range(KT):
                            if u == FIRST[f"tma{layer}"] and tt == 0:
                                pe.wait_ge(h_shifted, 2 * (layer * KT + k + 1))
                            mm = pe.matmul(ps[:, bank, 0:cols], hT[:, k, tt * P:(tt + 1) * P],
                                           ring[:, j, k * cols:(k + 1) * cols], start=(k == 0), stop=(k == KT - 1))
                    mm.then_inc(unit_done, 1)
                return body

            def feature_major(j, u, i):
                tile, full = FM_ORDER[i]
                c0, n = unit_tokens(layer, full)
                pe_unit_ready(pe, j, u)
                for m in range(min(2, FM_TILES - tile)):
                    for k in range(KT):
                        mm = pe.matmul(ps[:, 2 * (j % 2) + m, 0:n], ring[:, j, (m * KT + k) * P:(m * KT + k + 1) * P],
                                       hT[:, k, c0:c0 + n], start=(k == 0), stop=(k == KT - 1))
                mm.then_inc(unit_done, 1)
            straight_units(f"tma{layer}", token_major(272, 4))
            straight_units(f"fm{layer}", feature_major, after=(0, lambda: pe_gate_rows(pe, layer)))
            pe_gate_columns(pe, layer)
            straight_units(f"tmb{layer}", token_major(384, 6))

        def straight_units(phase, body, after=None):
            first, n = FIRST[phase], dict((a, b) for a, b, _ in PHASES)[phase]
            for i in range(n):
                body((first + i) % SLOTS, first + i, i)
                if after and after[0] == i:
                    after[1]()

        def evacuate_project(eng, copy, my_out, layer, me, gate_rows):
            def token_major(cols, at, spare):
                def body(j, u, i):
                    eng.wait_ge(unit_done, u + 1)
                    bank = spare if me else 2 * (j % 2)
                    copy(tm[:, 2 * me:2 * me + 2, at:at + cols], ps[:, bank:bank + 2, 0:cols]).then_inc(my_out, 1)
                return body

            def feature_major(j, u, i):
                tile, full = FM_ORDER[i]
                c0, n = unit_tokens(layer, full)
                eng.wait_ge(unit_done, u + 1)
                if tile + 1 < FM_TILES:
                    ins = copy(proj[:, tile + me, c0:c0 + n], ps[:, 2 * (j % 2) + me, 0:n])
                else:
                    if me:
                        eng.wait_ge(act_out, u + 1)
                    ins = copy(proj[:, tile, me * T:(me + 1) * T], ps[:, 2 * (j % 2), me * T:(me + 1) * T])
                ins.then_inc(my_out, 1)
            straight_units(f"tma{layer}", token_major(272, MV, 4))
            straight_units(f"fm{layer}", feature_major, after=(0, lambda: gate_rows(eng, layer)))
            straight_units(f"tmb{layer}", token_major(384, AV, 6))

        qk_sq, qk_sum, qk_rt, qk_n, qk_rot, qk_cos, qk_r = (
            sem(f"qk_{x}") for x in ("sq", "sum", "rt", "n", "rot", "cos", "r"))
        qk_sin = sem("qk_sin")
        qa = Area(mixer_free)
        qk_buf = [[qa(TA) for _ in range(2)] for _ in range(4)]

        def qk_tiles(layer):
            c0, n = unit_tokens(layer, False)
            return [(AQ + m, c0, n, f"q_norm{layer}") for m in range(4)] + [(AK, 0, TA, f"k_norm{layer}")]

        def pe_qk(pe, layer):
            for i, (m, c0, n, _) in enumerate(qk_tiles(layer), 5 * layer):
                pe.wait_ge(qk_sq, i + 1)
                if i >= 2:
                    pe.wait_ge(qk_rt, i - 1)
                pe.matmul(ps[:, 4 + i % 2, 0:n], K("blockones"), qk_buf[0][i % 2][:, 0:n], start=True, stop=True)\
                    .then_inc(qk_sum, 1)
                if i > 5 * layer:
                    rotate(pe, i - 1, qk_tiles(layer)[i - 1 - 5 * layer])
                if i == 5 * layer + 1:
                    pe_pool_means(pe, layer)
            pe_pool_mix(pe, layer)
            rotate(pe, 5 * layer + 4, qk_tiles(layer)[4])

        def rotate(pe, i, tile):
            m, c0, n, _ = tile
            pe.wait_ge(qk_n, i + 1)
            if i >= 2:
                pe.wait_ge(qk_r, i - 1)
            pe.matmul(ps[:, 6 + i % 2, 0:n], K("rot1"), qk_buf[1][i % 2][:, 0:n], start=True, stop=True)\
                .then_inc(qk_rot, 1)

        def act_qk(act, layer):
            for i, (m, c0, n, _) in enumerate(qk_tiles(layer), 5 * layer):
                if i >= 2:
                    act.wait_ge(qk_sum, i - 1)
                act.activation(qk_buf[0][i % 2][:, 0:n], proj[:, m, c0:c0 + n], ACT.Square, scale=0.125)\
                    .then_inc(qk_sq, 1)
                if i > 5 * layer:
                    root(act, i - 1, qk_tiles(layer)[i - 1 - 5 * layer][2])
                if i == 5 * layer + 3:
                    act_pool_means(act, layer)
            root(act, 5 * layer + 4, qk_tiles(layer)[4][2])
            act_pool_mix(act, layer)

        def root(act, i, n):
            act.wait_ge(qk_sum, i + 1)
            if i >= 2:
                act.wait_ge(qk_r, i - 1)
            act.activation(qk_buf[3][i % 2][:, 0:n], ps[:, 4 + i % 2, 0:n], ACT.Sqrt, bias=eps_col[:, 0:1]).then_inc(qk_rt, 1)

        def dve_qk(dve, layer):
            def finish(i, tile):
                m, c0, n, _ = tile
                dve.wait_ge(qk_rot, i + 1)
                dve.tensor_tensor(qk_buf[3][i % 2][:, 0:n], ps[:, 6 + i % 2, 0:n], K("sin1")[:, c0:c0 + n], ALU.mult)\
                    .then_inc(qk_sin, 1)
            tiles = qk_tiles(layer)
            for i, (m, c0, n, gain) in enumerate(tiles, 5 * layer):
                dve.wait_ge(qk_rt, i + 1)
                link(dve.reciprocal(qk_buf[3][i % 2][:, 0:n], qk_buf[3][i % 2][:, 0:n]))
                if i >= 2:
                    dve.wait_ge(qk_cos, i - 1)
                dve.scalar_tensor_tensor(out=qk_buf[1][i % 2][:, 0:n], in0=proj[:, m, c0:c0 + n], scalar=C(gain),
                                         in1=qk_buf[3][i % 2][:, 0:n], op0=ALU.mult, op1=ALU.mult).then_inc(qk_n, 1)
                dve.wait_ge(qk_n, i + 1)
                if i > 5 * layer:
                    finish(i - 1, tiles[i - 1 - 5 * layer])
            finish(5 * layer + 4, tiles[4])

        def pool_qk(pool, layer):
            for i, (m, c0, n, _) in enumerate(qk_tiles(layer), 5 * layer):
                pool.wait_ge(qk_n, i + 1)
                if i >= 2:
                    pool.wait_ge(qk_r, i - 1)
                pool.tensor_tensor(qk_buf[2][i % 2][:, 0:n], qk_buf[1][i % 2][:, 0:n], K("cos1")[:, c0:c0 + n], ALU.mult)\
                    .then_inc(qk_cos, 1)
                if i > 5 * layer:
                    add_parts(pool, i - 1, qk_tiles(layer)[i - 1 - 5 * layer])
            add_parts(pool, 5 * layer + 4, qk_tiles(layer)[4])

        def add_parts(pool, i, tile):
            m, c0, n, _ = tile
            pool.wait_ge(qk_cos, i + 1)
            pool.wait_ge(qk_sin, i + 1)
            pool.tensor_tensor(proj[:, m, c0:c0 + n], qk_buf[2][i % 2][:, 0:n], qk_buf[3][i % 2][:, 0:n], ALU.add)\
                .then_inc(qk_r, 1)

        at_s, at_max, at_exp, at_p, at_t, at_pt, at_o, at_out = (
            sem(f"at_{x}") for x in ("scores", "max", "exp", "probs", "turned", "probsT", "o", "out"))
        aa = Area(mixer_free)
        probs = [aa(TA) for _ in range(3)]
        probsT = [aa(TA) for _ in range(2)]
        at_small = aa(4 * 64).rearrange("p (k n) -> p k n", k=4)

        def attention_units(layer):
            tiles = range(4) if layer < DEPTH - 1 else range(2, 4)
            return [(qt, h // 2, h % 2, (2 if qt < 2 else 4) * P) for qt in tiles for h in range(8)]

        AT_BASE = [0, 32, 48]

        def pe_attention(pe, layer):
            units, base = attention_units(layer), AT_BASE[layer]
            n = len(units)
            for i in range(n + 3):
                if i < n:
                    qt, j, b, nk = units[i]
                    if i >= 3:
                        pe.wait_ge(at_exp, base + i - 2)
                    pe.matmul(ps[:, 3 + i % 3, 0:nk], proj[64 * b:64 * b + 64, AQ + j, qt * P:(qt + 1) * P],
                              proj[64 * b:64 * b + 64, AK, 0:nk], start=True, stop=True).then_inc(at_s, 1)
                if 2 <= i < n + 2:
                    x = i - 2
                    nk = units[x][3]
                    pe.wait_ge(at_p, base + x + 1)
                    if x >= 2:
                        pe.wait_ge(at_pt, base + x - 1)
                    for s in range(nk // P):
                        mm = pe.transpose(ps[:, 6 + x % 2, s * P:(s + 1) * P], probs[x % 3][:, s * P:(s + 1) * P], K("ident"))
                    mm.then_inc(at_t, 1)
                if i >= 3:
                    x = i - 3
                    qt, j, b, nk = units[x]
                    pe.wait_ge(at_pt, base + x + 1)
                    if x >= 6 and b == 0:
                        pe.wait_ge(at_out, (base + x) // 2 - 2)
                    for s in range(nk // P):
                        mm = pe.matmul(ps[64 * b:64 * b + 64, (x // 2) % 3, 0:P], tm[:, s, AV + 64 * b:AV + 64 * b + 64],
                                       probsT[x % 2][:, s * P:(s + 1) * P], start=(s == 0), stop=(s == nk // P - 1),
                                       skip_group_check=True)
                    mm.then_inc(at_o, 1)

        def act_attention(act, layer):
            units, base = attention_units(layer), AT_BASE[layer]
            n = len(units)
            for i in range(n + 2):
                if i < n:
                    nk = units[i][3]
                    act.wait_ge(at_max, base + i + 1)
                    if i >= 3:
                        act.wait_ge(at_t, base + i - 2)
                    act.activation(probs[i % 3][:, 0:nk], ps[:, 3 + i % 3, 0:nk], ACT.Exp, scale=0.125,
                                   bias=at_small[:, 1, i:i + 1], accum_out=at_small[:, 2, i:i + 1]).then_inc(at_exp, 1)
                if i >= 2:
                    x = i - 2
                    nk = units[x][3]
                    act.wait_ge(at_t, base + x + 1)
                    if x >= 2:
                        act.wait_ge(at_o, base + x - 1)
                    act.activation(probsT[x % 2][:, 0:nk], ps[:, 6 + x % 2, 0:nk], ACT.Copy).then_inc(at_pt, 1)

        def dve_attention(dve, layer):
            units, base = attention_units(layer), AT_BASE[layer]
            n = len(units)
            for i in range(n + 4):
                if i < n:
                    nk = units[i][3]
                    dve.wait_ge(at_s, base + i + 1)
                    link(dve.tensor_reduce(at_small[:, 0, i:i + 1], ps[:, 3 + i % 3, 0:nk], AX, ALU.max))
                    dve.tensor_scalar(at_small[:, 1, i:i + 1], at_small[:, 0, i:i + 1], -0.125, None, ALU.mult)\
                        .then_inc(at_max, 1)
                if 1 <= i <= n:
                    x = i - 1
                    dve.wait_ge(at_exp, base + x + 1)
                    link(dve.reciprocal(at_small[:, 3, x:x + 1], at_small[:, 2, x:x + 1]))
                    pr = probs[x % 3][:, 0:units[x][3]]
                    dve.tensor_scalar(pr, pr, at_small[:, 3, x:x + 1], None, ALU.mult).then_inc(at_p, 1)
                if i >= 4:
                    x = i - 4
                    qt, j, b, nk = units[x]
                    if b == 1:
                        dve.wait_ge(at_o, base + x + 1)
                        dve.tensor_copy(mixT[:, j, qt * P:(qt + 1) * P], ps[:, (x // 2) % 3, 0:P]).then_inc(at_out, 1)

        pl_mean, pl_in, pl_y = (sem(f"pl_{x}") for x in ("mean", "in", "y"))
        pa = Area(qa.at)
        pooled = pa(2 * TA).rearrange("p (g t) -> p g t", t=TA)

        def pool_segments(layer):
            return (0, 1) if layer < DEPTH - 1 else (1,)

        def pe_pool_means(pe, layer):
            for seg in pool_segments(layer):
                for g in range(4):
                    b = 64 * (g % 2)
                    for s in range(2):
                        mm = pe.matmul(ps[b:b + 64, seg, (g // 2) * T:(g // 2 + 1) * T],
                                       tm[:, 2 * seg + s, PP + 64 * g:PP + 64 * g + 64],
                                       K("band")[:, (s * 4 + g) * T:(s * 4 + g + 1) * T], start=(s == 0), stop=(s == 1),
                                       skip_group_check=True)
            mm.then_inc(pl_mean, 1)

        def pe_pool_mix(pe, layer):
            pe.wait_ge(pl_in, layer + 1)
            c0, n = unit_tokens(layer, False)
            for g in range(4):
                b = 64 * (g % 2)
                mm = pe.matmul(ps[b:b + 64, 2 + g // 2, 0:n], C(f"pool_w{layer}", 64 * (g // 2), 64, slice(b, b + 64)),
                               pooled[b:b + 64, g // 2, c0:c0 + n], start=True, stop=True, skip_group_check=True)
            mm.then_inc(pl_y, 1)

        def act_pool_means(act, layer):
            act.wait_ge(pl_mean, layer + 1)
            for seg in pool_segments(layer):
                ins = act.activation(pooled[:, :, seg * T:(seg + 1) * T], ps[:, seg, :].rearrange("p (g t) -> p g t", g=2),
                                     ACT.Copy)
            ins.then_inc(pl_in, 1)

        def act_pool_mix(act, layer):
            act.wait_ge(pl_y, layer + 1)
            c0, n = unit_tokens(layer, False)
            for g in range(2):
                act.activation(mixT[:, 6 + g, c0:c0 + n], ps[:, 2 + g, 0:n], ACT.Copy, scale=C(f"pool_scale{layer}", g))

        ml_t, ml_abs, ml_ln, ml_rows, ml_cols, ml_enm = (
            sem(f"ml_{x}") for x in ("gates_t", "abs", "ln", "rows", "cols", "enm"))
        ml_nb, ml_nbs, ml_s, ml_z, ml_e, ml_ez, ml_p, ml_num, ml_h = (
            sem(f"ml_{x}") for x in ("nb", "nb_sb", "s", "z", "e", "masked", "p", "num", "h"))
        ml_sq, ml_hn, ml_hT, ml_one = (sem(f"ml_{x}") for x in ("sq", "hn", "hT", "vones"))
        ml_cols_taken = sem("ml_cols_taken")
        ma = Area(mixer_free)
        vones = ma(4 * 4 * 65).rearrange("p (t h c) -> p t h c", t=4, h=4)
        ml_pre = mixT[0:4, 0:4, :]
        ml_neg = mixT[0:4, 4:6, :]
        ml_e1 = mixT[0:4, 6:8, :]
        zero_row = ma(TA)
        cols = ma(64).rearrange("p (k d t h) -> p k d t h", k=2, d=2, t=4)
        nb = ma(2 * 2 * TA).rearrange("p (b d t) -> p b d t", b=2, d=2)
        pbuf = ma(8 * TA).rearrange("p (s d t) -> p s d t", s=4, d=2)
        ml_row = pbuf[0:4, 0:3, :, :].rearrange("p s d t -> p (s d) t")
        ebuf = ma(4 * TA).rearrange("p (b d t) -> p b d t", b=2, d=2)
        hsum = hT[:, 0:2, :].rearrange("p a (t h v) -> p (a t) h v", h=4, v=64)
        hnum = hT[:, 2:6, :].rearrange("p (d a) (t h v) -> p d (a t) h v", d=2, h=4, v=64)
        hden = ma(3 * 2 * 4).rearrange("p (k d t) -> p k d t", k=3, d=2)
        hss = ma(2 * 16).rearrange("p (k n) -> p k n", k=2)

        def ml_range(s, d, c0):
            lo, hi = (s * P, TA) if d == 0 else ((0, TA) if s < 2 else (T, T + P) if s == 2 else (T, TA))
            return max(lo, c0), hi

        def ml_sources(tt, d):
            if d == 0:
                return range(0, tt + 1)
            return range(tt, 2) if tt < 2 else [0, 1] + list(range(tt, 4))

        def ml_tiles(layer):
            return range(0, 4) if layer < DEPTH - 1 else range(2, 4)

        def pe_gate_rows(pe, layer):
            pe.wait_ge(act_out, FIRST[f"tma{layer}"] + 1)
            pe.wait_ge(dve_out, FIRST[f"tma{layer}"] + 1)
            for ty in range(4):
                for tt in range(4):
                    mm = pe.transpose(ps[0:4, 4 + ty, tt * P:(tt + 1) * P], tm[:, tt, MG + 4 * ty:MG + 4 * ty + 4], K("ident"))
            mm.then_inc(ml_t, 1)

        def pe_gate_columns(pe, layer):
            pe.wait_ge(ml_rows, layer + 1)
            for k, row in enumerate((2, 0)):
                for d in range(2):
                    for tt in range(4):
                        mm = pe.transpose(ps[:, 4, 4 * ((k * 2 + d) * 4 + tt):4 * ((k * 2 + d) * 4 + tt) + 4],
                                          ml_row[:, row + d, tt * P:(tt + 1) * P], K("ident")[0:4, 0:4])
            mm.then_inc(ml_cols, 1)

        def pe_mlstm(pe, layer):
            c0, _ = unit_tokens(layer, False)

            def running_max(h):
                for d in range(2):
                    n = 2 * (4 * layer + h) + d
                    if h:
                        pe.wait_ge(ml_nbs, n - 1)
                    elif d == 1:
                        pe.wait_ge(ml_cols_taken, layer + 1)
                    pe.matmul(ps[:, 5 - d, 0:TA], K("sel")[0:4, h * P:(h + 1) * P], ml_neg[:, d, :], start=True, stop=True)\
                        .then_inc(ml_nb, 1)
            def sums(h):
                hh = 4 * layer + h
                pe.wait_ge(ml_p, 4 * hh + 4)
                if h >= 1:
                    pe.wait_ge(ml_h, hh)
                for d in range(2):
                    for tt in ml_tiles(layer):
                        src = list(ml_sources(tt, d))
                        for s in src:
                            mm = pe.matmul(ps[:, 2 + d, 65 * tt:65 * tt + 65], pbuf[:, s, d, tt * P:(tt + 1) * P],
                                           vones[:, s, h, :], start=(s == src[0]), stop=(s == src[-1]))
                mm.then_inc(ml_num, 1)

            running_max(0)
            for h in range(4):
                hh = 4 * layer + h
                b = 64 * (h % 2)
                for s in range(4):
                    n = 4 * hh + s
                    if n >= 2 + 16 * layer:
                        pe.wait_ge(ml_p, n - 1)
                    pe.matmul(ps[:, n % 2, c0:TA], proj[b:b + 64, MK + h // 2, s * P:(s + 1) * P],
                              proj[b:b + 64, MQ + h // 2, c0:TA], start=True, stop=True).then_inc(ml_s, 1)
                    if s == 3 and h < 3:
                        running_max(h + 1)
                    pe_ada_unit(pe, layer, 4 * h + s)
                    if s == 0 and h >= 1:
                        sums(h - 1)
            sums(3)
            pe_ada_unit(pe, layer, 16)
            pe.wait_ge(ml_hn, layer + 1)
            for tt in ml_tiles(layer):
                for f in range(2):
                    mm = pe.transpose(ps[:, f, tt * P:(tt + 1) * P],
                                      hsum[:, tt, 2 * f:2 * f + 2, :].rearrange("p h v -> p (h v)"), K("ident"))
            mm.then_inc(ml_hT, 1)

        def act_gate_rows(act, layer):
            act.wait_ge(ml_abs, layer + 1)
            alink(act.activation(ml_e1, ml_e1, ACT.Exp, scale=-1.0))
            act.activation(ml_e1, ml_e1, ACT.Ln, bias=1.0).then_inc(ml_ln, 1)

        def act_mlstm(act, layer):
            c0, n = unit_tokens(layer, False)
            act.wait_ge(ml_cols, layer + 1)
            act.activation(cols[:, 1].rearrange("p d t h -> p (d t h)"), ps[:, 4, 32:64], ACT.Exp, scale=-1.0)\
                .then_inc(ml_enm, 1)

            def take_running_max(h):
                hh = 4 * layer + h
                for d in range(2):
                    act.wait_ge(ml_nb, 2 * hh + d + 1)
                    if h >= 2:
                        act.wait_ge(ml_z, 8 * (hh - 1))
                    act.activation(nb[:, h % 2, d, :], ps[:, 5 - d, 0:TA], ACT.Copy).then_inc(ml_nbs, 1)
            take_running_max(0)
            for h in range(4):
                for s in range(4):
                    for d in range(2):
                        lo, hi = ml_range(s, d, c0)
                        m = 8 * (4 * layer + h) + 2 * s + d
                        act.wait_ge(ml_z, m + 1)
                        act.activation(ebuf[:, s % 2, d, lo:hi], ebuf[:, s % 2, d, lo:hi], ACT.Exp).then_inc(ml_e, 1)
                    take_ada_rows(act, act_copy(act), act_out, 0, layer, 4 * h + s - 1)
                    if s == 2 and h < 3:
                        take_running_max(h + 1)
            take_ada_rows(act, act_copy(act), act_out, 0, layer, 15)
            act.wait_ge(ml_h, 4 * layer + 4)
            act.wait_ge(ml_hsum, layer + 1)
            t0 = ml_tiles(layer)[0]
            act.activation(hnum[:, 0, t0:4], hsum[:, t0:4], ACT.Square, scale=0.125).then_inc(ml_sq, 1)
            act.activation(proj[:, MO:MO + 2, c0:TA], proj[:, MO:MO + 2, c0:TA], ACT.Sigmoid).then_inc(ml_sig, 1)
            act.wait_ge(ml_ss, layer + 1)
            nn = (4 - t0) * 4
            act.activation(hss[:, 1, 0:nn], hss[:, 0, 0:nn], ACT.Sqrt, bias=eps_col[:, 0:1]).then_inc(ml_rt, 1)

        ml_hsum, ml_sig, ml_ss, ml_rt = sem("ml_hsum"), sem("ml_sig"), sem("ml_ss"), sem("ml_rt")

        def pool_mlstm(pool, layer):
            c0, _ = unit_tokens(layer, False)
            pool.memset(vones[:, :, :, 64:65], 1.0)
            for tt in range(4):
                ins = pool.tensor_copy(vones[:, tt, :, 0:64], tm[:, tt, MV:MV + 256].rearrange("p (h v) -> p h v", h=4))
            ins.then_inc(ml_one, 1)
            for h in range(4):
                for s in range(4):
                    for d in range(2):
                        m = 8 * (4 * layer + h) + 2 * s + d
                        pool.wait_ge(ml_e, m + 1)
                        lo, hi = ml_range(s, d, c0)
                        if lo <= s * P < hi:
                            diag = ebuf[:, s % 2, d, s * P:(s + 1) * P]
                            pool.tensor_tensor(diag, diag, K(f"tri{d}"), ALU.mult).then_inc(ml_ez, 1)

        def dve_gate_rows(dve, layer):
            dve.memset(zero_row, 0.0)
            dve.wait_ge(ml_t, layer + 1)
            for ty in range(4):
                ins = dve.tensor_scalar(ml_pre[:, ty, :], ps[0:4, 4 + ty, :], C(f"b_gates{layer}", ty, 1, slice(0, 4)), None, ALU.add)
            link(ins)
            lf, li = ml_pre[:, 1:4:2, :], ml_pre[:, 0:4:2, :]
            dve.scalar_tensor_tensor(out=ml_e1, in0=lf, scalar=-1.0, in1=lf, op0=ALU.mult, op1=ALU.max).then_inc(ml_abs, 1)
            dve.wait_ge(ml_ln, layer + 1)
            link(dve.scalar_tensor_tensor(out=lf, in0=lf, scalar=0.0, in1=ml_e1, op0=ALU.min, op1=ALU.subtract))
            z = zero_row[0:4, :]
            B, Dr, M = (ml_row[:, 2 * k:2 * k + 2, :] for k in range(3))

            def scans(dst, a, b, op):
                dve.tensor_tensor_scan(dst[:, 0, :], a[:, 0, :], b[:, 0, :], 0.0, op, op)
                link(dve.tensor_tensor_scan(dst[:, 1, 0:T][:, ::-1], a[:, 1, 0:T][:, ::-1], b[:, 1, 0:T][:, ::-1], 0.0, op, op))
                link(dve.tensor_tensor_scan(dst[:, 1, T:TA][:, ::-1], a[:, 1, T:TA][:, ::-1], b[:, 1, T:TA][:, ::-1],
                                            dst[:, 1, 0:1], op, op))
            scans(B, lf, z.unsqueeze(1).broadcast_to([4, 2, TA]), ALU.add)
            link(dve.tensor_tensor(Dr, li, B, ALU.subtract))
            scans(M, Dr, Dr, ALU.max)
            dve.tensor_scalar(ml_neg, M, -1.0, None, ALU.mult)
            dve.tensor_tensor(B, B, M, ALU.add).then_inc(ml_rows, 1)

        def dve_mlstm(dve, layer):
            c0, _ = unit_tokens(layer, False)
            dve.wait_ge(ml_enm, layer + 1)
            dve.tensor_copy(cols[:, 0].rearrange("p d t h -> p (d t h)"), ps[:, 4, 0:32]).then_inc(ml_cols_taken, 1)
            dve.wait_ge(ml_cols_taken, layer + 1)
            t0 = ml_tiles(layer)[0]

            def log_weights(n):
                h, s = n // 4, n % 4
                for d in range(2):
                    lo, hi = ml_range(s, d, c0)
                    dve.wait_ge(ml_nbs, 2 * (4 * layer + h) + d + 1)
                    dve.tensor_scalar(ebuf[:, s % 2, d, lo:hi], nb[:, h % 2, d, lo:hi], cols[:, 0, d, s, h:h + 1], 0.0,
                                      ALU.add, ALU.min).then_inc(ml_z, 1)

            def outputs(h):
                hh = 4 * layer + h
                dve.wait_ge(ml_num, hh + 1)
                both = ps[:, 2:4, 0:260].rearrange("p d (t c) -> p d t c", c=65)[:, :, t0:4]
                link(dve.tensor_copy(hden[:, 0, :, t0:4], both[:, :, :, 64]))
                link(dve.scalar_tensor_tensor(out=hden[:, 1, :, t0:4], in0=hden[:, 0, :, t0:4], scalar=-1.0,
                                              in1=hden[:, 0, :, t0:4], op0=ALU.mult, op1=ALU.max))
                link(dve.tensor_tensor(hden[:, 1, :, t0:4], hden[:, 1, :, t0:4], cols[:, 1, :, t0:4, h], ALU.max))
                link(dve.reciprocal(hden[:, 2, :, t0:4], hden[:, 1, :, t0:4]))
                for d in range(2):
                    ins = dve.tensor_tensor(hnum[:, d, t0:4, h, :], both[:, d, :, 0:64],
                                            hden[:, 2, d, t0:4].unsqueeze(2).broadcast_to([P, 4 - t0, 64]), ALU.mult)
                ins.then_inc(ml_h, 1)
                dve.wait_ge(ml_h, hh + 1)

            copy = lambda o, i: dve.tensor_copy(o, i)
            ez = ML_EZ[layer]
            log_weights(0)
            for n in range(16):
                h, s = n // 4, n % 4
                hh, m = 4 * layer + h, 16 * layer + n
                if n + 1 < 16:
                    log_weights(n + 1)
                take_ada_rows(dve, copy, dve_out, 1, layer, n - 1)
                dve.wait_ge(ml_s, m + 1)
                if s == 0 and h >= 1:
                    dve.wait_ge(ml_num, hh)
                for d in range(2):
                    lo, hi = ml_range(s, d, c0)
                    dve.wait_ge(ml_e, 2 * m + d + 1)
                    if lo <= s * P < hi:
                        ez += 1
                        dve.wait_ge(ml_ez, ez)
                    ins = dve.scalar_tensor_tensor(out=pbuf[:, s, d, lo:hi], in0=ps[:, m % 2, lo:hi], scalar=0.125,
                                                   in1=ebuf[:, s % 2, d, lo:hi], op0=ALU.mult, op1=ALU.mult)
                ins.then_inc(ml_p, 1)
                dve.wait_ge(ml_p, m + 1)
                if s == 1 and h >= 1:
                    outputs(h - 1)
            take_ada_rows(dve, copy, dve_out, 1, layer, 15)
            outputs(3)
            dve.tensor_tensor(hsum[:, t0:4], hnum[:, 0, t0:4], hnum[:, 1, t0:4], ALU.add).then_inc(ml_hsum, 1)
            dve.wait_ge(ml_sq, layer + 1)
            nn = (4 - t0) * 4
            dve.tensor_reduce(hss[:, 0, 0:nn], hnum[:, 0, t0:4].rearrange("p t h v -> p (t h) v"), AX, ALU.add)\
                .then_inc(ml_ss, 1)
            dve.wait_ge(ml_rt, layer + 1)
            link(dve.reciprocal(hss[:, 1, 0:nn], hss[:, 1, 0:nn]))
            hs = hsum[:, t0:4].rearrange("p t h v -> p (t h) v")
            dve.tensor_tensor(hs, hs, hss[:, 1, 0:nn].unsqueeze(2).broadcast_to([P, nn, 64]), ALU.mult).then_inc(ml_hn, 1)
            dve.wait_ge(ml_hT, layer + 1)
            dve.wait_ge(ml_sig, layer + 1)
            for f in range(2):
                dve.scalar_tensor_tensor(out=mixT[:, 4 + f, c0:TA], in0=ps[:, f, c0:TA], scalar=C(f"ml_norm{layer}", f),
                                         in1=proj[:, MO + f, c0:TA], op0=ALU.mult, op1=ALU.mult)
            dve.wait_ge(ada_cols, layer + 1)
            dve_mod(dve, layer, False, 7, ADA_HALF)
            if layer + 1 < DEPTH:
                dve_mod(dve, layer + 1, True, 7, ADA_HALF)

        def ez_total(layer):
            c0 = unit_tokens(layer, False)[0]
            return 4 * sum(ml_range(s, d, c0)[0] <= s * P < ml_range(s, d, c0)[1] for s in range(4) for d in range(2))

        ML_EZ = [0, ez_total(0)]

        a = Area()
        rproj = a(R_TILES * T).rearrange("p (m t) -> p m t", t=T)
        attnT = a(2 * T).rearrange("p (m t) -> p m t", t=T)
        yT = a(KT * T).rearrange("p (m t) -> p m t", t=T)
        second_free = a.at
        a = Area(second_free)
        qkT = a(12 * T).rearrange("p (m t) -> p m t", t=T)
        vtm = a(2 * 768).rearrange("p (k c) -> p k c", c=768)
        s_probs = [a(768) for _ in range(3)]
        s_probsT = [a(768) for _ in range(2)]
        s_masked = [a(768) for _ in range(2)]
        s_small = a(64).rearrange("p (k n) -> p k n", k=4)
        s_cos = [a(2 * T) for _ in range(2)]
        s_sin = [a(2 * T) for _ in range(2)]
        a = Area(second_free)
        ya = a(KT * T).rearrange("p (m t) -> p m t", t=T)
        yr = a(KT * T).rearrange("p (m t) -> p m t", t=T)
        merged = a(KT * T).rearrange("p (m t) -> p m t", t=T)

        def copy_out(eng, copy, my_out, phase, pieces):
            def body(j, u, i):
                eng.wait_ge(unit_done, u + 1)
                for o, s in pieces(j, i):
                    ins = copy(o, s)
                ins.then_inc(my_out, 1)
            over_units(eng, phase, body)

        def three_tiles(dst, me):
            def pieces(j, i):
                if me == 0:
                    return [(dst[:, bass.ds(i * 3, 2), :], ps[:, 2 * (j % 2), :].rearrange("p (m t) -> p m t", t=T))]
                return [(dst[:, bass.ds(i * 3 + 2, 1), :], ps[:, 2 * (j % 2) + 1, 0:T].unsqueeze(1))]
            return pieces

        def value_halves(me):
            def pieces(j, i):
                return [(vtm[:, me, i * 384:(i + 1) * 384], ps[:, 2 * (j % 2) + me, 0:384])]
            return pieces

        def lora_tiles(me):
            def pieces(j, i):
                if me == 0:
                    return [(rproj[:, RL:RL + 2, :], ps[:, 2 * (j % 2), :].rearrange("p (m t) -> p m t", t=T))]
                return [(rproj[0:32, RL + 2, :], ps[0:32, 2 * (j % 2) + 1, 0:T])]
            return pieces

        def bank_each(dst, me, per):
            def pieces(j, i):
                return [(dst[:, i * 2 * per + me * per:i * 2 * per + (me + 1) * per, :],
                         ps[:, 2 * (j % 2) + me, 0:per * T].rearrange("p (m t) -> p m t", t=T))]
            return pieces

        def pe_values(pe):
            def body(j, u, i):
                pe_unit_ready(pe, j, u)
                for tt in range(2):
                    for k in range(KT):
                        mm = pe.matmul(ps[:, 2 * (j % 2) + tt, 0:384], hT[:, k, T + tt * P:T + (tt + 1) * P],
                                       ring[:, j, k * 384:(k + 1) * 384], start=(k == 0), stop=(k == KT - 1))
                mm.then_inc(unit_done, 1)
            straight_units("v", body)

        def pe_lora(pe):
            def body(j, u, i):
                pe_unit_ready(pe, j, u)
                for at, m, bank, o in ((0, P, 0, 0), (P, P, 0, T), (2 * P, 32, 1, 0)):
                    for k in range(KT):
                        w = ring[:, j, k * 288 + at:k * 288 + at + m]
                        mm = pe.matmul(ps[0:m, 2 * (j % 2) + bank, o:o + T], w, hT[:, k, T:TA],
                                       start=(k == 0), stop=(k == KT - 1))
                mm.then_inc(unit_done, 1)
            straight_units("lora", body)

        sr_rot, sr_cos, sr_out = (sem(f"sr_{x}") for x in ("rot", "cos", "out"))
        two = lambda v: v.rearrange("p (m t) -> p m t", t=T)

        def pe_rope(pe):
            for i in range(6):
                if i >= 2:
                    pe.wait_ge(sr_out, i - 1)
                pe.matmul(ps[:, 4 + i % 2, :], K("rot2"), qkT[:, 2 * i:2 * i + 2, :].rearrange("p m t -> p (m t)"),
                          start=True, stop=True).then_inc(sr_rot, 1)

        def pool_rope(pool):
            for i in range(6):
                if i >= 2:
                    pool.wait_ge(sr_out, i - 1)
                pool.tensor_tensor(two(s_cos[i % 2]), qkT[:, 2 * i:2 * i + 2, :],
                                   K("cos2").unsqueeze(1).broadcast_to([P, 2, T]), ALU.mult).then_inc(sr_cos, 1)

        def dve_rope(dve):
            for i in range(6):
                dve.wait_ge(sr_rot, i + 1)
                link(dve.tensor_tensor(two(s_sin[i % 2]), two(ps[:, 4 + i % 2, :]),
                                       K("sin2").unsqueeze(1).broadcast_to([P, 2, T]), ALU.mult))
                dve.wait_ge(sr_cos, i + 1)
                dve.tensor_tensor(qkT[:, 2 * i:2 * i + 2, :], two(s_cos[i % 2]), two(s_sin[i % 2]), ALU.add)\
                    .then_inc(sr_out, 1)

        S_UNITS = [(qt, hh) for qt in range(2) for hh in range(4)]
        s_max, s_copied = sem("s_max"), sem("s_copied")
        SB = 48

        def score_banks(i):
            return 4 if i % 2 == 0 else 2

        def s_scores(i, w):
            return ps[:, score_banks(i):score_banks(i) + 2, :].rearrange("p b n -> p (b n)")[:, 0:w]

        def pe_dilated(pe):
            n = len(S_UNITS)
            for i in range(n + 3):
                if i < n:
                    qt, hh = S_UNITS[i]
                    nk = (qt + 1) * P
                    b = 64 * (hh % 2)
                    if i >= 2:
                        pe.wait_ge(s_max, i - 1)
                    for g in range(3):
                        m = (4 * g + hh) // 2
                        o = score_banks(i) * 512 + g * nk
                        mm = pe.matmul(ps[:, o // 512, o % 512:o % 512 + nk], qkT[b:b + 64, m, qt * P:(qt + 1) * P],
                                       qkT[b:b + 64, 6 + m, 0:nk], start=True, stop=True)
                    mm.then_inc(at_s, 1)
                if 2 <= i < n + 2:
                    x = i - 2
                    qt, hh = S_UNITS[x]
                    blocks = 3 * (qt + 1)
                    pe.wait_ge(at_p, SB + x + 1)
                    if x >= 1:
                        pe.wait_ge(at_pt, SB + x)
                    for s in range(blocks):
                        mm = pe.transpose(ps[:, 6 + s // 4, (s % 4) * P:(s % 4 + 1) * P],
                                          s_probs[x % 3][:, s * P:(s + 1) * P], K("ident"))
                    mm.then_inc(at_t, 1)
                if i >= 3:
                    unit = i - 3
                    qt, hh = S_UNITS[unit]
                    b = 64 * (hh % 2)
                    pe.wait_ge(at_pt, SB + unit + 1)
                    blocks = [(g, s) for g in range(3) for s in range(qt + 1)]
                    for x, (g, s) in enumerate(blocks):
                        v = vtm[:, s, (4 * g + hh) * 64:(4 * g + hh + 1) * 64]
                        o = (unit // 2) * P
                        mm = pe.matmul(ps[b:b + 64, 0, o:o + P], v, s_probsT[unit % 2][:, x * P:(x + 1) * P],
                                       start=(x == 0), stop=(x == len(blocks) - 1), skip_group_check=True)
                    mm.then_inc(at_o, 1)

        def act_dilated(act):
            def turn(i):
                w = 3 * (S_UNITS[i][0] + 1) * P
                act.wait_ge(at_t, SB + i + 1)
                if i >= 2:
                    act.wait_ge(at_o, SB + i - 1)
                act.activation(s_probsT[i % 2][:, 0:w], ps[:, 6:8, :].rearrange("p b n -> p (b n)")[:, 0:w], ACT.Copy)\
                    .then_inc(at_pt, 1)
            for i, (qt, hh) in enumerate(S_UNITS):
                w = 3 * (qt + 1) * P
                act.wait_ge(at_max, SB + i + 1)
                if i >= 3:
                    act.wait_ge(at_t, SB + i - 2)
                act.activation(s_probs[i % 3][:, 0:w], s_masked[i % 2][:, 0:w], ACT.Exp, scale=0.125,
                               bias=s_small[:, 1, i:i + 1], accum_out=s_small[:, 2, i:i + 1]).then_inc(at_exp, 1)
                if i >= 2:
                    turn(i - 2)
            turn(len(S_UNITS) - 2)
            turn(len(S_UNITS) - 1)

        def dve_dilated(dve):
            n = len(S_UNITS)
            for i in range(n + 1):
                if i < n:
                    qt, hh = S_UNITS[i]
                    w = 3 * (qt + 1) * P
                    dve.wait_ge(at_s, SB + i + 1)
                    if i >= 2:
                        dve.wait_ge(at_exp, SB + i - 1)
                    dve.tensor_tensor(s_masked[i % 2][:, 0:w], s_scores(i, w), K(f"see{qt}"), ALU.add).then_inc(s_max, 1)
                    dve.wait_ge(s_max, i + 1)
                    link(dve.tensor_reduce(s_small[:, 0, i:i + 1], s_masked[i % 2][:, 0:w], AX, ALU.max))
                    dve.tensor_scalar(s_small[:, 1, i:i + 1], s_small[:, 0, i:i + 1], -0.125, None, ALU.mult)\
                        .then_inc(at_max, 1)
                if i >= 1:
                    w = 3 * (S_UNITS[i - 1][0] + 1) * P
                    dve.wait_ge(at_exp, SB + i)
                    link(dve.reciprocal(s_small[:, 3, i - 1:i], s_small[:, 2, i - 1:i]))
                    pr = s_probs[(i - 1) % 3][:, 0:w]
                    dve.tensor_scalar(pr, pr, s_small[:, 3, i - 1:i], None, ALU.mult).then_inc(at_p, 1)
            dve.wait_ge(at_o, SB + n)
            dve.tensor_copy(attnT.rearrange("p m (q t) -> p q m t", q=2),
                            ps[:, 0, :].rearrange("p (q m t) -> p q m t", q=2, m=2))

        GROUPS = KT // 2
        (rw_log, rw_exp, rw_kk, rw_sq, rw_ss, rw_mx, rw_rt, rw_rk, rw_bon, rw_b, rw_lora) = (
            sem(f"rw_{x}") for x in ("log", "exp", "kk", "sq", "ss", "mx", "rt", "rk", "bonus", "b", "lora"))
        (rw_tr, rw_taken, rw_gram, rw_gm, rw_aab, rw_X, rw_P, rw_Pc, rw_U, rw_T, rw_f, rw_fc, rw_z) = (
            sem(f"rw_{x}") for x in ("turned", "taken", "gram", "masked", "aab", "x", "p", "p_sb", "tp", "t", "f",
                                     "f_sb", "z"))
        (rs_u, rs_U, rs_s, rs_st, rs_y, gn_c, gn_sq, gn_ss, gn_rt, gn_n, gn_t) = (
            sem(f"rs_{x}") for x in ("u", "u_sb", "s", "state", "y", "centred", "sq", "ss", "rt", "normed", "turned"))
        a = Area(second_free)
        pair = lambda: a(2 * T).rearrange("p (j t) -> p j t", j=2)
        g_gate, g_bonus, g_eW = pair(), pair(), pair()
        g_ar = a(4 * T).rearrange("p (j x t) -> p j x t", j=2, x=2)
        g_kt, g_bt = pair(), pair()
        g_at, g_kh, g_bh, g_v = (a(2 * T).rearrange("p (q d) -> p q d", d=HD) for _ in range(4))
        later = a.at
        g_gm = a(8 * 4 * CHUNK).rearrange("p (q x) -> p q x", q=8)
        g_T = a(8 * 2 * CHUNK).rearrange("p (q x t) -> p q x t", q=8, x=2)
        g_X = a((LEVELS - 1) * 8 * CHUNK).rearrange("p (l q t) -> p l q t", l=LEVELS - 1, q=8)
        g_P, g_F, g_Z = (a(8 * CHUNK).rearrange("p (q t) -> p q t", q=8) for _ in range(3))
        g_TA = a(8 * CHUNK).rearrange("p (j c t) -> p j c t", j=2, c=4)
        g_y = a(8 * CHUNK).rearrange("p (q t) -> p q t", q=8)
        g_st = a(2 * 2 * HD).rearrange("p (b j v) -> p b j v", b=2, j=2)
        g_small = a(32).rearrange("p (k n) -> p k n", k=4)
        a = Area(later)
        e_sg, e_ai, e_ls, e_lp, e_le, e_eWp, e_eWi, e_eWe, e_kk, e_rn, e_b, e_kh, e_bh = (pair() for _ in range(13))
        e_sh = a(4 * T).rearrange("p (m t) -> p m t", t=T)

        def shift(eng, lk, tile, n, buf, rows=P):
            z, d = rproj[0:rows, tile:tile + n, :], buf[0:rows, 0:n, :]
            eng.tensor_tensor(d[:, :, 1:T], z[:, :, 0:T - 1], z[:, :, 1:T], ALU.subtract)
            lk(eng.tensor_scalar(d[:, :, 0:1], z[:, :, 0:1], -1.0, None, ALU.mult))
            lk(eng.tensor_tensor(d, d, C("mu", tile, n, slice(0, rows)).unsqueeze(2).broadcast_to([rows, n, T]), ALU.mult))
            lk(eng.tensor_tensor(z, z, d, ALU.add))

        def per_tile(name, g):
            return C(name, 2 * g, 2).unsqueeze(2).broadcast_to([P, 2, T])

        def unit_of(q):
            return q // 4, (q // 2) % 2, q % 2

        def pe_rwkv(pe):
            meet["pe"]()
            for g in range(GROUPS):
                for j in range(2):
                    m = (2 * g + j) * P
                    o = j * T
                    pe.matmul(ps[:, 4, o:o + T], K("wa2")[0:64, m:m + P], rproj[0:64, RL, :], start=True, stop=True)
                    pe.matmul(ps[:, 5, o:o + T], K("wa2")[64:P, m:m + P], rproj[64:P, RL, :], start=True, stop=True)
                    pe.matmul(ps[:, 6, o:o + T], K("g2a")[:, m:m + P], rproj[:, RL + 1, :], start=True, stop=False)
                    mm = pe.matmul(ps[:, 6, o:o + T], K("g2b")[0:32, m:m + P], rproj[0:32, RL + 2, :],
                                   start=False, stop=True)
                mm.then_inc(rw_lora, 1)
                meet["pe"]()
                pe.wait_ge(rw_sq, g + 1)
                pe.matmul(ps[:, 7, :], K("blockones"), e_rn.rearrange("p j t -> p (j t)"), start=True, stop=True)\
                    .then_inc(rw_ss, 1)
                pe_gate(pe, 2 * g)
                pe.wait_ge(rw_rk, g + 1)
                pe.matmul(ps[:, 3, :], K("blockones"), e_le.rearrange("p j t -> p (j t)"), start=True, stop=True)\
                    .then_inc(rw_bon, 1)
                meet["pe"]()
                for bank, src in enumerate((None, e_kh, e_bh, rproj[:, RV + 2 * g:RV + 2 * g + 2, :])):
                    for tt in range(2):
                        for j in range(2):
                            x = (g_ar[:, j, 0] if src is None else src[:, j])[:, tt * P:(tt + 1) * P]
                            mm = pe.transpose(ps[:, bank, (2 * tt + j) * P:(2 * tt + j + 1) * P], x, K("ident"))
                    mm.then_inc(rw_tr, 1)
                for q in range(8):
                    tt, j, hb = unit_of(q)
                    b = 64 * hb
                    for p in range(2):
                        c = 2 * tt + p
                        o = j * 256
                        rows = slice(64 * p, 64 * p + 64)
                        rhs = g_ar[b:b + 64, j, :, c * 64:c * 64 + 64]
                        pe.matmul(ps[rows, 4 + 2 * hb + tt, o:o + 128], g_kt[b:b + 64, j, c * 64:c * 64 + 64], rhs,
                                  start=True, stop=True, skip_group_check=True)
                        mm = pe.matmul(ps[rows, 4 + 2 * hb + tt, o + 128:o + 256], g_bt[b:b + 64, j, c * 64:c * 64 + 64], rhs,
                                       start=True, stop=True, skip_group_check=True)
                mm.then_inc(rw_gram, 1)
                pe.wait_ge(rw_taken, g + 1)
                for q in range(8):
                    tt, j, hb = unit_of(q)
                    b = 64 * hb
                    for p in range(2):
                        c = 2 * tt + p
                        o = (q // 2) * 64
                        mm = pe.matmul(ps[64 * p:64 * p + 64, 2 * hb, o:o + 64], g_ar[b:b + 64, j, 0, c * 64:c * 64 + 64],
                                       g_bt[b:b + 64, j, c * 64:c * 64 + 64], start=True, stop=True, skip_group_check=True)
                mm.then_inc(rw_aab, 1)
                meet["pe"]()
                for l in range(LEVELS - 1):
                    pe.wait_ge(rw_X, g * (LEVELS - 1) + l + 1)
                    for half in range(2):
                        n = (g * (LEVELS - 1) + l) * 2 + half
                        if l >= 1:
                            pe.wait_ge(rw_T, n - 1)
                        for q in range(4 * half, 4 * half + 4):
                            for p in range(2):
                                rows = slice(64 * p, 64 * p + 64)
                                mm = pe.matmul(ps[rows, 4 + half, (q % 4) * 64:(q % 4) * 64 + 64], g_X[rows, l, q, :], g_T[rows, q, 0, :],
                                               start=True, stop=True, skip_group_check=True)
                        mm.then_inc(rw_P, 1)
                    for half in range(2):
                        n = (g * (LEVELS - 1) + l) * 2 + half
                        pe.wait_ge(rw_Pc, n + 1)
                        for q in range(4 * half, 4 * half + 4):
                            o = (q % 4) * 128
                            for p in range(2):
                                rows = slice(64 * p, 64 * p + 64)
                                pe.matmul(ps[rows, 6 + half, o:o + 64], g_T[rows, q, 1, :], g_P[rows, q, :],
                                          start=True, stop=True, skip_group_check=True)
                                mm = pe.matmul(ps[rows, 6 + half, o + 64:o + 128], g_P[rows, q, :], g_T[rows, q, 1, :],
                                               start=True, stop=True, skip_group_check=True)
                        mm.then_inc(rw_U, 1)
                for q in range(8):
                    for p in range(2):
                        rows = slice(64 * p, 64 * p + 64)
                        mm = pe.matmul(ps[rows, 0, q * 64:q * 64 + 64], g_gm[rows, q, 0:64], g_v[rows, q, :],
                                       start=True, stop=True, skip_group_check=True)
                mm.then_inc(rw_f, 1)
                pe.wait_ge(rw_T, (g + 1) * (LEVELS - 1) * 2)
                for q in range(8):
                    tt, j, hb = unit_of(q)
                    for p in range(2):
                        rows = slice(64 * p, 64 * p + 64)
                        o = (2 * j + tt) * 64
                        pe.matmul(ps[64 * hb:64 * hb + 64, 2 + p, o:o + 64], g_at[rows, q, :], g_T[rows, q, 1, :],
                                  start=True, stop=True, skip_group_check=True)
                pe.wait_ge(rw_fc, g + 1)
                for q in range(8):
                    for p in range(2):
                        rows = slice(64 * p, 64 * p + 64)
                        mm = pe.matmul(ps[rows, 1, q * 64:q * 64 + 64], g_T[rows, q, 1, :], g_F[rows, q, :],
                                       start=True, stop=True, skip_group_check=True)
                mm.then_inc(rw_z, 1)
                meet["pe"]()
                for c in range(4):
                    tt, p = c // 2, c % 2
                    rows = slice(64 * p, 64 * p + 64)
                    heads = [(4 * tt + x, x // 2, 64 * (x % 2)) for x in range(4)]
                    st = g_st[:, c % 2]
                    if c:
                        pe.wait_ge(rs_st, 3 * g + c)
                        for q, j, b in heads:
                            mm = pe.matmul(ps[rows, 7 if b else 3, j * 64:j * 64 + 64],
                                           g_TA[b:b + 64, j, c, :], st[b:b + 64, j, :], start=True, stop=True,
                                           skip_group_check=True)
                        mm.then_inc(rs_u, 1)
                        pe.wait_ge(rs_U, 3 * g + c)
                    if c < 3:
                        for q, j, b in heads:
                            o = (c % 2) * 128 + j * 64
                            pe.matmul(ps[b:b + 64, 4, o:o + 64], g_kh[rows, q, :], g_v[rows, q, :], start=True, stop=False,
                                      skip_group_check=True)
                            mm = pe.matmul(ps[b:b + 64, 4, o:o + 64], g_bh[rows, q, :], g_Z[rows, q, :], start=False,
                                           stop=True, skip_group_check=True)
                        mm.then_inc(rs_s, 1)
                    for q, j, b in heads:
                        o = ps[rows, 5, q * 64:q * 64 + 64]
                        pe.matmul(o, g_gm[rows, q, 64:128], g_v[rows, q, :], start=True, stop=False, skip_group_check=True)
                        pe.matmul(o, g_gm[rows, q, 192:256], g_Z[rows, q, :], start=False, stop=True, skip_group_check=True)
                        mm = pe.matmul(ps[rows, 0 if b else 6, (q // 2) * 64:(q // 2) * 64 + 64],
                                       g_ar[b:b + 64, j, 1, c * 64:c * 64 + 64], st[b:b + 64, j, :], start=True, stop=True,
                                       skip_group_check=True)
                mm.then_inc(rs_y, 1)
                pe_gate(pe, 2 * g + 1)
                pe.wait_ge(gn_n, g + 1)
                for tt in range(2):
                    for j in range(2):
                        mm = pe.transpose(ps[:, 6, j * T + tt * P:j * T + (tt + 1) * P],
                                          g_y[:, 4 * tt + 2 * j:4 * tt + 2 * j + 2, :].rearrange("p q t -> p (q t)"),
                                          K("ident"))
                mm.then_inc(gn_t, 1)
                meet["pe"]()

        def act_rwkv(act):
            act.activation(rproj[0:64, RL, :], rproj[0:64, RL, :], ACT.Tanh)
            act.activation(rproj[:, RL + 1, :], rproj[:, RL + 1, :], ACT.Sigmoid)
            act.activation(rproj[0:32, RL + 2, :], rproj[0:32, RL + 2, :], ACT.Sigmoid)
            meet["act"]()
            for g in range(GROUPS):
                act.wait_ge(rw_lora, g + 1)
                for j in range(2):
                    act.activation(e_sg[:, j, :], ps[:, 4, j * T:(j + 1) * T], ACT.Sigmoid, bias=C("w0", 2 * g + j))
                    act.activation(e_ai[:, j, :], ps[:, 5, j * T:(j + 1) * T], ACT.Sigmoid, bias=C("a0", 2 * g + j))
                act.activation(g_gate, two(ps[:, 6, :]), ACT.Copy)
                meet["act"]()
                act.wait_ge(rw_kk, g + 1)
                act.activation(e_rn, e_kk, ACT.Square).then_inc(rw_sq, 1)
                act.wait_ge(rw_log, g + 1)
                act.activation(g_eW, e_ls, ACT.Exp, scale=-DECAY)
                act.activation(e_eWp, e_lp, ACT.Exp, scale=-DECAY)
                act.activation(e_eWi, e_ls, ACT.Exp, scale=DECAY)
                act.activation(e_eWe, e_le, ACT.Exp, scale=-DECAY).then_inc(rw_exp, 1)
                act.wait_ge(rw_mx, g + 1)
                act.activation(e_rn, e_rn, ACT.Sqrt).then_inc(rw_rt, 1)
                act_gate(act, 2 * g)
                meet["act"]()
                act.wait_ge(rw_tr, 4 * g + 1)
                act.activation(g_at, ps[:, 0, :].rearrange("p (q d) -> p q d", d=HD), ACT.Copy)
                act.wait_ge(rw_tr, 4 * g + 3)
                act.activation(g_bh, ps[:, 2, :].rearrange("p (q d) -> p q d", d=HD), ACT.Copy).then_inc(rw_taken, 1)
                act.wait_ge(rw_tr, 4 * g + 4)
                act.activation(g_v, ps[:, 3, :].rearrange("p (q d) -> p q d", d=HD), ACT.Copy)
                meet["act"]()
                for l in range(LEVELS - 1):
                    for half in range(2):
                        n = (g * (LEVELS - 1) + l) * 2 + half
                        act.wait_ge(rw_P, n + 1)
                        act.activation(g_P[:, 4 * half:4 * half + 4, :],
                                       ps[:, 4 + half, 0:256].rearrange("p (q t) -> p q t", q=4), ACT.Copy)\
                            .then_inc(rw_Pc, 1)
                act.wait_ge(rw_f, g + 1)
                act.activation(g_F, ps[:, 0, :].rearrange("p (q t) -> p q t", q=8), ACT.Copy).then_inc(rw_fc, 1)
                act.wait_ge(rw_z, g + 1)
                for p in range(2):
                    act.activation(g_TA[:, :, p::2, :], ps[:, 2 + p, 0:256].rearrange("p (j c t) -> p j c t", j=2, c=2), ACT.Copy)
                meet["act"]()
                act.wait_ge(gn_c, g + 1)
                act.activation(g_F, g_y, ACT.Square, scale=0.125).then_inc(gn_sq, 1)
                act.wait_ge(gn_ss, g + 1)
                act.activation(g_small[:, 3, :], g_small[:, 2, :], ACT.Sqrt, bias=eps_col[:, 1:2]).then_inc(gn_rt, 1)
                act_gate(act, 2 * g + 1)
                meet["act"]()

        def pool_rwkv(pool):
            meet["pool"]()
            for g in range(GROUPS):
                meet["pool"]()
                pool.wait_ge(rw_b, g + 1)
                pool.wait_ge(rw_exp, g + 1)
                pool.tensor_tensor(e_kh, rproj[:, RK + 2 * g:RK + 2 * g + 2, :], e_eWe, ALU.mult)
                pool.tensor_tensor(e_bh, e_b, e_eWe, ALU.mult)
                meet["pool"]()
                pool.wait_ge(rw_gm, g + 1)
                for l in range(1, LEVELS):
                    pool.tensor_tensor(g_X[:, l - 1], g_gm[:, :, 128:192],
                                       K("levT")[:, l * 64:(l + 1) * 64].unsqueeze(1).broadcast_to([P, 8, 64]), ALU.mult)\
                        .then_inc(rw_X, 1)
                    if l == 1:
                        meet["pool"]()
                meet["pool"]()
                meet["pool"]()

        def dve_rkv(dve):
            def unit(j, u, i):
                dve.wait_ge(unit_done, u + 1)
                dve.tensor_copy(rproj[:, 3 * i + 2, :], ps[:, 2 * (j % 2) + 1, 0:T]).then_inc(dve_out, 1)
                dve.wait_ge(dve_out, u + 1)
                dve.wait_ge(act_out, u + 1)
                shift(dve, link, 3 * i, 3, e_sh)
            straight_units("rkv", unit)
            u = FIRST["lora"]
            copy_out(dve, lambda o, i: dve.tensor_copy(o, i), dve_out, "lora", lora_tiles(1))
            dve.wait_ge(dve_out, u + 1)
            dve.wait_ge(act_out, u + 1)
            shift(dve, link, RL, 2, e_sh)
            shift(dve, link, RL + 2, 1, e_sh, 32)
            meet["dve"]()

        def dve_rwkv(dve):
            meet["dve"]()
            for g in range(GROUPS):
                r, k, v = (rproj[:, x + 2 * g:x + 2 * g + 2, :] for x in (RR, RK, RV))
                meet["dve"]()
                dve.tensor_tensor(e_kk, k, per_tile("k_k", g), ALU.mult).then_inc(rw_kk, 1)
                flat = lambda x: x.rearrange("p j t -> p (j t)")
                link(dve.tensor_tensor_scan(flat(e_ls), K("reset"), flat(e_sg), 0.0, ALU.mult, ALU.add))
                dve.tensor_tensor(e_lp, e_ls, e_sg, ALU.subtract)
                chunks = lambda x: flat(x).rearrange("p (n t) -> p n t", t=CHUNK)
                dve.tensor_tensor(chunks(e_le), chunks(e_ls)[:, :, CHUNK - 1:CHUNK].broadcast_to([P, 8, CHUNK]), chunks(e_ls),
                                  ALU.subtract).then_inc(rw_log, 1)
                link(dve.scalar_tensor_tensor(out=e_b, in0=e_ai, scalar=-1.0, in1=per_tile("k_a", g), op0=ALU.add, op1=ALU.mult))
                link(dve.scalar_tensor_tensor(out=k, in0=e_b, scalar=1.0, in1=k, op0=ALU.add, op1=ALU.mult))
                dve.wait_ge(rw_ss, g + 1)
                dve.tensor_scalar(flat(e_rn), ps[:, 7, :], 1e-24, None, ALU.max).then_inc(rw_mx, 1)
                dve.wait_ge(rw_rt, g + 1)
                link(dve.reciprocal(e_rn, e_rn))
                link(dve.tensor_tensor(e_kk, e_kk, e_rn, ALU.mult))
                dve.tensor_tensor(e_b, e_kk, e_ai, ALU.mult).then_inc(rw_b, 1)
                dve.wait_ge(rw_b, g + 1)
                dve.wait_ge(rw_exp, g + 1)
                link(dve.tensor_tensor(e_lp, r, k, ALU.mult))
                dve.tensor_tensor(e_le, e_lp, per_tile("r_k", g), ALU.mult).then_inc(rw_rk, 1)
                dve.scalar_tensor_tensor(out=g_ar[:, :, 0, :], in0=e_kk, scalar=-1.0, in1=e_eWp, op0=ALU.mult, op1=ALU.mult)
                dve.tensor_tensor(g_ar[:, :, 1, :], r, g_eW, ALU.mult)
                dve.tensor_tensor(g_kt, k, e_eWi, ALU.mult)
                dve.tensor_tensor(g_bt, e_b, e_eWi, ALU.mult)
                dve.wait_ge(rw_bon, g + 1)
                link(dve.tensor_tensor(g_bonus, two(ps[:, 3, :]), v, ALU.mult))
                meet["dve"]()
                dve.wait_ge(rw_tr, 4 * g + 2)
                dve.tensor_copy(g_kh, ps[:, 1, :].rearrange("p (q d) -> p q d", d=HD))
                dve.wait_ge(rw_gram, g + 1)
                for x in range(4):
                    q0 = 4 * (x % 2) + x // 2
                    ins = dve.tensor_tensor(g_gm[:, q0:q0 + 3:2, :], ps[:, 4 + x, :].rearrange("p (q n) -> p q n", q=2),
                                            K("gram").unsqueeze(1).broadcast_to([P, 2, 256]), ALU.mult)
                ins.then_inc(rw_gm, 1)
                dve.wait_ge(rw_gm, g + 1)
                all8 = lambda m: m.unsqueeze(1).broadcast_to([P, 8, 64])
                link(dve.tensor_tensor(g_T[:, :, 1, :], g_gm[:, :, 128:192], all8(K("levT")[:, 0:64]), ALU.mult))
                link(dve.tensor_tensor(g_T[:, :, 1, :], g_T[:, :, 1, :], all8(K("eye64")), ALU.add))
                dve.wait_ge(rw_aab, g + 1)
                for hb in range(2):
                    ins = dve.tensor_tensor(g_T[:, hb::2, 0, :], ps[:, 2 * hb, 0:256].rearrange("p (q t) -> p q t", q=4),
                                            K("lev0").unsqueeze(1).broadcast_to([P, 4, 64]), ALU.mult)
                link(ins)
                dve.memset(g_st[:, 0], 0.0)
                link(dve.tensor_tensor(g_T[:, :, 0, :], g_T[:, :, 0, :], all8(K("eye64")), ALU.add))
                meet["dve"]()
                for l in range(LEVELS - 1):
                    for half in range(2):
                        n = (g * (LEVELS - 1) + l) * 2 + half
                        dve.wait_ge(rw_U, n + 1)
                        t = g_T[:, 4 * half:4 * half + 4].rearrange("p q x t -> p (q x t)")
                        dve.tensor_tensor(t, t, ps[:, 6 + half, :], ALU.add).then_inc(rw_T, 1)
                dve.wait_ge(rw_z, g + 1)
                dve.tensor_copy(g_Z, ps[:, 1, :].rearrange("p (q t) -> p q t", q=8))
                meet["dve"]()
                for c in range(4):
                    tt, p = c // 2, c % 2
                    rows = slice(64 * p, 64 * p + 64)
                    if c:
                        dve.wait_ge(rs_u, 3 * g + c)
                        for hb in range(2):
                            u = g_Z[rows, 4 * tt + hb:4 * tt + 4:2, :]
                            ins = dve.tensor_tensor(u, u, ps[rows, 3 + 4 * hb, 0:128].rearrange("p (q t) -> p q t", q=2), ALU.add)
                        ins.then_inc(rs_U, 1)
                    if c < 3:
                        dve.wait_ge(rs_s, 3 * g + c + 1)
                        new = g_st[:, (c + 1) % 2]
                        o = ps[:, 4, (c % 2) * 128:(c % 2) * 128 + 128].rearrange("p (j v) -> p j v", j=2)
                        if c == 0:
                            dve.tensor_copy(new, o).then_inc(rs_st, 1)
                        else:
                            wc = g_eW[:, :, c * CHUNK + CHUNK - 1:c * CHUNK + CHUNK].broadcast_to([P, 2, HD])
                            link(dve.tensor_tensor(g_st2, g_st[:, c % 2], wc, ALU.mult))
                            dve.tensor_tensor(new, g_st2, o, ALU.add).then_inc(rs_st, 1)
                        dve.wait_ge(rs_st, 3 * g + c + 1)
                dve.wait_ge(rs_y, g + 1)
                link(dve.tensor_copy(g_y, ps[:, 5, :].rearrange("p (q t) -> p q t", q=8)))
                for hb in range(2):
                    y = g_y[:, hb::2, :]
                    ins = dve.tensor_tensor(y, y, ps[:, 0 if hb else 6, 0:256].rearrange("p (q t) -> p q t", q=4), ALU.add)
                link(ins)
                link(dve.tensor_reduce(g_small[:, 0, :], g_y, AX, ALU.add))
                link(dve.tensor_scalar(g_small[:, 1, :], g_small[:, 0, :], -1.0 / HD, None, ALU.mult))
                dve.tensor_tensor(g_y, g_y, g_small[:, 1, :].unsqueeze(2).broadcast_to([P, 8, HD]), ALU.add).then_inc(gn_c, 1)
                dve.wait_ge(gn_sq, g + 1)
                dve.wait_ge(gn_c, g + 1)
                dve.tensor_reduce(g_small[:, 2, :], g_F, AX, ALU.add).then_inc(gn_ss, 1)
                dve.wait_ge(gn_rt, g + 1)
                link(dve.reciprocal(g_small[:, 3, :], g_small[:, 3, :]))
                dve.tensor_tensor(g_y, g_y, g_small[:, 3, :].unsqueeze(2).broadcast_to([P, 8, HD]), ALU.mult).then_inc(gn_n, 1)
                dve.wait_ge(gn_t, g + 1)
                for j in range(2):
                    m = 2 * g + j
                    ins = dve.tensor_scalar(yT[:, m, :], ps[:, 6, j * T:(j + 1) * T], C("ln_w", m), C("ln_b", m),
                                            ALU.mult, ALU.add)
                link(ins)
                y = yT[:, 2 * g:2 * g + 2, :]
                link(dve.tensor_tensor(y, y, g_bonus, ALU.add))
                link(dve.tensor_tensor(y, y, g_gate, ALU.mult))
                meet["dve"]()
                dve.drain().then_inc(dve_out, 2)

        g_st2 = g_P.rearrange("p q t -> p (q t)")[:, 0:128].rearrange("p (j v) -> p j v", j=2)

        y_gated = sem("y_gated")

        def pe_gate(pe, i):
            u = FIRST["gates"] + i
            j = u % SLOTS
            pe_unit_ready(pe, j, u)
            for m in range(2):
                for k in range(KT):
                    mm = pe.matmul(ps[:, 1 + i % 2, m * T:(m + 1) * T], ring[:, j, (m * KT + k) * P:(m * KT + k + 1) * P],
                                   hT[:, k, T:TA], start=(k == 0), stop=(k == KT - 1))
            mm.then_inc(unit_done, 1)

        def act_gate(act, i):
            act.wait_ge(unit_done, FIRST["gates"] + i + 1)
            for m, dst in enumerate((xT, hT)):
                ins = act.activation(dst[:, i, 0:T], ps[:, 1 + i % 2, m * T:(m + 1) * T], ACT.Sigmoid,
                                     bias=C("gate_bias", i + 8 * m))
            ins.then_inc(act_out, 1)

        def pool_merge(pool):
            pool.wait_ge(act_out, FIRST["attn_up"] + 2)
            pool.wait_ge(dve_out, FIRST["attn_up"] + 2)
            pool.tensor_tensor(ya, ya, xT[:, :, 0:T], ALU.mult).then_inc(y_gated, 1)

        def dve_merge(dve):
            dve.wait_ge(act_out, FIRST["rwkv_out"] + 4)
            dve.wait_ge(dve_out, FIRST["rwkv_out"] + 4)
            link(dve.tensor_tensor(yr, yr, hT[:, :, 0:T], ALU.mult))
            dve.wait_ge(y_gated, 1)
            dve.tensor_tensor(merged, ya, yr, ALU.add)

        def gate_of(layer, part):
            def gates(m, c0):
                return [(lo, hi, mod[layer][:, bass.ds(m + part * KT, 1), s:s + 1].rearrange("p a b -> p (a b)"))
                        for s in range(2) for lo, hi in [(s * T - c0, s * T - c0 + T)] if lo >= 0]
            return lambda c0: (lambda m: gates(m, c0))

        half = lambda m: [(0, T, 0.5)]
        whole = lambda m: [(0, T, 1.0)]

        def scale_of(layer, i, c0):
            return lambda m: segments(c0, None, lambda s: scl[layer][:, i, m, s:s + 1])

        def shift_of(layer, part, c0):
            return lambda m: segments(c0, None, lambda s: mod[layer][:, part * KT + m, s:s + 1])

        def plain(name):
            return lambda m: [(0, T, C(name, m))]

        block = ctx.enter_context(nc.Block())

        @block.tensor
        def _(pe):
            meet["pe"] = Meet(pe, "pe")
            pe.wait_ge(params_in, 48)
            for layer in range(DEPTH):
                c0, n = unit_tokens(layer, False)
                if layer == 0:
                    meet["pe"]()
                    pe_ada(pe)
                    meet["pe"]()
                pe_norm(pe, 2 * layer, 0, TA)
                pe_project(pe, layer)
                meet["pe"]()
                pe_mlstm(pe, layer)
                meet["pe"]()
                pe_qk(pe, layer)
                meet["pe"]()
                pe_attention(pe, layer)
                meet["pe"]()
                pe_feature_tiles(pe, f"out{layer}", 2, mixT, c0, n)
                meet["pe"]()
                pe_norm(pe, 2 * layer + 1, c0, n)
                pe_ffn(pe, layer)
                meet["pe"]()
            pe_norm(pe, 4, T, T)
            meet["pe"]()
            pe_norm(pe, 5, T, T)
            pe_ffn(pe, 2)
            meet["pe"]()
            pe_norm(pe, 6, T, T)
            meet["pe"]()
            pe_feature_tiles(pe, "qk", 3, hT, T, T)
            pe_values(pe)
            meet["pe"]()
            pe.wait_ge(second_in, 16)
            pe_rope(pe)
            meet["pe"]()
            pe_dilated(pe)
            meet["pe"]()
            pe_feature_tiles(pe, "rkv", 3, hT, T, T)
            pe_lora(pe)
            meet["pe"]()
            pe_rwkv(pe)
            pe_feature_tiles(pe, "attn_up", 4, attnT, 0, T, kt=2)
            pe_feature_tiles(pe, "rwkv_out", 2, yT, 0, T, per_bank=1)
            meet["pe"]()
            pe_feature_tiles(pe, "w_o", 2, merged, 0, T)
            meet["pe"]()
            pe_norm(pe, 7, T, T)
            pe_ffn(pe, 3)
            meet["pe"]()
            pe_norm(pe, 8, T, T)
            meet["pe"]()

        @block.scalar
        def _(act):
            meet["act"] = Meet(act, "act")
            links["act"] = Chain(act, chains["act"])
            act.wait_ge(params_in, 48)
            for layer in range(DEPTH):
                c0, n = unit_tokens(layer, False)
                if layer == 0:
                    act.activation(cond[:, :, 0:2], C("cond", 0, 16).rearrange("p (k s) -> p k s", s=2), ACT.Silu)
                    meet["act"]()
                    copy_rows(act, act_copy(act), act_out, 0)
                    meet["act"]()
                act_norm(act, 2 * layer, 0, TA)
                act_shift_h(act, layer, shift_of(layer, 0, 0))
                evacuate_project(act, act_copy(act), act_out, layer, 0, act_gate_rows)
                meet["act"]()
                act_mlstm(act, layer)
                meet["act"]()
                act_qk(act, layer)
                meet["act"]()
                act_attention(act, layer)
                meet["act"]()
                act_residual(act, f"out{layer}", n, gate_of(layer, 2)(c0), 2)
                meet["act"]()
                act_norm_parts(act, 2 * layer + 1, layer, shift_of(layer, 3, c0))
                act_ffn(act, layer, gate_of(layer, 5)(c0))
                meet["act"]()
            act.dma_start(const[:, COMMON_N:COMMON_N + TWO_N], dram["const2"]).then_inc(second_in, 16)
            act_norm(act, 4, T, T)
            meet["act"]()
            act_norm_parts(act, 5, 2, None)
            act_ffn(act, 2, half)
            meet["act"]()
            act_norm(act, 6, T, T)
            meet["act"]()
            copy_out(act, act_copy(act), act_out, "qk", three_tiles(qkT, 0))
            copy_out(act, act_copy(act), act_out, "v", value_halves(0))
            meet["act"]()
            meet["act"]()
            act_dilated(act)
            meet["act"]()
            copy_out(act, act_copy(act), act_out, "rkv", three_tiles(rproj, 0))
            copy_out(act, act_copy(act), act_out, "lora", lora_tiles(0))
            meet["act"]()
            act_rwkv(act)
            copy_out(act, act_copy(act), act_out, "attn_up", bank_each(ya, 0, 2))
            copy_out(act, act_copy(act), act_out, "rwkv_out", bank_each(yr, 0, 1))
            meet["act"]()
            act_residual(act, "w_o", T, whole, 2)
            meet["act"]()
            act_norm_parts(act, 7, 3, None)
            act_ffn(act, 3, half)
            meet["act"]()
            act_norm(act, 8, T, T)
            meet["act"]()

        @block.vector
        def _(dve):
            meet["dve"] = Meet(dve, "dve")
            links["dve"] = Chain(dve, chains["dve"])
            dve.memset(eps_col[:, 0:1], EPS)
            dve.memset(eps_col[:, 1:2], GN_EPS)
            copy = lambda o, s: dve.tensor_copy(o, s)
            for layer in range(DEPTH):
                c0, n = unit_tokens(layer, False)
                if layer == 0:
                    dve.memset(cond[:, :, 2:32], 0.0)
                    dve.wait_ge(params_in, 48)
                    meet["dve"]()
                    copy_rows(dve, copy, dve_out, 1)
                    meet["dve"]()
                    dve_mod(dve, 0, True, 4, 0)
                dve_norm(dve, 2 * layer, 0, TA, hT, scale_of(layer, 0, 0))
                evacuate_project(dve, copy, dve_out, layer, 1, dve_gate_rows)
                meet["dve"]()
                dve_mlstm(dve, layer)
                meet["dve"]()
                dve_qk(dve, layer)
                meet["dve"]()
                dve_attention(dve, layer)
                meet["dve"]()
                dve_residual(dve, f"out{layer}", c0, n, 2)
                meet["dve"]()
                dve_norm_parts(dve, 2 * layer + 1, layer, scale_of(layer, 1, c0), shift_of(layer, 3, c0))
                dve_ffn(dve, layer)
                meet["dve"]()
            dve_norm(dve, 4, T, T, xT, plain("final_norm"))
            meet["dve"]()
            dve_norm_parts(dve, 5, 2, plain("ffn1_norm"), None)
            dve_ffn(dve, 2)
            meet["dve"]()
            dve_norm(dve, 6, T, T, hT, plain("mix_norm"))
            meet["dve"]()
            copy_out(dve, copy, dve_out, "qk", three_tiles(qkT, 1))
            copy_out(dve, copy, dve_out, "v", value_halves(1))
            meet["dve"]()
            dve.wait_ge(second_in, 16)
            dve_rope(dve)
            meet["dve"]()
            dve_dilated(dve)
            meet["dve"]()
            dve_rkv(dve)
            dve_rwkv(dve)
            copy_out(dve, copy, dve_out, "attn_up", bank_each(ya, 1, 2))
            copy_out(dve, copy, dve_out, "rwkv_out", bank_each(yr, 1, 1))
            dve_merge(dve)
            meet["dve"]()
            dve_residual(dve, "w_o", T, T, 2)
            meet["dve"]()
            dve_norm_parts(dve, 7, 3, plain("ffn2_norm"), None)
            dve_ffn(dve, 3)
            meet["dve"]()
            dve_norm(dve, 8, T, T, hT, plain("final_norm_2"))
            meet["dve"]()

        @block.gpsimd
        def _(pool):
            meet["pool"] = Meet(pool, "pool")
            links["pool"] = Chain(pool, chains["pool"])
            pool.wait_ge(params_in, 48)
            for layer in range(DEPTH):
                for _ in range(1 if layer else 3):
                    meet["pool"]()
                pool_mlstm(pool, layer)
                meet["pool"]()
                pool_qk(pool, layer)
                for _ in range(4):
                    meet["pool"]()
            for _ in range(4):
                meet["pool"]()
            pool.wait_ge(second_in, 16)
            pool_rope(pool)
            meet["pool"]()
            meet["pool"]()
            meet["pool"]()
            pool_rwkv(pool)
            pool_merge(pool)
            for _ in range(4):
                meet["pool"]()

        @block.sync
        def _(sp):
            sp.dma_start(par[:, :], dram["par"]).then_inc(params_in, 16)
            sp.dma_start(const[:, 0:COMMON_N + ONE_N], dram["const"]).then_inc(params_in, 16)
            sp.dma_start(xT[:, :, :].rearrange("p k t -> p (k t)"), dram["x"]).then_inc(params_in, 16)
            load_weights(sp)
            sp.wait_ge(met["dve"], meet["dve"].n)
            sp.dma_start(out, hT[:, :, T:TA]).then_inc(stored, 16)
            sp.wait_ge(stored, 16)
        assert len({m.n for m in meet.values()}) == 1, {k: m.n for k, m in meet.items()}


def feature_columns(v):
    return np.asarray(v).reshape(-1, P).T


def tiles(w, cols):
    k, m = w.shape
    return w.reshape(k // P, P, m // cols, cols).transpose(2, 1, 0, 3).reshape(m // cols, P, -1)


def joined(t, n):
    u = t.shape[0] // n
    return t.reshape(u, n, P, -1).transpose(0, 2, 1, 3).reshape(u, P, -1)


def layout(i):
    i = {k: np.asarray(v) for k, v in i.items()}
    w = {}
    heads = [h for j in range(4) for h in (j, 4 + j)]
    for l in range(DEPTH):
        ada = tiles(i["w_ada"][l], ADA_COLS)
        w[f"ada{l}a"], w[f"ada{l}b"] = ada[:ADA_FIRST], ada[ADA_FIRST:]
        offs = np.cumsum([0, 512, 128, 128, 256, 256, 256, 256, 16, 256])
        aq, ak, av, mq, mk, mv, mo, mg, pp = (i["w_in"][l][:, a:b] for a, b in zip(offs[:-1], offs[1:]))
        aq = aq.reshape(D, 8, HD)[:, heads].reshape(D, 512)
        fm = tiles(np.concatenate([aq[:, :256], mk, aq[:, 256:], mq, mo, ak, np.zeros_like(ak)], 1), P)
        w[f"fm{l}"] = joined(fm, 2)
        w[f"tma{l}"] = tiles(np.concatenate([mv, mg], 1), 272)
        w[f"tmb{l}"] = tiles(np.concatenate([av, pp], 1), 384)
        wo = i["w_out"][l]
        wo = np.concatenate([wo[:512].reshape(8, HD, D)[heads].reshape(512, D), wo[512:]], 0)
        w[f"out{l}"] = joined(tiles(wo, P), 2)
        for r, g, u, d in ((l, i["w_ffn_gate"][l], i["w_ffn_up"][l], i["w_ffn_down"][l]),
                           (2 + l, *(i[f"ffn{1 + l}_w_{x}_2"][0] for x in ("gate", "up", "down")))):
            up, at = np.concatenate([tiles(g, P), tiles(u, P)], 2), 0
            for x, f in enumerate(FFN_PARTS[r]):
                w[f"up{r}_{x}"] = up[at:at + f]
                w[f"down{r}_{x}"] = joined(tiles(d[at * P:(at + f) * P], P), DOWN_TILES[r])
                at += f
    w2 = i["w_in_2"][0]
    w["qk"] = joined(tiles(w2[:, :1536], P), 3)
    w["v"] = tiles(w2[:, 1536:2304], 384)
    w["rkv"] = joined(tiles(w2[:, 2304:2304 + 3072], P), 3)
    w["lora"] = tiles(w2[:, 5376:5664], 288)
    w["attn_up"] = joined(tiles(i["attn_w_up_2"][0], P), 4)
    w["rwkv_out"] = joined(tiles(i["rwkv_w_out_2"][0], P), 2)
    gt = tiles(w2[:, 5664:], P)
    w["gates"] = np.concatenate([gt[:8], gt[8:]], 2)
    w["w_o"] = joined(tiles(i["w_o_2"][0], P), 2)

    par = np.zeros((P, PAR_N), np.float32)

    def put(name, v, rows=slice(0, P)):
        at, n = PAR_AT[name]
        par[rows, at:at + n] = v
    for l in range(DEPTH):
        for name in ("norm_mix", "norm_ffn", "b_ada", "ml_norm", "pool_scale"):
            put(f"{name}{l}", feature_columns(i[name][l]))
        for name in ("q_norm", "k_norm"):
            put(f"{name}{l}", np.tile(i[name][l], 2)[:, None])
        put(f"b_gates{l}", i["b_gates"][l].reshape(4, 4).T, slice(0, 4))
        put(f"pool_w{l}", i["pool_w"][l].reshape(2, 2, HD, HD).transpose(1, 2, 0, 3).reshape(P, -1))
    put("final_norm", feature_columns(i["final_norm"]))
    put("final_norm_2", feature_columns(i["final_norm_2"]))
    for name in ("ffn1_norm", "mix_norm", "ffn2_norm", "gate_bias"):
        put(name, feature_columns(i[name + "_2"][0]))
    mu = np.concatenate([i["rwkv_mu_2"][0], np.zeros(R_TILES * P - 3360, np.float32)])
    put("mu", feature_columns(mu))
    for name in ("w0", "a0", "k_k", "k_a", "r_k", "ln_w", "ln_b"):
        put(name, feature_columns(i[f"rwkv_{name}_2"][0].reshape(-1)))
    put("cond", np.stack([feature_columns(i["c_ctx"]), feature_columns(i["c"][0])], 2).reshape(P, -1))
    x = np.concatenate([i["ctx"][0], i["x"][0]], 0)
    x = x.reshape(TA, KT, P).transpose(2, 1, 0).reshape(P, -1)
    wa2 = np.concatenate([i["rwkv_w2_2"][0], i["rwkv_a2_2"][0]], 0)
    g2 = i["rwkv_g2_2"][0]
    g2b = np.concatenate([g2[P:], np.zeros((2 * P - len(g2), D), np.float32)], 0)
    const = np.concatenate([CONSTS[k] for k in COMMON + BLOCK1], 1)
    const2 = np.concatenate([CONSTS[k] for k in BLOCK2] + [wa2, g2[:P], g2b], 1)
    return {"par": par, "const": const, "const2": const2, "x": x, **{f"w_{k}": v for k, v in w.items()}}


def kernel(**inputs):
    import concourse.bacc as bacc
    from concourse.bass_utils import run_bass_kernel_spmd

    nc = bacc.Bacc("TRN2", target_bir_lowering=False, num_devices=1)
    arrays, dram = {}, {}
    for name, a in layout(inputs).items():
        arrays[f"{name}_dram"] = a = np.ascontiguousarray(a, dtype=np.float32)
        dram[name] = nc.dram_tensor(f"{name}_dram", a.shape, F32, kind="ExternalInput").ap()
    out = nc.dram_tensor("out_dram", (P, KT, T), F32, kind="ExternalOutput").ap()
    build(nc, dram, out)
    r = run_bass_kernel_spmd(nc, [arrays], core_ids=[0])
    y = r.results[0]["out_dram"]
    return np.ascontiguousarray(y.transpose(2, 1, 0).reshape(1, T, D))
```
